# Optimizing a Trainium2 kernel written in Bass

```python
import math
import jax, jax.numpy as jnp
from jax import lax
import numpy as np

D_MODEL = 1024
BATCH = 1
SEQ = 2048
DEPTH = 1

D_MIX = D_MODEL
HG_HEADS = 4
HG_DK = 128
HG_DV = 128
HG_WIDTH = HG_HEADS * HG_DV
HG_CHUNK = 64
AT_HEADS = 8
AT_HEAD_DIM = 64
AT_WIDTH = AT_HEADS * AT_HEAD_DIM
DILATED_PATTERNS = ((128, 1), (512, 4), (2048, 16))
ATT_BLOCK = 128
ROPE_THETA = 10000.0
NORM_EPS = 1e-6
IN_SPLITS = (HG_HEADS * HG_DK, HG_HEADS * HG_DK, HG_WIDTH, HG_WIDTH,
             AT_WIDTH, AT_WIDTH, AT_WIDTH, AT_WIDTH)
IN_COLS = sum(IN_SPLITS)

kernel_name = "hgrn2_dilated_attn_parallel_hybrid"

def rms_norm(x, w):
    xf = x.astype(jnp.float32)
    y = xf * lax.rsqrt(jnp.mean(xf * xf, axis=-1, keepdims=True) + NORM_EPS)
    return y * w.astype(jnp.float32)

def rope(x, positions):
    half = x.shape[-1] // 2
    inv_freq = 1.0 / (ROPE_THETA ** (jnp.arange(half, dtype=jnp.float32) / half))
    ang = positions.astype(jnp.float32)[:, None] * inv_freq[None, :]
    cos = jnp.cos(ang)[:, None, :]
    sin = jnp.sin(ang)[:, None, :]
    x1, x2 = x[..., :half], x[..., half:]
    return jnp.concatenate([x1 * cos - x2 * sin, x2 * cos + x1 * sin], axis=-1)

def hgrn2_mixer(q, f_logit, i, lb):
    B, S, H, DK = q.shape
    DV = i.shape[-1]
    C = HG_CHUNK
    nC = S // C
    log_f = jnp.logaddexp(jnp.log(lb), jnp.log1p(-lb) + jax.nn.log_sigmoid(f_logit))
    k = -jnp.expm1(log_f)
    q = jax.nn.silu(q)

    def chunks(t):
        return t.reshape(B, nC, C, H, t.shape[-1]).transpose(1, 0, 3, 2, 4)

    causal = (jnp.arange(C)[:, None] >= jnp.arange(C)[None, :])[:, :, None]

    def step(state, inp):
        qc, kc, vc, gc = inp
        b = jnp.cumsum(gc, axis=2)
        o_inter = jnp.einsum('bhck,bhkv->bhcv', qc * jnp.exp(b), state)
        diff = b[:, :, :, None, :] - b[:, :, None, :, :]
        decay = jnp.exp(jnp.where(causal, diff, -jnp.inf))
        scores = jnp.einsum('bhtk,bhtsk,bhsk->bhts', qc, decay, kc)
        o_intra = jnp.einsum('bhts,bhsv->bhtv', scores, vc)
        b_last = b[:, :, -1:, :]
        k_dec = kc * jnp.exp(b_last - b)
        new_state = jnp.exp(b_last[:, :, 0, :])[..., None] * state + \
            jnp.einsum('bhsk,bhsv->bhkv', k_dec, vc)
        return new_state, o_inter + o_intra

    state0 = jnp.zeros((B, H, DK, DV), jnp.float32)
    _, out = lax.scan(step, state0, (chunks(q), chunks(k), chunks(i), chunks(log_f)))
    return out.transpose(1, 0, 3, 2, 4).reshape(B, S, H, DV)

def dilated_window_attention(q, k, v, window, dilation):
    B, S, H, Dh = q.shape
    span = window // dilation
    assert span <= ATT_BLOCK
    BLK = ATT_BLOCK
    L = S // dilation
    nb = -(-L // BLK)
    Lp = nb * BLK

    def to_sub(t):
        t = t.reshape(B, L, dilation, H, Dh).transpose(0, 2, 3, 1, 4)
        return jnp.pad(t, ((0, 0), (0, 0), (0, 0), (0, Lp - L), (0, 0)))

    def band(t):
        tp = jnp.pad(t, ((0, 0), (0, 0), (0, 0), (BLK, 0), (0, 0)))
        tp = tp.reshape(B, dilation, H, nb + 1, BLK, Dh)
        return jnp.concatenate([tp[:, :, :, :-1], tp[:, :, :, 1:]], axis=-2)

    qb = to_sub(q).reshape(B, dilation, H, nb, BLK, Dh)
    kb = band(to_sub(k))
    vb = band(to_sub(v))
    s = jnp.einsum('bdhnqc,bdhnkc->bdhnqk', qb, kb) * (Dh ** -0.5)
    qi = jnp.arange(BLK)[:, None]
    kj = jnp.arange(2 * BLK)[None, :]
    dist = qi + BLK - kj
    key_idx = jnp.arange(nb)[:, None, None] * BLK + kj[None] - BLK
    valid = (dist >= 0)[None] & (dist <= span)[None] & (key_idx >= 0)
    s = jnp.where(valid, s, -jnp.inf)
    m = jnp.max(s, axis=-1, keepdims=True)
    p = jnp.exp(s - m)
    l = jnp.sum(p, axis=-1, keepdims=True)
    o = jnp.einsum('bdhnqk,bdhnkc->bdhnqc', p, vb) / l
    lse = (m + jnp.log(l))[..., 0]
    o = o.reshape(B, dilation, H, Lp, Dh)[:, :, :, :L].transpose(0, 3, 1, 2, 4).reshape(B, S, H, Dh)
    lse = lse.reshape(B, dilation, H, Lp)[..., :L].transpose(0, 3, 1, 2).reshape(B, S, H)
    return o, lse

def setup_inputs(seed: int = 0) -> dict:
    key = jax.random.key(seed)
    ks = jax.random.split(key, 8)
    x = jax.random.normal(ks[0], (BATCH, SEQ, D_MODEL), jnp.float32)
    norm_w = 1.0 + 0.02 * jax.random.normal(ks[1], (DEPTH, D_MODEL), jnp.float32)
    w_in = jax.random.normal(ks[2], (DEPTH, D_MODEL, IN_COLS), jnp.float32) * D_MODEL ** -0.5
    hgrn_lb_logits = 0.5 * jax.random.normal(ks[3], (DEPTH + 1, HG_HEADS * HG_DK), jnp.float32)
    hg_norm_w = 1.0 + 0.02 * jax.random.normal(ks[4], (DEPTH, HG_HEADS * HG_DV), jnp.float32)
    w_out = jax.random.normal(ks[5], (DEPTH, D_MIX, D_MODEL), jnp.float32) * D_MIX ** -0.5
    final_norm_w = 1.0 + 0.02 * jax.random.normal(ks[6], (D_MODEL,), jnp.float32)
    return {"x": x, "norm_w": norm_w, "w_in": w_in, "hgrn_lb_logits": hgrn_lb_logits,
            "hg_norm_w": hg_norm_w, "w_out": w_out, "final_norm_w": final_norm_w}

def reference(x, norm_w, w_in, hgrn_lb_logits, hg_norm_w, w_out, final_norm_w):
    B, S, _ = x.shape
    positions = jnp.arange(S, dtype=jnp.int32)
    lb_table = jnp.cumsum(jax.nn.softmax(hgrn_lb_logits.astype(jnp.float32), axis=0), axis=0)
    split_points = list(np.cumsum(IN_SPLITS)[:-1])
    h = x
    for layer in range(DEPTH):
        u = rms_norm(h, norm_w[layer])
        proj = jnp.einsum('bsd,dc->bsc', u, w_in[layer].astype(jnp.float32))
        hg_q, hg_f, hg_i, hg_z, at_q, at_k, at_v, at_z = jnp.split(proj, split_points, axis=-1)

        lb = jnp.clip(lb_table[layer], 1e-6, 1.0 - 1e-6).reshape(HG_HEADS, HG_DK)
        o_hg = hgrn2_mixer(hg_q.reshape(B, S, HG_HEADS, HG_DK),
                           hg_f.reshape(B, S, HG_HEADS, HG_DK),
                           hg_i.reshape(B, S, HG_HEADS, HG_DV), lb)
        g = hg_norm_w[layer].astype(jnp.float32).reshape(HG_HEADS, HG_DV)
        o_hg = o_hg * lax.rsqrt(jnp.mean(o_hg * o_hg, axis=-1, keepdims=True) + NORM_EPS) * g
        o_hg = o_hg.reshape(B, S, HG_WIDTH) * jax.nn.silu(hg_z)

        q = rope(at_q.reshape(B, S, AT_HEADS, AT_HEAD_DIM), positions)
        k = rope(at_k.reshape(B, S, AT_HEADS, AT_HEAD_DIM), positions)
        v = at_v.reshape(B, S, AT_HEADS, AT_HEAD_DIM)
        outs, lses = [], []
        for window, dilation in DILATED_PATTERNS:
            o_i, lse_i = dilated_window_attention(q, k, v, window, dilation)
            outs.append(o_i)
            lses.append(lse_i)
        mix_w = jax.nn.softmax(jnp.stack(lses, axis=0), axis=0)[..., None]
        o_at = jnp.sum(mix_w * jnp.stack(outs, axis=0), axis=0)
        o_at = o_at.reshape(B, S, AT_WIDTH) * jax.nn.silu(at_z)

        mixed = jnp.concatenate([o_hg, o_at], axis=-1)
        y = jnp.einsum('bsc,cd->bsd', mixed, w_out[layer].astype(jnp.float32))
        h = h + y.astype(h.dtype)
    return rms_norm(h, final_norm_w).astype(x.dtype)


_drawn_inputs = setup_inputs


def setup_inputs(seed=0):
    import zlib

    import numpy as np

    out = dict(_drawn_inputs(seed))
    spreads = {}
    factors = {'norm_w': 4.613, 'hgrn_lb_logits': 2.71, 'hg_norm_w': 7.514, 'final_norm_w': 2.738}
    for name, (base, spread) in spreads.items():
        noise = np.random.default_rng([zlib.crc32(name.encode()), seed]).standard_normal(out[name].shape)
        drawn = base * np.exp(spread * noise) if base else spread * noise
        out[name] = __import__('jax').numpy.asarray(drawn.astype(out[name].dtype))
    for name, factor in factors.items():
        out[name] = (out[name] * factor).astype(out[name].dtype)
    return out
```

```python
from contextlib import ExitStack

import numpy as np

import concourse.bass as bass
from concourse import mybir

F32 = mybir.dt.float32
F32R = mybir.dt.float32r
I32 = mybir.dt.int32
ALU = mybir.AluOpType
ACT = mybir.ActivationFunctionType

P = 128
SEQ, D = 2048, 1024
KT_N = D // P
TILES = SEQ // P
HG_UNITS, AT_UNITS = 4, 4
UNITS = HG_UNITS + AT_UNITS
GC = 256
PIECES = 4
OUT_GROUPS = D // GC
BLOCKS = 4
BT = SEQ // BLOCKS
CH = BT // P
HD = 64
EPS = 1e-6
LEVELS = 5
FILLS = 14
MASKED = -1e30
ONE = 1

HG_STEPS = [("P", 0), ("L", 0), ("P", 1), ("M", 0), ("L", 1), ("P", 2), ("O", 0), ("M", 1), ("L", 2),
            ("P", 3), ("O", 1), ("M", 2), ("L", 3), ("T", 0), ("T", 1), ("O", 2), ("M", 3), ("T", 2),
            ("T", 3), ("O", 3)] + [("T", t) for t in range(4, TILES)]


def attention_steps(with_next):
    steps = [("X", 0), ("X", 1), ("Y", 0), ("X", 2), ("Y", 1), ("X", 3), ("Y", 2), ("Y", 3)]
    nxt = 0
    for i in range(TILES + 2):
        if i < TILES:
            steps.append(("G", i))
        if i + 4 < TILES:
            steps.append(("X", i + 4))
        elif with_next:
            steps.append(("T", nxt))
            nxt += 1
        if i >= 2 and (i - 2) % CH == CH - 1:
            steps.append(("C", (i - 2) // CH))
        if 1 <= i <= TILES:
            steps.append(("V", i - 1))
        if i + 4 < TILES:
            steps.append(("Y", i + 4))
        if i < TILES:
            steps.append(("S", i))
    if with_next:
        steps += [("T", t) for t in range(nxt, TILES)]
    return steps


def build(nc, x, w_groups, norm_w, gate_g, lb_logits, final_w, rope, near_mask, far_mask, tri_masks, out):
    vg_dram = nc.dram_tensor("values_gates", (UNITS, SEQ, GC), F32, kind="Internal").ap()
    mixed_dram = nc.dram_tensor("mixed", (SEQ, D), F32, kind="Internal").ap()
    stat_dram = nc.dram_tensor("far_stats", (AT_UNITS, BLOCKS, BT * 4), F32, kind="Internal").ap()

    with ExitStack() as ctx:
        def sb(name, shape, dt=F32):
            return ctx.enter_context(nc.sbuf_tensor(name, shape, dt))

        def sem(name):
            return ctx.enter_context(nc.semaphore(name))

        bank = [ctx.enter_context(nc.psum_tensor(f"bank{i}", [P, 512], F32)) for i in range(8)]

        u_hi = sb("u_hi", [P, KT_N, SEQ], F32R)
        u_lo = sb("u_lo", [P, KT_N, SEQ], F32R)
        w_hi = [sb(f"w_hi{s}", [P, KT_N, GC], F32R) for s in range(2)]
        w_lo = [sb(f"w_lo{s}", [P, KT_N, GC], F32R) for s in range(2)]
        stage = [sb(f"stage{s}", [P, 2, GC]) for s in range(2)]
        ident = sb("ident", [P, P])
        vg_tile = [sb(f"vg_tile{s}", [P, GC]) for s in range(2)]
        nw = sb("nw", [P, KT_N])

        ROOM = 14000
        room = sb("room", [P, ROOM])

        class Room:
            def __init__(self):
                self.at = 0

            def take(self, *shape):
                n = int(np.prod(shape))
                a = room[:, self.at:self.at + n]
                self.at += n
                assert self.at <= ROOM, self.at
                if len(shape) == 2:
                    a = a.rearrange("p (a b) -> p a b", a=shape[0])
                elif len(shape) == 3:
                    a = a.rearrange("p (a b c) -> p a b c", a=shape[0], b=shape[1])
                return a

        r = Room()
        tri = r.take(3 * P).bitcast(I32).rearrange("p (m t) -> p m t", m=3)
        lb_all, omlb_all = r.take(HG_UNITS), r.take(HG_UNITS)
        lb, omlb = r.take(1), r.take(1)
        lb_in, lb_tmp = r.take(2, HG_UNITS), r.take(HG_UNITS)
        half_neg = r.take(16)
        g_all = r.take(HG_UNITS + 1, P)
        g_cur = r.take(P)
        qb, kb, fb, Ab, Rb, Vb = (r.take(BT) for _ in range(6))
        sgq, osq = r.take(BT), r.take(BT)
        base_k, base_q, lev8, lev16, lev32, lev64 = (r.take(BT) for _ in range(6))
        q_in = r.take(BT)
        st = r.take(CH, P)
        k_tok = r.take(CH, P)
        states = [r.take(CH, P) for _ in range(2)]
        tot = {h: r.take(BT // h) for h in (8, 16, 32, 64, 128)}
        vg_blk = [r.take(CH, GC) for _ in range(2)]
        ms_o, rs_o = r.take(CH), r.take(CH)
        p = Room()
        p.at = r.at - 2 * CH * GC - 2 * CH
        xt = [p.take(D) for _ in range(2)]
        p2 = Room()
        p2.at = (3 * P + 2 * HG_UNITS + 2 + 3 * HG_UNITS + 16 + (HG_UNITS + 1) * P + P)
        xn = [p2.take(D) for _ in range(2)]
        xsq = p2.take(D)
        un = [p2.take(KT_N, P) for _ in range(2)]
        ss, rstd = p2.take(TILES), p2.take(TILES)

        a = Room()
        kT, far_v = a.take(SEQ), a.take(TILES, P)
        near_v = a.take(8, P)
        qT = [a.take(BT) for _ in range(2)]
        p_near, p_far = a.take(2, 2 * P), a.take(2, BT)
        pT = [a.take(4, P) for _ in range(3)]
        oT_near, oT_far = a.take(BT), a.take(BT)
        gate, comb = a.take(CH, P), a.take(CH, P)
        rope_sb = a.take(TILES, 2, HD // 2)
        near_m, far_m = a.take(2 * P), a.take(BT)
        roped = [a.take(4, HD) for _ in range(2)]
        rtmp = a.take(4, HD)
        st_near = [a.take(CH, 4) for _ in range(2)]
        st_far = [a.take(CH, 4) for _ in range(2)]
        st_farn = [a.take(CH, 4) for _ in range(2)]
        top, ea, eb, den, rden, wa, wb, tsum = (a.take(CH, 2) for _ in range(8))

        o = Room()
        mx = [o.take(D) for _ in range(2)]
        xr = [o.take(D) for _ in range(2)]
        hh = [o.take(D) for _ in range(2)]
        hsq = o.take(D)
        fw = o.take(D)
        ms_f, rs_f = o.take(TILES), o.take(TILES)
        o_half = o.take(1)
        mT_hi = [u_hi[:, 4 + s, 0:D].rearrange("p (k t) -> p k t", k=KT_N) for s in range(2)]
        mT_lo = [u_lo[:, 4 + s, 0:D].rearrange("p (k t) -> p k t", k=KT_N) for s in range(2)]
        wo_hi = w_hi + [u_hi[:, g, :].rearrange("p (k c) -> p k c", k=KT_N) for g in range(2)]
        wo_lo = w_lo + [u_lo[:, g, :].rearrange("p (k c) -> p k c", k=KT_N) for g in range(2)]

        const_ready, tri_landed, lb_landed = sem("const_ready"), sem("tri_landed"), sem("lb_landed")
        lb_step, lb_ready, g_landed = sem("lb_step"), sem("lb_ready"), sem("g_landed")
        x_landed0, x_landed1, xsq_done = sem("x_landed0"), sem("x_landed1"), sem("xsq_done")
        rstd_done, xn_done, xT_done = sem("rstd_done"), sem("xn_done"), sem("xT_done")
        un_done, uhi_done, ulo_done = sem("un_done"), sem("uhi_done"), sem("ulo_done")
        w_landed0, w_landed1, hi_done = sem("w_landed0"), sem("w_landed1"), sem("hi_done")
        lo_done, vz_ready, sig_done = sem("lo_done"), sem("vz_ready"), sem("sig_done")
        gate_done, gated, vg_stored0 = sem("gate_done"), sem("gated"), sem("vg_stored0")
        vg_stored1, q_ready, f_ready = sem("vg_stored1"), sem("q_ready"), sem("f_ready")
        sq_done, f_read, q_read = sem("sq_done"), sem("f_read"), sem("q_read")
        fk_ready, lev_ready, lev_mm = sem("fk_ready"), sem("lev_ready"), sem("lev_mm")
        lev_read, kt_mm, kt_read = sem("lev_read"), sem("kt_mm"), sem("kt_read")
        u_mm, st_ready, o_mm = sem("u_mm"), sem("st_ready"), sem("o_mm")
        osq_done, rs_done, out_done0 = sem("osq_done"), sem("rs_done"), sem("out_done0")
        out_done1, vg_loaded0, vg_loaded1 = sem("out_done1"), sem("vg_loaded0"), sem("vg_loaded1")
        out_stored0, out_stored1, cur_ready = sem("out_stored0"), sem("out_stored1"), sem("cur_ready")
        passed_sp, passed_dve, passed_pool = sem("passed_sp"), sem("passed_dve"), sem("passed_pool")
        rs_half, dve_comb, exp_comb = sem("rs_half"), sem("dve_comb"), sem("exp_comb")
        dve_step, pool_step, qk_ready = sem("dve_step"), sem("pool_step"), sem("qk_ready")
        roped_done, yT_mm, yT_read = sem("roped_done"), sem("yT_mm"), sem("yT_read")
        s_ready, s_taken, e_done = sem("s_ready"), sem("s_taken"), sem("e_done")
        pt_mm, pt_read, pv_mm = sem("pt_mm"), sem("pt_read"), sem("pv_mm")
        oT_read, tab_landed, nv_landed0 = sem("oT_read"), sem("tab_landed"), sem("nv_landed0")
        nv_landed1, fv_landed, gate_landed = sem("nv_landed1"), sem("fv_landed"), sem("gate_landed")
        stat_stored, stat_landed0, stat_landed1 = sem("stat_stored"), sem("stat_landed0"), sem("stat_landed1")
        comb_done, comb_stored, mx_landed0 = sem("comb_done"), sem("comb_stored"), sem("mx_landed0")
        mx_landed1, mT_mm, mhi_done = sem("mx_landed1"), sem("mT_mm"), sem("mhi_done")
        mlo_done, y_ready, hsum_done = sem("mlo_done"), sem("y_ready"), sem("hsum_done")
        hsq_done, frs_done, fin_done = sem("hsq_done"), sem("frs_done"), sem("fin_done")
        fin_stored0, fin_stored1 = sem("fin_stored0"), sem("fin_stored1")
        x_landed = [x_landed0, x_landed1]
        w_landed = [w_landed0, w_landed1]
        vg_stored = [vg_stored0, vg_stored1]
        vg_loaded = [vg_loaded0, vg_loaded1]
        out_stored = [out_stored0, out_stored1]
        nv_landed = [nv_landed0, nv_landed1]
        stat_landed = [stat_landed0, stat_landed1]
        mx_landed = [mx_landed0, mx_landed1]
        fin_stored = [fin_stored0, fin_stored1]

        def dst_of(group_slot, part):
            return (wo_hi if part == 0 else wo_lo)[group_slot]

        INTER = 6

        def vz_bank(t, attn):
            if attn:
                return bank[0] if t < INTER or t % 2 else bank[1]
            return bank[0] if t % 2 else bank[7]

        ctx.enter_context(nc.allow_non_contiguous_dma(reason="strips of 512 bytes and more"))
        block = ctx.enter_context(nc.Block())

        @block.sync
        def _(sp):
            def after(semaphore, value):
                sp.wait_ge(semaphore, value)
                if not isinstance(value, int):
                    sp.sem_inc(passed_sp, 1)

            def load_piece(n, i):
                if not (isinstance(n, int) and 4 * n + i < 2):
                    after(lo_done, n * 4 + (i - 1))
                sp.dma_start(stage[i % 2][:, :, :],
                             w_groups[bass.ds(n, 1), :, 2 * i:2 * i + 2, :].rearrange("a p k c -> (a p) k c"))\
                    .then_inc(w_landed[i % 2], 16)

            def phase1_store(U, t, scaled):
                after(gated if scaled else gate_done, U * 16 + (t + 1))
                sp.dma_start(vg_dram[bass.ds(U, 1), t * P:(t + 1) * P, :].rearrange("a t c -> (a t) c"),
                             vg_tile[t % 2][:, :]).then_inc(vg_stored[t % 2], 16)

            for counted in (q_read, f_read, kt_read, st_ready, out_done0, out_done1, lev_ready, kt_mm,
                            u_mm, osq_done, rs_done, fk_ready, o_mm, out_stored0, out_stored1, s_ready,
                            pv_mm, pt_mm, yT_mm, stat_stored, comb_done, comb_stored):
                sp.sem_inc(counted, ONE)

            sp.dma_start(nw[:, :], norm_w).then_inc(const_ready, 16)
            for t in range(2):
                sp.dma_start(xt[t], x[t * P:(t + 1) * P, :]).then_inc(x_landed[t], 16)
            load_piece(0, 0)
            load_piece(0, 1)
            sp.dma_start(lb_in, lb_logits).then_inc(lb_landed, 16)
            sp.dma_start(tri, tri_masks).then_inc(tri_landed, 16)
            sp.dma_start(g_all, gate_g).then_inc(g_landed, 16)
            for t in range(2, TILES):
                after(xn_done, t - 1)
                sp.dma_start(xt[t % 2], x[t * P:(t + 1) * P, :]).then_inc(x_landed[t % 2], 16)
                if t < 4:
                    load_piece(0, t)
                if t - 4 in (1, 4, 7, 10):
                    load_piece(1, (t - 5) // 3)
                if t >= 7:
                    phase1_store(0, t - 7, True)
            for t in range(TILES - 7, TILES):
                phase1_store(0, t, True)

            with sp.Fori(0, HG_UNITS) as u:
                def load_vg(b):
                    if b == 0:
                        after(vg_stored[0], u * 128 + 128)
                        after(vg_stored[1], u * 128 + 128)
                    after(out_stored[b % 2], u * 32 + (16 * (b // 2) + ONE))
                    src = vg_dram[bass.ds(u, 1), b * BT:(b + 1) * BT, :]
                    sp.dma_start(vg_blk[b % 2], src.rearrange("a (c t) n -> (a t) c n", c=CH))\
                        .then_inc(vg_loaded[b % 2], 16)

                for kind, i in HG_STEPS:
                    if kind == "P":
                        load_piece(2 * u + 2, i)
                        if i < 2:
                            load_vg(i)
                    elif kind == "O":
                        after((out_done0, out_done1)[i % 2], u * 2 + (i // 2 + 1 + ONE))
                        dst = mixed_dram[i * BT:(i + 1) * BT, bass.ds(u * P, P)]
                        sp.dma_start(dst.rearrange("(c t) n -> t c n", c=CH), vg_blk[i % 2][:, :, P:GC])\
                            .then_inc(out_stored[i % 2], 16)
                        if i < 2:
                            load_vg(i + 2)
                    elif kind == "T":
                        if i in (1, 4, 7, 10):
                            load_piece(2 * u + 3, (i - 1) // 3)
                        phase1_store(u + 1, i, True)

            after(out_stored[0], HG_UNITS * 32 + ONE)
            after(out_stored[1], HG_UNITS * 32 + ONE)
            sp.dma_start(rope_sb, rope).then_inc(tab_landed, 16)
            sp.dma_start(near_m, near_mask).then_inc(tab_landed, 16)
            sp.dma_start(far_m, far_mask).then_inc(tab_landed, 16)

            def attention(v, with_next):
                U = v + HG_UNITS
                T0 = v * TILES

                def load_near(g):
                    if g >= 2:
                        after(pv_mm, T0 + (4 * (g - 1) + 1 + ONE))
                    src = vg_dram[bass.ds(U, 1), g * BT:(g + 1) * BT, 0:P]
                    sp.dma_start(near_v[:, (4 * g) % 8:(4 * g) % 8 + 4, :],
                                 src.rearrange("a (c t) n -> (a t) c n", c=CH)).then_inc(nv_landed[g % 2], 16)

                def load_gate(g):
                    after(comb_stored, v * 64 + (16 * g + ONE))
                    src = vg_dram[bass.ds(U, 1), g * BT:(g + 1) * BT, P:GC]
                    sp.dma_start(gate, src.rearrange("a (c t) n -> (a t) c n", c=CH)).then_inc(gate_landed, 16)

                after(vg_stored[0], U * 128 + 128)
                after(vg_stored[1], U * 128 + 128)
                after(pv_mm, T0 + ONE)
                load_near(0)
                for g in range(BLOCKS):
                    src = vg_dram[bass.ds(U, 1), g * BT:(g + 1) * BT, 0:P]
                    sp.dma_start(far_v[:, 4 * g:4 * g + 4, :],
                                 src.rearrange("a (i q) n -> (a i) q n", q=4)).then_inc(fv_landed, 16)
                load_near(1)
                load_gate(0)
                for kind, i in attention_steps(with_next):
                    if kind == "S":
                        if i in (0, 3, 6, 9):
                            load_piece(2 * U + 2, i // 3)
                        if i % 4 == 2 and 4 <= i < 12:
                            load_near(i // 4 + 1)
                        if i % 4 == 3:
                            g = i // 4
                            after(e_done, T0 * 4 + 16 * (g + 1))
                            sd = stat_dram[bass.ds(v, 1), g, :]
                            sp.dma_start(sd.rearrange("a (i w) -> (a i) w", i=P),
                                         st_far[g % 2].rearrange("p a b -> p (a b)")).then_inc(stat_stored, 16)
                            after(stat_stored, v * 64 + 16 * (g + 1) + ONE)
                            sp.dma_start(st_farn[g % 2], sd.rearrange("a (c t w) -> (a t) c w", c=CH, w=4))\
                                .then_inc(stat_landed[g % 2], 16)
                    elif kind == "C":
                        after(comb_done, v * 4 + (i + 1 + ONE))
                        dst = mixed_dram[i * BT:(i + 1) * BT, bass.ds(U * P, P)]
                        sp.dma_start(dst.rearrange("(c t) n -> t c n", c=CH), gate).then_inc(comb_stored, 16)
                        if i + 1 < BLOCKS:
                            load_gate(i + 1)
                    elif kind == "T":
                        if i in (1, 4, 7, 10):
                            load_piece(2 * U + 3, (i - 1) // 3)
                        phase1_store(U + 1, i, False)

            with sp.Fori(0, AT_UNITS - 1) as v:
                attention(v, True)
            attention(AT_UNITS - 1, False)

            for n in range(1, OUT_GROUPS):
                for i in range(PIECES):
                    load_piece(2 * UNITS + n, i)
            after(comb_stored, AT_UNITS * 64 + ONE)
            sp.dma_start(fw, final_w).then_inc(tab_landed, 16)
            for t in range(TILES):
                if t >= 2:
                    after(mT_mm, t - 1)
                    after(hsum_done, t - 1)
                sp.dma_start(mx[t % 2], mixed_dram[t * P:(t + 1) * P, :]).then_inc(mx_landed[t % 2], 16)
                sp.dma_start(xr[t % 2], x[t * P:(t + 1) * P, :]).then_inc(mx_landed[t % 2], 16)
                if t >= 2:
                    after(fin_done, t - 1)
                    sp.dma_start(out[(t - 2) * P:(t - 1) * P, :], hh[t % 2]).then_inc(fin_stored[t % 2], 16)
            for t in (TILES - 2, TILES - 1):
                after(fin_done, t + 1)
                sp.dma_start(out[t * P:(t + 1) * P, :], hh[t % 2]).then_inc(fin_stored[t % 2], 16)
            after(fin_stored[0], TILES // 2 * 16)
            after(fin_stored[1], TILES // 2 * 16)

        @block.tensor
        def _(pe):
            def split_matmuls(dst, lhs_hi, lhs_lo, rhs_hi, rhs_lo):
                for k in range(KT_N):
                    nc.tensor.matmul(dst, lhs_hi(k), rhs_hi(k), start=(k == 0), stop=False)
                    nc.tensor.matmul(dst, lhs_hi(k), rhs_lo(k), start=False, stop=False)
                    last = nc.tensor.matmul(dst, lhs_lo(k), rhs_hi(k), start=False, stop=(k == KT_N - 1))
                return last

            def phase1_tile(U, t, attn):
                first = isinstance(U, int) and U == 0
                if t == 0:
                    pe.wait_ge(lo_done, U * 8 + 4)
                if attn:
                    if t == 0:
                        pe.wait_ge(roped_done, U * 16 - 16 * HG_UNITS)
                    elif t < INTER:
                        pe.wait_ge(gate_done, U * 16 + t)
                    elif t == INTER:
                        pe.wait_ge(s_taken, U * 64 - (64 * HG_UNITS - 4))
                    else:
                        pe.wait_ge(gate_done, U * 16 + (t - 1))
                elif t >= 2:
                    pe.wait_ge(gate_done, U * 16 + (t - 1))
                elif t == 1 and not first:
                    pe.wait_ge(q_read, U * 4 + ONE)
                sl = slice(t * P, (t + 1) * P)
                last = split_matmuls(vz_bank(t, attn)[:, 0:GC],
                                     lambda k: u_hi[:, k, sl], lambda k: u_lo[:, k, sl],
                                     lambda k: w_hi[0][:, k, :], lambda k: w_lo[0][:, k, :])
                last.then_inc(vz_ready, 1)

            pe.wait_ge(const_ready, 16 + 1)
            pe.sem_inc(lev_mm, LEVELS)

            def x_transposes(t):
                pe.wait_ge(xn_done, t + 1)
                if t >= 2:
                    pe.wait_ge(un_done, t - 1)
                for k in range(KT_N):
                    last = nc.tensor.transpose(bank[1 + 2 * (t % 2) + k // 4][:, (k % 4) * P:(k % 4 + 1) * P],
                                               xn[t % 2][:, k * P:(k + 1) * P], ident[:, :])
                last.then_inc(xT_done, 1)

            x_transposes(0)
            x_transposes(1)
            for t in range(TILES):
                if t + 2 < TILES:
                    x_transposes(t + 2)
                pe.wait_ge(ulo_done, t + 1)
                phase1_tile(0, t, False)

            level_ops = [(base_k, base_q), (lev8, lev8), (lev16, lev16), (lev32, lev32), (lev64, lev64)]
            with pe.Fori(0, HG_UNITS) as u:
                for kind, b in HG_STEPS:
                    if kind == "P":
                        if b == 0:
                            pe.wait_ge(lo_done, u * 8 + 8)
                            pe.wait_ge(gate_done, u * 16 + 16)
                        sl = slice(b * BT, (b + 1) * BT)
                        pe.wait_ge(q_read, u * 4 + (b + ONE))
                        split_matmuls(bank[0][:, :], lambda k: w_hi[1][:, k, 0:P], lambda k: w_lo[1][:, k, 0:P],
                                      lambda k: u_hi[:, k, sl], lambda k: u_lo[:, k, sl]).then_inc(q_ready, 1)
                        pe.wait_ge(f_read, u * 4 + (b + ONE))
                        last = split_matmuls(bank[1][:, :], lambda k: w_hi[1][:, k, P:GC], lambda k: w_lo[1][:, k, P:GC],
                                             lambda k: u_hi[:, k, sl], lambda k: u_lo[:, k, sl])
                        last.then_inc(f_ready, 1)
                    elif kind == "M":
                        pe.wait_ge(lev_ready, u * 4 + (b + 1 + ONE))
                        pe.wait_ge(kt_read, u * 4 + (b + ONE))
                        for c in range(CH):
                            last = nc.tensor.transpose(bank[4][:, c * P:(c + 1) * P], kb[:, c * P:(c + 1) * P], ident[:, :])
                        last.then_inc(kt_mm, 1)
                        for l, (ka, qa) in enumerate(level_ops):
                            pe.wait_ge(lev_read, u * (4 * LEVELS) + (b * LEVELS + l + 1))
                            for c in range(CH):
                                if l < LEVELS - 1:
                                    last = nc.tensor.matmul(bank[2 + l % 2][:, c * P:(c + 1) * P], ka[:, c * P:(c + 1) * P],
                                                            qa[:, c * P:(c + 1) * P], start=True, stop=True)
                                else:
                                    last = nc.tensor.matmul(bank[2 + l % 2][0:64, c * P + 64:(c + 1) * P],
                                                            ka[:, c * P:c * P + 64], qa[:, c * P + 64:(c + 1) * P],
                                                            start=True, stop=True)
                            last.then_inc(lev_mm, 1)
                        pe.wait_ge(kt_read, u * 4 + (b + 1 + ONE))
                        pe.wait_ge(vg_loaded[b % 2], u * 32 + 16 * (b // 2 + 1))
                        pe.wait_ge(st_ready, u * 4 + (b + ONE))
                        for c in range(CH):
                            last = nc.tensor.matmul(bank[5][:, c * P:(c + 1) * P], k_tok[:, c, :], vg_blk[b % 2][:, c, 0:P],
                                                    start=True, stop=True)
                        last.then_inc(u_mm, 1)
                    elif kind == "O":
                        pe.wait_ge(st_ready, u * 4 + (b + 1 + ONE))
                        pe.wait_ge(out_done0, u * 2 + (b + 1) // 2 + ONE)
                        pe.wait_ge(out_done1, u * 2 + (b // 2 + ONE))
                        for c in range(CH):
                            nc.tensor.matmul(bank[6][:, c * P:(c + 1) * P], st[:, c, :], vg_blk[b % 2][:, c, 0:P],
                                             start=True, stop=False)
                            last = nc.tensor.matmul(bank[6][:, c * P:(c + 1) * P], q_in[:, c * P:(c + 1) * P],
                                                    states[b % 2][:, c, :], start=False, stop=True)
                        last.then_inc(o_mm, 1)
                    elif kind == "T":
                        phase1_tile(u + 1, b, False)

            def attention(v, with_next):
                U = v + HG_UNITS
                T0 = v * TILES
                for kind, i in attention_steps(with_next):
                    g, j = i // CH, i % CH
                    if kind == "X":
                        if i == 0:
                            pe.wait_ge(lo_done, U * 8 + 8)
                            pe.wait_ge(gate_done, U * 16 + 16)
                        else:
                            pe.wait_ge(roped_done, T0 + i)
                        sl = slice(i * P, (i + 1) * P)
                        last = split_matmuls(bank[0][:, 0:GC], lambda k: u_hi[:, k, sl], lambda k: u_lo[:, k, sl],
                                             lambda k: w_hi[1][:, k, :], lambda k: w_lo[1][:, k, :])
                        last.then_inc(qk_ready, 1)
                    elif kind == "Y":
                        pe.wait_ge(roped_done, T0 + (i + 1))
                        if i >= 1:
                            pe.wait_ge(yT_read, T0 + i)
                        if i >= 4:
                            pe.wait_ge(s_taken, T0 * 4 + (4 * (i - 4) + 6))
                        for h in range(2):
                            last = nc.tensor.transpose(bank[1][:, h * P:(h + 1) * P],
                                                       roped[i % 2][:, 2 * h:2 * h + 2, :].rearrange("p a b -> p (a b)"),
                                                       ident[:, :])
                        last.then_inc(yT_mm, 1)
                    elif kind == "G":
                        pe.wait_ge(yT_read, T0 + min(max(4 * g + 4, i + 4), TILES))
                        q = qT[g % 2]
                        lo = P if i == 0 else 0
                        for h in range(2):
                            hs = slice(HD * h, HD * h + HD)
                            pe.wait_ge(s_taken, T0 * 4 + (4 * i + 1 + h))
                            last = nc.tensor.matmul(bank[2 - h][:, lo:2 * P], q[hs, j * P:(j + 1) * P],
                                                    kT[hs, (i - 1) * P + lo:(i + 1) * P], start=True, stop=True)
                            last.then_inc(s_ready, 1)
                        for h in range(2):
                            hs = slice(HD * h, HD * h + HD)
                            pe.wait_ge(s_taken, T0 * 4 + (4 * i + 3 + h))
                            last = nc.tensor.matmul(bank[3 + h][:, 0:P * (g + 1)], q[hs, j::4], kT[hs, j:BT * (g + 1):4],
                                                    start=True, stop=True)
                            last.then_inc(s_ready, 1)
                    elif kind == "V":
                        fill = v * (FILLS * 4) + (FILLS * g + 3 * j)
                        fb_ = FILLS * g + 3 * j
                        lo = 1 if i == 0 else 0
                        for f in range(3):
                            pe.wait_ge(e_done, T0 * 4 + (4 * i + (2, 3, 4)[f]))
                            pe.wait_ge(pt_read, fill + (f + 1))
                            bk = bank[5 + (fb_ + f) % 2]
                            if f == 0:
                                src = [(2 * h + kk, p_near[:, h, kk * P:(kk + 1) * P]) for h in range(2) for kk in range(lo, 2)]
                            else:
                                src = [(kk, p_far[:, f - 1, kk * P:(kk + 1) * P]) for kk in range(g + 1)]
                            for slot, ap in src:
                                last = nc.tensor.transpose(bk[:, slot * P:(slot + 1) * P], ap, ident[:, :])
                            last.then_inc(pt_mm, 1)
                        if i >= 1:
                            pe.wait_ge(oT_read, T0 + i)
                        if j == 0:
                            pe.wait_ge(nv_landed[g % 2], v * 32 + 16 * (g // 2 + 1))
                            pe.wait_ge(fv_landed, v * 64 + 64)
                        pe.wait_ge(pt_read, fill + (1 + 2))
                        for h in range(2):
                            hs = slice(HD * h, HD * h + HD)
                            for kk in range(lo, 2):
                                nc.tensor.matmul(bank[7][hs, 0:P], near_v[:, (i - 1 + kk) % 8, hs], pT[0][:, 2 * h + kk, :],
                                                 start=(kk == lo), stop=(kk == 1))
                        for h in range(2):
                            hs = slice(HD * h, HD * h + HD)
                            pe.wait_ge(pt_read, fill + (2 + h + 2))
                            for kk in range(g + 1):
                                last = nc.tensor.matmul(bank[7][hs, P:2 * P], far_v[:, 4 * kk + j, hs], pT[1 + h][:, kk, :],
                                                        start=(kk == 0), stop=(kk == g))
                        last.then_inc(pv_mm, 1)
                    elif kind == "C":
                        g = i
                        pe.wait_ge(oT_read, T0 + 4 * (g + 1))
                        for f, src in enumerate((oT_near, oT_far)):
                            fill = v * (FILLS * 4) + (FILLS * g + 12 + f)
                            pe.wait_ge(pt_read, fill + 1)
                            for c in range(CH):
                                last = nc.tensor.transpose(bank[5 + f][:, c * P:(c + 1) * P], src[:, c * P:(c + 1) * P], ident[:, :])
                            last.then_inc(pt_mm, 1)
                    elif kind == "T":
                        phase1_tile(U + 1, i, True)

            with pe.Fori(0, AT_UNITS - 1) as v:
                attention(v, True)
            attention(AT_UNITS - 1, False)

            pe.wait_ge(pt_read, FILLS * 4 * AT_UNITS + 2)
            pe.wait_ge(lo_done, 4 * (2 * UNITS + OUT_GROUPS))

            def mixed_transposes(t):
                pe.wait_ge(mx_landed[t % 2], 32 * (t // 2 + 1))
                if t >= 2:
                    pe.wait_ge(mlo_done, t - 1)
                for k in range(KT_N):
                    last = nc.tensor.transpose(bank[1 + 2 * (t % 2) + k // 4][:, (k % 4) * P:(k % 4 + 1) * P],
                                               mx[t % 2][:, k * P:(k + 1) * P], ident[:, :])
                last.then_inc(mT_mm, 1)

            mixed_transposes(0)
            for t in range(TILES):
                if t + 1 < TILES:
                    mixed_transposes(t + 1)
                pe.wait_ge(mlo_done, t + 1)
                if t >= 2:
                    pe.wait_ge(hsum_done, t - 1)
                for n in range(OUT_GROUPS):
                    yb = (bank[5 + n // 2], (bank[7], bank[0])[n // 2])[t % 2]
                    last = split_matmuls(yb[:, (n % 2) * GC:(n % 2 + 1) * GC],
                                         lambda k: mT_hi[t % 2][:, k, :], lambda k: mT_lo[t % 2][:, k, :],
                                         lambda k: wo_hi[n][:, k, :], lambda k: wo_lo[n][:, k, :])
                last.then_inc(y_ready, 1)

        @block.scalar
        def _(act):
            def split_hi(n, i, slot):
                act.wait_ge(w_landed[i % 2], n * 32 + 16 * (i // 2 + 1))
                nc.scalar.copy(dst_of(slot, 0)[:, 2 * i:2 * i + 2, :], stage[i % 2][:, :, :]).then_inc(hi_done, 1)

            def phase1_tile(U, t, attn):
                vz = vz_bank(t, attn)
                act.wait_ge(vz_ready, U * 16 + (t + 1))
                if not (isinstance(U, int) and U == 0 and t < 2):
                    act.wait_ge(vg_stored[t % 2], U * 128 + 16 * (t // 2))
                nc.scalar.copy(vg_tile[t % 2][:, 0:P], vz[:, 0:P])
                nc.scalar.activation(vg_tile[t % 2][:, P:GC], vz[:, P:GC], ACT.Sigmoid).then_inc(sig_done, 1)
                if t in (1, 4, 7, 10):
                    if attn:
                        act.wait_ge(qk_ready, U * 16 - 16 * HG_UNITS)
                    elif not isinstance(U, int):
                        act.wait_ge(f_ready, U * 4)
                    split_hi(2 * U + 1, (t - 1) // 3, 1)

            act.wait_ge(lb_landed, 16)
            act.wait_ge(lb_step, 2)
            nc.scalar.activation(lb_in, lb_in, ACT.Exp).then_inc(lb_step, 1)
            for t in range(TILES):
                act.wait_ge(x_landed[t % 2], 16 * (t // 2 + 1))
                if t >= 1:
                    act.wait_ge(xsq_done, t)
                nc.scalar.activation(xsq, xt[t % 2], ACT.Square, accum_out=ss[:, t:t + 1]).then_inc(xsq_done, 1)
                if t >= 1:
                    act.wait_ge(un_done, t)
                    nc.scalar.copy(u_hi[:, :, (t - 1) * P:t * P], un[(t - 1) % 2]).then_inc(uhi_done, 1)
                if t < 4:
                    split_hi(0, t, 0)
                if t >= 3:
                    phase1_tile(0, t - 3, False)
            act.wait_ge(un_done, TILES)
            nc.scalar.copy(u_hi[:, :, (TILES - 1) * P:], un[(TILES - 1) % 2]).then_inc(uhi_done, 1)
            for t in range(TILES - 3, TILES):
                phase1_tile(0, t, False)

            with act.Fori(0, HG_UNITS) as u:
                for kind, b in HG_STEPS:
                    if kind == "P":
                        act.wait_ge(q_ready, u * 4 + (b + 1))
                        act.wait_ge(q_read, u * 4 + (b + ONE))
                        nc.scalar.activation(sgq, bank[0][:, :], ACT.Sigmoid).then_inc(sq_done, 1)
                        act.wait_ge(f_ready, u * 4 + (b + 1))
                        act.wait_ge(lev_ready, u * 4 + (b + ONE))
                        act.wait_ge(kt_mm, u * 4 + (b + ONE))
                        nc.scalar.activation(fb, bank[1][:, :], ACT.Sigmoid)
                        nc.scalar.activation(kb, bank[1][:, :], ACT.Sigmoid, scale=-1.0).then_inc(f_read, 1)
                        act.wait_ge(vz_ready, u * 16 + 16)
                        split_hi(2 * u + 2, b, 0)
                    elif kind == "M":
                        act.wait_ge(kt_mm, u * 4 + (b + 1 + ONE))
                        act.wait_ge(u_mm, u * 4 + (b + ONE))
                        nc.scalar.copy(k_tok.rearrange("p c k -> p (c k)"), bank[4][:, :]).then_inc(kt_read, 1)
                    elif kind == "O":
                        act.wait_ge(o_mm, u * 4 + (b + 1 + ONE))
                        act.wait_ge(osq_done, u * 4 + (b + ONE))
                        act.wait_ge(rs_done, u * 4 + (b + ONE))
                        for c in range(CH):
                            last = nc.scalar.activation(osq[:, c * P:(c + 1) * P], bank[6][:, c * P:(c + 1) * P],
                                                        ACT.Square, accum_out=ms_o[:, c:c + 1])
                        last.then_inc(osq_done, 1)
                    elif kind == "T":
                        phase1_tile(u + 1, b, False)

            def attention(v, with_next):
                U = v + HG_UNITS
                T0 = v * TILES
                for kind, i in attention_steps(with_next):
                    g, j = i // CH, i % CH
                    if kind == "Y":
                        act.wait_ge(yT_mm, T0 + (i + 1 + ONE))
                        if i == 0:
                            act.wait_ge(s_ready, T0 * 4 + ONE)
                        elif j == 0 and g >= 2:
                            act.wait_ge(s_ready, T0 * 4 + (16 * (g - 1) + ONE))
                        nc.scalar.activation(qT[g % 2][:, j * P:(j + 1) * P], bank[1][:, 0:P], ACT.Copy, scale=-(HD ** -0.5))
                        nc.scalar.copy(kT[:, i * P:(i + 1) * P], bank[1][:, P:2 * P]).then_inc(yT_read, 1)
                    elif kind == "S":
                        lo = P if i == 0 else 0
                        for n in range(4):
                            h = n % 2
                            act.wait_ge(s_taken, T0 * 4 + (4 * i + n + 1 + 4))
                            buf = p_near[:, h, lo:] if n < 2 else p_far[:, h, 0:P * (g + 1)]
                            stt = (st_near if n < 2 else st_far)[g % 2]
                            nc.scalar.activation(buf, buf, ACT.Exp, scale=-1.0, bias=stt[:, j, h:h + 1],
                                                 accum_out=stt[:, j, 2 + h:3 + h]).then_inc(e_done, 1)
                        if i in (0, 3, 6, 9):
                            act.wait_ge(vz_ready, U * 16 + 16)
                            split_hi(2 * U + 2, i // 3, 0)
                    elif kind == "V":
                        fill = v * (FILLS * 4) + (FILLS * g + 3 * j)
                        lo = 2 if i == 0 else 0
                        for f in (0, 2):
                            act.wait_ge(pt_mm, fill + (f + 1 + ONE))
                            if f == 0:
                                act.wait_ge(pv_mm, T0 + i + ONE)
                            act.wait_ge(pt_read, fill + (f + 2))
                            fb_ = FILLS * g + 3 * j + f
                            if f == 0 and i == 0:
                                nc.scalar.copy(pT[0][:, 1, :], bank[5 + fb_ % 2][:, P:2 * P])
                                nc.scalar.copy(pT[0][:, 3, :], bank[5 + fb_ % 2][:, 3 * P:4 * P]).then_inc(pt_read, 1)
                            else:
                                n = 4 if f == 0 else g + 1
                                nc.scalar.copy(pT[f][:, 0:n, :].rearrange("p a b -> p (a b)"),
                                               bank[5 + fb_ % 2][:, 0:n * P]).then_inc(pt_read, 1)
                        act.wait_ge(pv_mm, T0 + (i + 1 + ONE))
                        if j == 0 :
                            act.wait_ge(pt_mm, v * (FILLS * 4) + FILLS * g + ONE)
                        nc.scalar.copy(oT_near[:, j * P:(j + 1) * P], bank[7][:, 0:P])
                        nc.scalar.copy(oT_far[:, j::4], bank[7][:, P:2 * P]).then_inc(oT_read, 1)
                    elif kind == "C":
                        g = i
                        act.wait_ge(dve_comb, v * 8 + (2 * g + 1))
                        nc.scalar.activation(ea, ea, ACT.Exp)
                        nc.scalar.activation(eb, eb, ACT.Exp).then_inc(exp_comb, 1)
                    elif kind == "T":
                        phase1_tile(U + 1, i, True)

            with act.Fori(0, AT_UNITS - 1) as v:
                attention(v, True)
            attention(AT_UNITS - 1, False)

            act.wait_ge(qk_ready, AT_UNITS * TILES)
            for n in range(1, OUT_GROUPS):
                for i in range(PIECES):
                    split_hi(2 * UNITS + n, i, n)
            for t in range(TILES + 2):
                if t < TILES:
                    act.wait_ge(mT_mm, t + 1)
                    if t >= 2:
                        act.wait_ge(y_ready, t - 1)
                    for q in range(2):
                        last = nc.scalar.copy(mT_hi[t % 2][:, 4 * q:4 * q + 4, :].rearrange("p a b -> p (a b)"),
                                              bank[1 + 2 * (t % 2) + q][:, :])
                    last.then_inc(mhi_done, 1)
                if t >= 2:
                    act.wait_ge(hsum_done, t - 1)
                    if t >= 3:
                        act.wait_ge(hsq_done, t - 2)
                    nc.scalar.activation(hsq, hh[t % 2], ACT.Square, accum_out=ms_f[:, t - 2:t - 1]).then_inc(hsq_done, 1)

        @block.gpsimd
        def _(pool):
            def split_lo(n, i, slot):
                pool.wait_ge(hi_done, n * 4 + (i + 1))
                nc.gpsimd.tensor_tensor(dst_of(slot, 1)[:, 2 * i:2 * i + 2, :], stage[i % 2][:, :, :],
                                        dst_of(slot, 0)[:, 2 * i:2 * i + 2, :].bitcast(F32), ALU.subtract)\
                    .then_inc(lo_done, 1)

            def phase1_tile(U, t, scaled):
                if scaled:
                    pool.wait_ge(gate_done, U * 16 + (t + 1))
                    nc.gpsimd.tensor_tensor(vg_tile[t % 2][:, P:GC], vg_tile[t % 2][:, P:GC], g_cur, ALU.mult)\
                        .then_inc(gated, 1)
                if t in (1, 4, 7, 10):
                    split_lo(2 * U + 1, (t - 1) // 3, 1)

            nc.gpsimd.memset(ident[:, :], 0.0).then_inc(pool_step, 1)
            nc.gpsimd.memset(half_neg, -0.5).then_inc(pool_step, 1)
            pool.wait_ge(pool_step, 2)
            nc.gpsimd.affine_select(out=ident[:, :], in_=ident[:, :], compare_op=ALU.not_equal, fill=1.0,
                                    base=0, pattern=[[-1, P]], channel_multiplier=1).then_inc(const_ready, 1)
            step = 2
            for t in range(TILES):
                pool.wait_ge(xsq_done, t + 1)
                nc.gpsimd.tensor_scalar(ss[:, t:t + 1], ss[:, t:t + 1], 1.0 / D, EPS, ALU.mult, ALU.add).then_inc(pool_step, 1)
                step += 1
                pool.wait_ge(pool_step, step)
                nc.gpsimd.tensor_tensor(rstd[:, t:t + 1], ss[:, t:t + 1], half_neg[:, 0:1], ALU.pow).then_inc(rstd_done, 1)
                if t >= 1:
                    pool.wait_ge(uhi_done, t)
                    nc.gpsimd.tensor_tensor(u_lo[:, :, (t - 1) * P:t * P], un[(t - 1) % 2],
                                            u_hi[:, :, (t - 1) * P:t * P].bitcast(F32), ALU.subtract).then_inc(ulo_done, 1)
                if t == 0:
                    pool.wait_ge(g_landed, 16)
                    nc.gpsimd.tensor_copy(g_cur, g_all[:, 0, :]).then_inc(pool_step, 1)
                    step += 1
                if t < 4:
                    split_lo(0, t, 0)
                if t >= 5:
                    if t == 5:
                        pool.wait_ge(pool_step, step)
                    phase1_tile(0, t - 5, True)
            pool.wait_ge(uhi_done, TILES)
            nc.gpsimd.tensor_tensor(u_lo[:, :, (TILES - 1) * P:], un[(TILES - 1) % 2],
                                    u_hi[:, :, (TILES - 1) * P:].bitcast(F32), ALU.subtract).then_inc(ulo_done, 1)
            for t in range(TILES - 5, TILES):
                phase1_tile(0, t, True)

            pool.wait_ge(lb_ready, 1)
            with pool.Fori(0, HG_UNITS) as u:
                for kind, b in HG_STEPS:
                    if kind == "P":
                        if b == 0:
                            pool.wait_ge(fk_ready, u * 4 + ONE)
                            pool.wait_ge(gated, u * 16 + 16)
                            nc.gpsimd.tensor_copy(lb, lb_all[:, bass.ds(u, 1)])
                            nc.gpsimd.tensor_copy(omlb, omlb_all[:, bass.ds(u, 1)])
                            nc.gpsimd.tensor_copy(g_cur, g_all[:, bass.ds(u + 1, 1), :].rearrange("p a b -> p (a b)"))\
                                .then_inc(cur_ready, 1)
                            pool.wait_ge(cur_ready, u + 1)
                        pool.wait_ge(f_read, u * 4 + (b + 1 + ONE))
                        pool.sem_inc(passed_pool, 1)
                        nc.gpsimd.tensor_scalar(fb, fb, omlb[:, 0:1], lb[:, 0:1], ALU.mult, ALU.add)
                        nc.gpsimd.tensor_scalar(kb, kb, omlb[:, 0:1], None, ALU.mult).then_inc(fk_ready, 1)
                        split_lo(2 * u + 2, b, 0)
                    elif kind == "O":
                        pool.wait_ge(osq_done, u * 4 + (b + 1 + ONE))
                        if b % 2 == 0:
                            pool.wait_ge(out_done1, u * 2 + (b // 2 + ONE))
                        else:
                            pool.wait_ge(out_done0, u * 2 + (b + 1) // 2 + ONE)
                        pool.sem_inc(passed_pool, 1)
                        nc.gpsimd.tensor_scalar(rs_o, ms_o, 1.0 / P, EPS, ALU.mult, ALU.add).then_inc(rs_half, 1)
                        pool.wait_ge(rs_half, u * 4 + (b + 1))
                        nc.gpsimd.tensor_tensor(rs_o, rs_o, half_neg[:, 0:CH], ALU.pow).then_inc(rs_done, 1)
                    elif kind == "T":
                        phase1_tile(u + 1, b, True)

            def attention(v, with_next):
                U = v + HG_UNITS
                for kind, i in attention_steps(with_next):
                    if kind == "S" and i in (0, 3, 6, 9):
                        split_lo(2 * U + 2, i // 3, 0)
                    elif kind == "T":
                        phase1_tile(U + 1, i, False)

            with pool.Fori(0, AT_UNITS - 1) as v:
                attention(v, True)
            attention(AT_UNITS - 1, False)

            for n in range(1, OUT_GROUPS):
                for i in range(PIECES):
                    split_lo(2 * UNITS + n, i, n)
            pool.wait_ge(comb_stored, AT_UNITS * 64 + ONE)
            nc.gpsimd.memset(o_half, -0.5).then_inc(pool_step, 1)
            step += 1
            for t in range(TILES):
                pool.wait_ge(hsq_done, t + 1)
                nc.gpsimd.tensor_scalar(ms_f[:, t:t + 1], ms_f[:, t:t + 1], 1.0 / D, EPS, ALU.mult, ALU.add).then_inc(pool_step, 1)
                step += 1
                pool.wait_ge(pool_step, step)
                nc.gpsimd.tensor_tensor(rs_f[:, t:t + 1], ms_f[:, t:t + 1], o_half, ALU.pow).then_inc(frs_done, 1)

        @block.vector
        def _(dve):
            count = [0]

            def tick(ins):
                count[0] += 1
                ins.then_inc(dve_step, 1)
                return ins

            def settle():
                dve.wait_ge(dve_step, count[0])

            def restart():
                settle()
                dve.sem_clear(dve_step)
                count[0] = 0

            def tt(dst, a_, b_, op=ALU.mult):
                return nc.vector.tensor_tensor(dst, a_, b_, op)

            def phase1_tile(U, t, attn):
                vz = vz_bank(t, attn)
                dve.wait_ge(sig_done, U * 16 + (t + 1))
                tt(vg_tile[t % 2][:, P:GC], vz[:, P:GC], vg_tile[t % 2][:, P:GC]).then_inc(gate_done, 1)

            dve.wait_ge(lb_landed, 16)
            nc.vector.tensor_tensor(lb_tmp, lb_in[:, 0, :], lb_in[:, 1, :], ALU.max).then_inc(lb_step, 1)
            dve.wait_ge(lb_step, 1)
            nc.vector.tensor_tensor(lb_in, lb_in, lb_tmp[:, None, :].to_broadcast([P, 2, HG_UNITS]),
                                    ALU.subtract).then_inc(lb_step, 1)
            dve.wait_ge(lb_step, 3)
            tick(tt(lb_tmp, lb_in[:, 0, :], lb_in[:, 1, :], ALU.add))
            settle()
            tick(nc.vector.reciprocal(lb_tmp, lb_tmp))
            settle()
            tick(tt(lb_all, lb_in[:, 0, :], lb_tmp))
            settle()
            tick(nc.vector.tensor_scalar(lb_all, lb_all, 1e-6, 1.0 - 1e-6, ALU.max, ALU.min))
            settle()
            nc.vector.tensor_scalar(omlb_all, lb_all, -1.0, 1.0, ALU.mult, ALU.add).then_inc(lb_ready, 1)
            dve.wait_ge(const_ready, 17)
            for t in range(TILES + 1):
                if t < TILES:
                    dve.wait_ge(rstd_done, t + 1)
                    if t >= 2:
                        dve.wait_ge(xT_done, t - 1)
                    nc.vector.tensor_scalar(xn[t % 2], xt[t % 2], rstd[:, t:t + 1], None, ALU.mult).then_inc(xn_done, 1)
                if t >= 1:
                    dve.wait_ge(xT_done, t)
                    if t >= 3:
                        dve.wait_ge(ulo_done, t - 2)
                    for q in range(2):
                        last = tt(un[(t - 1) % 2][:, 4 * q:4 * q + 4, :],
                                  bank[1 + 2 * ((t - 1) % 2) + q][:, :].rearrange("p (k t) -> p k t", k=4),
                                  nw[:, 4 * q:4 * q + 4, None].to_broadcast([P, 4, P]))
                    last.then_inc(un_done, 1)
                if t >= 4:
                    phase1_tile(0, t - 4, False)
            for t in range(TILES - 3, TILES):
                phase1_tile(0, t, False)
            dve.wait_ge(ulo_done, TILES)
            tick(nc.vector.memset(st, 0.0))
            tick(nc.vector.memset(Rb, 1.0))
            dve.wait_ge(tri_landed, 16)
            dve.sem_inc(lev_read, 2)

            def halves(ap, h):
                v_ = ap.rearrange("p (n s h) -> p n s h", s=2, h=h)
                return v_[:, :, 0, :], v_[:, :, 1, :]

            def bc(t_ap, side, h):
                v_ = t_ap.rearrange("p (n s) -> p n s", s=2)[:, :, side]
                return v_[:, :, None].to_broadcast([P, v_.shape[1], h])

            restart()
            with dve.Fori(0, HG_UNITS) as u:
                for kind, b in HG_STEPS:
                    if kind == "P":
                        dve.wait_ge(sq_done, u * 4 + (b + 1))
                        settle()
                        tt(qb, bank[0][:, :], sgq).then_inc(q_read, 1)
                    elif kind == "L":
                        dve.wait_ge(fk_ready, u * 4 + (b + 1 + ONE))
                        dve.wait_ge(q_read, u * 4 + (b + 1 + ONE))
                        dve.wait_ge(lev_mm, u * 20 + (5 * b + 1))
                        settle()
                        f4 = fb.rearrange("p (n j) -> p n j", j=4)
                        A4 = Ab.rearrange("p (n j) -> p n j", j=4)
                        R4 = Rb.rearrange("p (n j) -> p n j", j=4)
                        A2, f2 = (z.rearrange("p (n j) -> p n j", j=2) for z in (Ab, fb))
                        tick(tt(A2[:, :, 1], f2[:, :, 0], f2[:, :, 1]))
                        tick(nc.vector.tensor_copy(A2[:, :, 0], f2[:, :, 0]))
                        tick(nc.vector.tensor_copy(R4[:, :, 2], f4[:, :, 3]))
                        settle()
                        tick(tt(R4[:, :, 0], A4[:, :, 3], f4[:, :, 1]))
                        tick(nc.vector.tensor_copy(R4[:, :, 1], A4[:, :, 3]))
                        settle()
                        tick(tt(A4[:, :, 2:4], A4[:, :, 2:4], A4[:, :, 1:2].to_broadcast([P, BT // 4, 2])))
                        A0, A1 = halves(Ab, 4)
                        R0, R1 = halves(Rb, 4)
                        V0, V1 = halves(Vb, 4)
                        q0, q1 = halves(qb, 4)
                        k0, k1 = halves(kb, 4)
                        Q0, Q1 = halves(base_q, 4)
                        K0, K1 = halves(base_k, 4)
                        tick(nc.vector.reciprocal(V0, R0))
                        settle()
                        tick(nc.vector.reciprocal(V1, A1))
                        tick(tt(K0, k0, R0))
                        tick(tt(Q1, q1, A1))
                        tick(tt(Q0, q0, V0))
                        settle()
                        tick(tt(K1, k1, V1))
                        T4 = A4[:, :, 3]
                        T4s = T4.rearrange("p (n s) -> p n s", s=2)
                        t4 = [T4s[:, :, z:z + 1].to_broadcast([P, BT // 8, 4]) for z in range(2)]
                        tick(tt(q0, q0, A0))
                        tick(tt(q1, Q1, t4[0]))
                        tick(tt(k0, K0, t4[1]))
                        tick(tt(tot[8], T4s[:, :, 0], T4s[:, :, 1]))
                        settle()
                        tick(tt(k1, k1, R1))
                        for l, (h, lev) in enumerate(((8, lev8), (16, lev16), (32, lev32), (64, lev64))):
                            dve.wait_ge(lev_mm, u * 20 + (5 * b + l + 2))
                            settle()
                            l0, l1 = halves(lev, h)
                            q0, q1 = halves(qb, h)
                            k0, k1 = halves(kb, h)
                            tick(nc.vector.tensor_copy(l0, k0))
                            tick(nc.vector.tensor_copy(l1, q1))
                            pair = tot[h].rearrange("p (n s) -> p n s", s=2)
                            tick(tt(tot[2 * h], pair[:, :, 0], pair[:, :, 1]))
                            settle()
                            tick(tt(k0, k0, bc(tot[h], 1, h)))
                            if h < 64:
                                tick(tt(q1, q1, bc(tot[h], 0, h)))
                            else:
                                dve.wait_ge(o_mm, u * 4 + (b + ONE))
                                i0, i1 = halves(q_in, h)
                                tick(tt(i1, q1, bc(tot[h], 0, h)))
                                tick(nc.vector.tensor_copy(i0, q0))
                        settle()
                        dve.sem_inc(lev_ready, 1)
                    elif kind == "M":
                        dve.wait_ge(o_mm, u * 4 + (b + ONE))
                        if b == 0:
                            tick(nc.vector.memset(states[0][:, 0, :], 0.0))
                        for l in range(LEVELS):
                            dve.wait_ge(lev_mm, u * 20 + (5 * b + l + 1 + LEVELS))
                            dve.wait_ge(lev_read, u * 20 + (5 * b + l + 2))
                            dve.sem_inc(passed_dve, 1)
                            settle()
                            src = bank[2 + l % 2][:, :].rearrange("p (c t) -> p c t", c=CH)
                            if l < 3:
                                last = nc.vector.copy_predicated(st, tri[:, l:l + 1, :].to_broadcast([P, CH, P]), src)
                            elif l == 3:
                                tick(nc.vector.tensor_copy(st[0:32, :, 32:64], src[0:32, :, 32:64]))
                                last = nc.vector.tensor_copy(st[64:96, :, 96:128], src[64:96, :, 96:128])
                            else:
                                last = nc.vector.tensor_copy(st[0:64, :, 64:128], src[0:64, :, 64:128])
                            last.then_inc(lev_read, 1)
                        dve.wait_ge(u_mm, u * 4 + (b + 1 + ONE))
                        for c in range(CH):
                            if b == BLOCKS - 1 and c == CH - 1:
                                continue
                            settle()
                            nxt = states[b % 2][:, c + 1, :] if c < CH - 1 else states[(b + 1) % 2][:, 0, :]
                            tick(nc.vector.scalar_tensor_tensor(out=nxt, in0=states[b % 2][:, c, :],
                                                                scalar=tot[128][:, c:c + 1],
                                                                in1=bank[5][:, c * P:(c + 1) * P],
                                                                op0=ALU.mult, op1=ALU.add))
                        dve.wait_ge(lev_read, u * 20 + (5 * b + LEVELS + 2))
                        settle()
                        dve.sem_inc(st_ready, 1)
                    elif kind == "O":
                        dve.wait_ge(rs_done, u * 4 + (b + 1 + ONE))
                        for c in range(CH):
                            last = (nc.vector.scalar_tensor_tensor(
                                out=vg_blk[b % 2][:, c, P:GC], in0=bank[6][:, c * P:(c + 1) * P],
                                scalar=rs_o[:, c:c + 1], in1=vg_blk[b % 2][:, c, P:GC], op0=ALU.mult, op1=ALU.mult))
                        last.then_inc((out_done0, out_done1)[b % 2], 1)
                    elif kind == "T":
                        phase1_tile(u + 1, b, False)
                restart()

            dve.sem_inc(s_taken, 4)
            dve.sem_inc(pt_read, 2)
            dve.wait_ge(tab_landed, 48)

            def attention(v, with_next):
                U = v + HG_UNITS
                T0 = v * TILES
                for kind, i in attention_steps(with_next):
                    g, j = i // CH, i % CH
                    if kind == "X":
                        dve.wait_ge(qk_ready, T0 + (i + 1))
                        if i >= 2:
                            dve.wait_ge(yT_mm, T0 + (i - 1 + ONE))
                        else:
                            dve.wait_ge(yT_mm, T0 + ONE)
                        x4 = bank[0][:, 0:GC].rearrange("p (n h c) -> p n h c", n=4, h=2)
                        r4 = roped[i % 2].rearrange("p n (h c) -> p n h c", h=2)
                        m4 = rtmp.rearrange("p n (h c) -> p n h c", h=2)
                        cos = rope_sb[:, i, 0:1, :].to_broadcast([P, 4, 32])
                        sin = rope_sb[:, i, 1:2, :].to_broadcast([P, 4, 32])
                        settle()
                        for h in range(2):
                            tick(tt(r4[:, :, h, :], x4[:, :, h, :], cos))
                            last = tick(tt(m4[:, :, h, :], x4[:, :, 1 - h, :], sin))
                        settle()
                        tick(tt(r4[:, :, 0, :], r4[:, :, 0, :], m4[:, :, 0, :], ALU.subtract))
                        tick(tt(r4[:, :, 1, :], r4[:, :, 1, :], m4[:, :, 1, :], ALU.add))
                        settle()
                        dve.sem_inc(roped_done, 1)
                    elif kind == "S":
                        lo = P if i == 0 else 0
                        for n in range(4):
                            h = n % 2
                            dve.wait_ge(s_ready, T0 * 4 + (4 * i + n + 1 + ONE))
                            if n in (0, 2):
                                f0 = v * (FILLS * 4) + (FILLS * ((i - 1) // 4) + 3 * ((i - 1) % 4) + (1 if n == 0 else 3))
                                if i >= 1:
                                    dve.wait_ge(pt_mm, f0 + ONE)
                                else:
                                    dve.wait_ge(pt_mm, v * (FILLS * 4) + ONE)
                            if n == 0 and j == 0 and g < 2:
                                dve.wait_ge(stat_stored, v * 64 + ONE)
                            if n == 0 and j == 0 and g >= 2:
                                dve.wait_ge(stat_stored, v * 64 + (16 * (g - 1) + ONE))
                            if n < 2:
                                src, msk, dst = bank[2 - h][:, lo:2 * P], near_m[:, lo:], p_near[:, h, lo:]
                            else:
                                src, msk, dst = bank[3 + h][:, 0:P * (g + 1)], far_m[:, BT - P * (g + 1):], p_far[:, h, 0:P * (g + 1)]
                            stt = (st_near if n < 2 else st_far)[g % 2]
                            dve.sem_inc(passed_dve, 1)
                            settle()
                            nc.vector.tensor_tensor_reduce(out=dst, in0=src, in1=msk, scale=1.0, scalar=3e38,
                                                           op0=ALU.add, op1=ALU.min, accum_out=stt[:, j, h:h + 1])\
                                .then_inc(s_taken, 1)
                    elif kind == "V":
                        fill = v * (FILLS * 4) + (FILLS * g + 3 * j)
                        fb_ = FILLS * g + 3 * j + 1
                        dve.wait_ge(pt_mm, fill + 2 + ONE)
                        dve.wait_ge(pv_mm, T0 + i + ONE)
                        dve.wait_ge(pt_read, fill + 3)
                        nc.vector.tensor_copy(pT[1][:, 0:g + 1, :].rearrange("p a b -> p (a b)"),
                                              bank[5 + fb_ % 2][:, 0:P * (g + 1)]).then_inc(pt_read, 1)
                    elif kind == "C":
                        g = i
                        near, far = st_near[g % 2], st_farn[g % 2]
                        fill = v * (FILLS * 4) + (FILLS * g + 12)
                        dve.wait_ge(stat_landed[g % 2], v * 32 + 16 * (g // 2 + 1))
                        settle()
                        tick(tt(top, near[:, :, 0:2], far[:, :, 0:2], ALU.min))
                        settle()
                        tick(tt(ea, top, near[:, :, 0:2], ALU.subtract))
                        tick(tt(eb, top, far[:, :, 0:2], ALU.subtract))
                        settle()
                        dve.sem_inc(dve_comb, 1)
                        dve.wait_ge(exp_comb, v * 4 + (g + 1))
                        tick(tt(den, ea, near[:, :, 2:4]))
                        tick(tt(tsum, eb, far[:, :, 2:4]))
                        settle()
                        tick(tt(den, den, tsum, ALU.add))
                        settle()
                        tick(nc.vector.reciprocal(rden, den))
                        settle()
                        tick(tt(wa, ea, rden))
                        tick(tt(wb, eb, rden))
                        settle()
                        dve.sem_inc(dve_comb, 1)
                        dve.wait_ge(pt_mm, fill + 1 + ONE)
                        dve.wait_ge(pt_read, fill + 2)
                        c4 = comb.rearrange("p c (h d) -> p (c h) d", h=2)

                        def v8(ap):
                            return ap.rearrange("p (n d) -> p n d", d=HD)

                        def w8(ap):
                            return ap.rearrange("p c h -> p (c h)")[:, :, None].to_broadcast([P, 2 * CH, HD])
                        dve.wait_ge(comb_done, v * 4 + (g + ONE))
                        tt(c4, v8(bank[5][:, :]), w8(wa)).then_inc(pt_read, 1)
                        dve.wait_ge(pt_mm, fill + 2 + ONE)
                        tick(tt(v8(bank[6][:, :]), v8(bank[6][:, :]), w8(wb)))
                        settle()
                        dve.wait_ge(pt_read, fill + 3)
                        tt(c4, v8(bank[6][:, :]), c4, ALU.add).then_inc(pt_read, 1)
                        dve.wait_ge(gate_landed, v * 64 + 16 * (g + 1))
                        dve.wait_ge(pt_read, fill + 4)
                        tt(gate, gate, comb).then_inc(comb_done, 1)
                    elif kind == "T":
                        phase1_tile(U + 1, i, True)
                restart()

            with dve.Fori(0, AT_UNITS - 1) as v:
                attention(v, True)
            attention(AT_UNITS - 1, False)

            dve.wait_ge(comb_stored, AT_UNITS * 64 + ONE)
            dve.wait_ge(tab_landed, 64)
            for t in range(TILES + 2):
                if t < TILES:
                    dve.wait_ge(mhi_done, t + 1)
                    for q in range(2):
                        last = tt(mT_lo[t % 2][:, 4 * q:4 * q + 4, :].rearrange("p a b -> p (a b)"),
                                  bank[1 + 2 * (t % 2) + q][:, :],
                                  mT_hi[t % 2][:, 4 * q:4 * q + 4, :].rearrange("p a b -> p (a b)").bitcast(F32), ALU.subtract)
                    last.then_inc(mlo_done, 1)
                if t >= 1 and t - 1 < TILES:
                    z = t - 1
                    dve.wait_ge(y_ready, z + 1)
                    if z >= 2:
                        dve.wait_ge(fin_stored[z % 2], 16 * (z // 2))
                    for q in range(2):
                        yb = (bank[5 + q], (bank[7], bank[0])[q])[z % 2]
                        last = tt(hh[z % 2][:, 512 * q:512 * q + 512], yb[:, :], xr[z % 2][:, 512 * q:512 * q + 512], ALU.add)
                    last.then_inc(hsum_done, 1)
                if t >= 2:
                    z = t - 2
                    dve.wait_ge(frs_done, z + 1)
                    nc.vector.scalar_tensor_tensor(out=hh[z % 2], in0=hh[z % 2], scalar=rs_f[:, z:z + 1], in1=fw,
                                                   op0=ALU.mult, op1=ALU.mult).then_inc(fin_done, 1)


def constants():
    half = HD // 2
    inv = (np.float32(1.0) / np.power(np.float32(10000.0), np.arange(half, dtype=np.float32) / np.float32(half))).astype(np.float32)
    ang = (np.arange(SEQ, dtype=np.float32)[:, None] * inv[None, :]).astype(np.float32)
    rope = np.stack([np.cos(ang), np.sin(ang)], 1).astype(np.float32).reshape(TILES, P, 2, half)
    rope = np.ascontiguousarray(rope.transpose(1, 0, 2, 3))
    qi = np.arange(P)[:, None]
    dist = qi + P - np.arange(2 * P)[None, :]
    near = np.where((dist >= 0) & (dist <= 128), 0.0, -MASKED).astype(np.float32)
    step = qi + (CH - 1) * P - np.arange(BT)[None, :]
    times = ((step >= 0) & (step <= 128)).astype(np.int64) + ((step >= 0) & (step % 4 == 0))
    far = np.where(times > 0, -np.log(np.maximum(times, 1)), -MASKED).astype(np.float32)
    si, ti = np.arange(P)[:, None], np.arange(P)[None, :]
    tri = [(si // 8 == ti // 8) & (si <= ti)]
    for h in (8, 16):
        tri.append((si // (2 * h) == ti // (2 * h)) & (si // h < ti // h))
    return rope, near, far, np.ascontiguousarray(np.stack(tri, 1).astype(np.int32))


def kernel(x, norm_w, w_in, hgrn_lb_logits, hg_norm_w, w_out, final_norm_w):
    import concourse.bacc as bacc
    from concourse.bass_utils import run_bass_kernel_spmd

    def tiles_of(w):
        return w.reshape(KT_N, P, GC).transpose(1, 0, 2)

    w = np.asarray(w_in)[0].reshape(D, 8, 4, P)
    groups = []
    for U in range(UNITS):
        f0 = 0 if U < HG_UNITS else 4
        for pair in ((f0 + 2, f0 + 3), (f0, f0 + 1)):
            groups.append(tiles_of(np.concatenate([w[:, c, U % 4, :] for c in pair], 1)))
    wo = np.asarray(w_out)[0]
    for n in range(OUT_GROUPS):
        groups.append(tiles_of(wo[:, n * GC:(n + 1) * GC]))
    g = np.asarray(hg_norm_w)[0].reshape(HG_UNITS, P)
    g = np.concatenate([g, np.ones((1, P), np.float32)], 0)
    rope, near, far, tri = constants()
    arrays = {
        "x": np.asarray(x)[0],
        "w_groups": np.stack(groups),
        "norm_w": np.asarray(norm_w)[0].reshape(KT_N, P).T,
        "gate_g": np.broadcast_to(g[None], (P, HG_UNITS + 1, P)),
        "lb_logits": np.asarray(hgrn_lb_logits).reshape(2, HG_UNITS, P).transpose(2, 0, 1),
        "final_w": np.broadcast_to(np.asarray(final_norm_w)[None], (P, D)),
        "rope": rope, "near_mask": near, "far_mask": far, "tri_masks": tri,
    }
    arrays = {f"in_{k}": np.ascontiguousarray(a) for k, a in arrays.items()}
    nc = bacc.Bacc("TRN2", target_bir_lowering=False, num_devices=1, dynamic_dma_scratch_size=1024)
    args = [nc.dram_tensor(k, a.shape, mybir.dt.from_np(a.dtype), kind="ExternalInput").ap() for k, a in arrays.items()]
    out = nc.dram_tensor("out_0", (SEQ, D), F32, kind="ExternalOutput").ap()
    build(nc, *args, out)
    r = run_bass_kernel_spmd(nc, [arrays], core_ids=[0])
    return r.results[0]["out_0"].reshape(1, SEQ, D)
```

```python
from contextlib import ExitStack

import numpy as np

import concourse.bass as bass
from concourse import mybir

F32 = mybir.dt.float32
F32R = mybir.dt.float32r
I32 = mybir.dt.int32
ALU = mybir.AluOpType
ACT = mybir.ActivationFunctionType

P = 128
SEQ, D = 2048, 1024
KT_N = D // P
TILES = SEQ // P
HG_UNITS, AT_UNITS = 4, 4
UNITS = HG_UNITS + AT_UNITS
GC = 256
PIECES = 4
OUT_GROUPS = D // GC
MX_SLOTS = 4
BLOCKS = 4
BT = SEQ // BLOCKS
CH = BT // P
HD = 64
EPS = 1e-6
PARTS = 3
LEVELS = 5
FILLS = 14
MASKED = -1e30
ONE = 1

HG_STEPS = ([("P", 0), ("K", 0), ("L", 0), ("P", 1), ("T", 0), ("T", 1),
             ("M", 0), ("K", 1), ("L", 1), ("P", 2), ("O", 0)] + [("T", t) for t in range(2, 6)]
            + [("M", 1), ("Z", 0), ("K", 2), ("L", 2), ("P", 3), ("O", 1)] + [("T", t) for t in range(6, 10)]
            + [("M", 2), ("Z", 1), ("K", 3), ("L", 3), ("T", 10), ("O", 2)] + [("T", t) for t in range(11, 15)]
            + [("M", 3), ("Z", 2), ("T", 15), ("O", 3), ("Z", 3)])
SPLIT_AT = {"prologue": (1, 4, 7, 10), "hgrn": (7, 9, 11, 13), "attention": (1, 4, 7, 10)}
"""Phase-1 tiles beside which the pieces of the unit's other weight group are split."""


def tiles_before(kind, b):
    return sum(k == "T" for k, _ in HG_STEPS[:HG_STEPS.index((kind, b))])


def blocks_before(kind, tile):
    return sum(k == kind for k, _ in HG_STEPS[:HG_STEPS.index(("T", tile))])


def attention_steps(with_next):
    steps = [("X", 0, 0), ("X", 1, 0), ("Y", 0, 0), ("X", 2, 0), ("Y", 1, 0), ("X", 3, 0), ("Y", 2, 0), ("X", 4, 0),
             ("Y", 3, 0)]
    steps = [(k, i, part) for k, i, _ in steps for part in (range(PARTS) if k == "X" else (0,))]
    nxt = 0
    for i in range(TILES + 2):
        if i + 5 < TILES:
            filler = [("X", i + 5, part) for part in range(PARTS)]
        elif with_next:
            filler = [("T", nxt, part) for part in range(PARTS)]
            nxt += 1
        else:
            filler = []
        if i < TILES:
            steps.append(("G", i, 0))
        steps += filler[0:1]
        closes = i >= 2 and (i - 2) % CH == CH - 1
        if closes:
            steps.append(("E", (i - 2) // CH, 0))
            steps.append(("C", (i - 2) // CH, 0))
            steps += filler[1:2]
        if 1 <= i <= TILES:
            steps.append(("F", i - 1, 0))
        if i < TILES:
            steps.append(("N", i, 0))
        if 1 <= i <= TILES:
            steps.append(("B", i - 1, 0))
        if not closes:
            steps += filler[1:2]
        if i + 4 < TILES:
            steps.append(("Y", i + 4, 0))
        if 1 <= i <= TILES:
            steps.append(("H", i - 1, 0))
        if i < TILES:
            steps.append(("R", i, 0))
        steps += filler[2:3]
        if 1 <= i <= TILES:
            steps.append(("W", i - 1, 0))
            if (i - 1) % CH == CH - 1:
                steps.append(("D", (i - 1) // CH, 0))
    if with_next:
        steps += [("T", t, part) for t in range(nxt, TILES) for part in range(PARTS)]
    return steps


def build(nc, x, w_groups, norm_w, gate_g, lb_logits, final_w, rope, near_mask, far_mask, tri_masks, out):
    vg_dram = nc.dram_tensor("values_gates", (UNITS, SEQ, GC), F32, kind="Internal").ap()
    mixed_dram = nc.dram_tensor("mixed", (SEQ, D), F32, kind="Internal").ap()
    stat_dram = nc.dram_tensor("far_stats", (AT_UNITS, BLOCKS, BT * 4), F32, kind="Internal").ap()

    with ExitStack() as ctx:
        def sb(name, shape, dt=F32):
            return ctx.enter_context(nc.sbuf_tensor(name, shape, dt))

        def sem(name):
            return ctx.enter_context(nc.semaphore(name))

        bank = [ctx.enter_context(nc.psum_tensor(f"bank{i}", [P, 512], F32)) for i in range(8)]

        u_hi = sb("u_hi", [P, KT_N, SEQ], F32R)
        u_lo = sb("u_lo", [P, KT_N, SEQ], F32R)
        w_hi = [sb(f"w_hi{s}", [P, KT_N, GC], F32R) for s in range(2)]
        w_lo = [sb(f"w_lo{s}", [P, KT_N, GC], F32R) for s in range(2)]
        stage = [sb(f"stage{s}", [P, 2, GC]) for s in range(2)]
        ident = sb("ident", [P, P])
        vg_tile = [sb(f"vg_tile{s}", [P, GC]) for s in range(2)]
        sg_tile = [sb(f"sg_tile{s}", [P, P]) for s in range(2)]
        nw = sb("nw", [P, KT_N])

        ROOM = 14000
        room = sb("room", [P, ROOM])

        class Room:
            def __init__(self):
                self.at = 0

            def take(self, *shape):
                n = int(np.prod(shape))
                a = room[:, self.at:self.at + n]
                self.at += n
                assert self.at <= ROOM, self.at
                if len(shape) == 2:
                    a = a.rearrange("p (a b) -> p a b", a=shape[0])
                elif len(shape) == 3:
                    a = a.rearrange("p (a b c) -> p a b c", a=shape[0], b=shape[1])
                return a

        r = Room()
        tri = r.take(3 * P).bitcast(I32).rearrange("p (m t) -> p m t", m=3)
        lb_all, omlb_all = r.take(HG_UNITS), r.take(HG_UNITS)
        lb, omlb = r.take(1), r.take(1)
        lb_in, lb_tmp = r.take(2, HG_UNITS), r.take(HG_UNITS)
        half_neg = r.take(16)
        g_all = r.take(HG_UNITS + 1, P)
        g_cur = r.take(P)
        qb, kb, fb, Ab, Rb, Vb = (r.take(BT) for _ in range(6))
        sgq, osq = r.take(BT), r.take(BT)
        base_k, base_q, lev8, lev16, lev32, lev64 = (r.take(BT) for _ in range(6))
        q_in = r.take(BT)
        st = r.take(CH, P)
        k_tok = r.take(CH, P)
        states = [r.take(CH, P) for _ in range(2)]
        tot = {h: r.take(BT // h) for h in (8, 16, 32, 64, 128)}
        vg_blk = [r.take(CH, GC) for _ in range(2)]
        ms_o, rs_o = r.take(CH), r.take(CH)
        p = Room()
        p.at = r.at - 2 * CH * GC - 2 * CH
        xt = [p.take(D) for _ in range(2)]
        p2 = Room()
        p2.at = (3 * P + 2 * HG_UNITS + 2 + 3 * HG_UNITS + 16 + (HG_UNITS + 1) * P + P)
        xn = [p2.take(D) for _ in range(2)]
        xsq = p2.take(D)
        un = [p2.take(KT_N, P) for _ in range(2)]
        ss, rstd = p2.take(TILES), p2.take(TILES)

        a = Room()
        kT, far_v = a.take(SEQ), a.take(TILES, P)
        near_v = a.take(8, P)
        qT = [a.take(BT) for _ in range(2)]
        p_near, p_far = a.take(2, 2 * P), a.take(2, BT)
        pT = [a.take(4, P) for _ in range(3)]
        oT_near, oT_far = a.take(BT), a.take(BT)
        gate, comb = a.take(CH, P), a.take(CH, P)
        rope_sb = a.take(TILES, 2, HD // 2)
        near_m, far_m = a.take(2 * P), a.take(BT)
        roped = [a.take(4, HD) for _ in range(2)]
        rtmp = a.take(4, HD)
        st_near = [a.take(CH, 4) for _ in range(2)]
        st_far = [a.take(CH, 4) for _ in range(2)]
        st_farn = [a.take(CH, 4) for _ in range(2)]
        top, ea, eb, den, rden, wa, wb, tsum = (a.take(CH, 2) for _ in range(8))

        o = Room()
        mx1, mx2 = o.take(D), o.take(D)
        xr = [o.take(D) for _ in range(3)]
        mx3 = o.take(D)
        xr.append(o.take(D))
        hh = [o.take(D) for _ in range(2)]
        hsq = o.take(D)
        fw = o.take(D)
        mx = [o.take(D), mx1, mx2, mx3]
        ms_f, rs_f, o_half = o.take(TILES), o.take(TILES), o.take(1)

        def strip(half, k):
            return [half[:, k, s * D:(s + 1) * D] for s in range(2)]

        mT_hi = [z.rearrange("p (k t) -> p k t", k=KT_N) for z in strip(u_hi, 4)]
        mT_lo = [z.rearrange("p (k t) -> p k t", k=KT_N) for z in strip(u_lo, 4)]
        wo_hi = w_hi + [u_hi[:, g, :].rearrange("p (k c) -> p k c", k=KT_N) for g in range(2)]
        wo_lo = w_lo + [u_lo[:, g, :].rearrange("p (k c) -> p k c", k=KT_N) for g in range(2)]

        const_ready, tri_landed, lb_landed = sem("const_ready"), sem("tri_landed"), sem("lb_landed")
        lb_step, lb_ready, g_landed = sem("lb_step"), sem("lb_ready"), sem("g_landed")
        x_landed0, x_landed1, xsq_done = sem("x_landed0"), sem("x_landed1"), sem("xsq_done")
        rstd_done, xn_done, xT_done = sem("rstd_done"), sem("xn_done"), sem("xT_done")
        un_done, uhi_done, ulo_done = sem("un_done"), sem("uhi_done"), sem("ulo_done")
        w_landed0, w_landed1, hi_done = sem("w_landed0"), sem("w_landed1"), sem("hi_done")
        lo_done, vz_ready, sig_done = sem("lo_done"), sem("vz_ready"), sem("sig_done")
        gate_done, gated, vg_stored0 = sem("gate_done"), sem("gated"), sem("vg_stored0")
        vg_stored1, q_ready, f_ready = sem("vg_stored1"), sem("q_ready"), sem("f_ready")
        sq_done, f_read, q_read = sem("sq_done"), sem("f_read"), sem("q_read")
        fk_ready, lev_ready, lev_mm = sem("fk_ready"), sem("lev_ready"), sem("lev_mm")
        lev_read, kt_mm, kt_read = sem("lev_read"), sem("kt_mm"), sem("kt_read")
        u_mm, st_ready, o_mm = sem("u_mm"), sem("st_ready"), sem("o_mm")
        osq_done, rs_done, out_done0 = sem("osq_done"), sem("rs_done"), sem("out_done0")
        out_done1, vg_loaded0, vg_loaded1 = sem("out_done1"), sem("vg_loaded0"), sem("vg_loaded1")
        out_stored0, out_stored1, cur_ready = sem("out_stored0"), sem("out_stored1"), sem("cur_ready")
        passed_sp, passed_dve, passed_pool = sem("passed_sp"), sem("passed_dve"), sem("passed_pool")
        rs_half, dve_comb, exp_comb = sem("rs_half"), sem("dve_comb"), sem("exp_comb")
        dve_step, pool_step, qk_ready = sem("dve_step"), sem("pool_step"), sem("qk_ready")
        roped_done, yT_mm, yT_read = sem("roped_done"), sem("yT_mm"), sem("yT_read")
        s_ready, s_taken, e_done = sem("s_ready"), sem("s_taken"), sem("e_done")
        pt_mm, pt_read, pv_mm = sem("pt_mm"), sem("pt_read"), sem("pv_mm")
        oT_read, tab_landed, nv_landed0 = sem("oT_read"), sem("tab_landed"), sem("nv_landed0")
        nv_landed1, fv_landed, gate_landed = sem("nv_landed1"), sem("fv_landed"), sem("gate_landed")
        stat_stored, stat_landed0, stat_landed1 = sem("stat_stored"), sem("stat_landed0"), sem("stat_landed1")
        comb_done, comb_stored, mx_landed0 = sem("comb_done"), sem("comb_stored"), sem("mx_landed0")
        mx_landed1, mT_mm, mhi_done = sem("mx_landed1"), sem("mT_mm"), sem("mhi_done")
        mlo_done, y_ready, hsum_done = sem("mlo_done"), sem("y_ready"), sem("hsum_done")
        hsq_done, frs_done, fin_done = sem("hsq_done"), sem("frs_done"), sem("fin_done")
        fin_stored0, fin_stored1 = sem("fin_stored0"), sem("fin_stored1")
        mx_landed2, mx_landed3 = sem("mx_landed2"), sem("mx_landed3")
        xr_landed = [sem(f"xr_landed{i}") for i in range(MX_SLOTS)]
        x_landed = [x_landed0, x_landed1]
        w_landed = [w_landed0, w_landed1]
        vg_stored = [vg_stored0, vg_stored1]
        vg_loaded = [vg_loaded0, vg_loaded1]
        out_stored = [out_stored0, out_stored1]
        nv_landed = [nv_landed0, nv_landed1]
        stat_landed = [stat_landed0, stat_landed1]
        mx_landed = [mx_landed0, mx_landed1, mx_landed2, mx_landed3]
        fin_stored = [fin_stored0, fin_stored1]

        def dst_of(group_slot, part):
            return (wo_hi if part == 0 else wo_lo)[group_slot]

        def out_pieces(i, with_next):
            if with_next or i < TILES - 6:
                return []
            return [(2 * UNITS + 1 + z // PIECES, z % PIECES) for z in range(2 * (i - TILES + 6), 2 * (i - TILES + 7))]

        INTER = 8

        def vz_bank(t, beside):
            return {"prologue": (bank[7], bank[0]), "hgrn": (bank[7], bank[4]),
                    "attention": (bank[0] if t < INTER else bank[1], bank[0])}[beside][t % 2]

        ctx.enter_context(nc.allow_non_contiguous_dma(reason="strips of 512 bytes and more"))
        block = ctx.enter_context(nc.Block())

        @block.sync
        def _(sp):
            def after(semaphore, value):
                sp.wait_ge(semaphore, value)
                if not isinstance(value, int):
                    sp.sem_inc(passed_sp, 1)

            def load_piece(n, i):
                if not (isinstance(n, int) and 4 * n + i < 2):
                    after(lo_done, n * 4 + (i - 1))
                sp.dma_start(stage[i % 2][:, :, :],
                             w_groups[bass.ds(n, 1), :, 2 * i:2 * i + 2, :].rearrange("a p k c -> (a p) k c"))\
                    .then_inc(w_landed[i % 2], 16)

            def phase1_store(U, t):
                after(gated, U * 16 + (t + 1))
                sp.dma_start(vg_dram[bass.ds(U, 1), t * P:(t + 1) * P, :].rearrange("a t c -> (a t) c"),
                             vg_tile[t % 2][:, :]).then_inc(vg_stored[t % 2], 16)

            for counted in (q_read, f_read, kt_read, st_ready, out_done0, out_done1, lev_ready, kt_mm,
                            u_mm, osq_done, rs_done, fk_ready, o_mm, out_stored0, out_stored1, s_ready,
                            pv_mm, pt_mm, yT_mm, stat_stored, comb_done, comb_stored):
                sp.sem_inc(counted, ONE)

            sp.dma_start(nw[:, :], norm_w).then_inc(const_ready, 16)
            for t in range(2):
                sp.dma_start(xt[t], x[t * P:(t + 1) * P, :]).then_inc(x_landed[t], 16)
            load_piece(0, 0)
            load_piece(0, 1)
            sp.dma_start(lb_in, lb_logits).then_inc(lb_landed, 16)
            sp.dma_start(tri, tri_masks).then_inc(tri_landed, 16)
            sp.dma_start(g_all, gate_g).then_inc(g_landed, 16)
            for t in range(2, TILES):
                after(xn_done, t - 1)
                sp.dma_start(xt[t % 2], x[t * P:(t + 1) * P, :]).then_inc(x_landed[t % 2], 16)
                if t < 4:
                    load_piece(0, t)
                if t - 4 in (1, 4, 7, 10):
                    load_piece(1, (t - 5) // 3)
                if t >= 7:
                    phase1_store(0, t - 7)
            for t in range(TILES - 7, TILES):
                phase1_store(0, t)

            with sp.Fori(0, HG_UNITS) as u:
                def load_vg(b):
                    if b == 0:
                        after(vg_stored[0], u * 128 + 128)
                        after(vg_stored[1], u * 128 + 128)
                    after(out_stored[b % 2], u * 32 + (16 * (b // 2) + ONE))
                    src = vg_dram[bass.ds(u, 1), b * BT:(b + 1) * BT, :]
                    sp.dma_start(vg_blk[b % 2], src.rearrange("a (c t) n -> (a t) c n", c=CH))\
                        .then_inc(vg_loaded[b % 2], 16)

                for kind, i in HG_STEPS:
                    if kind == "P":
                        if i == 0:
                            load_piece(2 * u + 2, 0)
                            load_piece(2 * u + 2, 1)
                            load_vg(0)
                            load_piece(2 * u + 2, 2)
                            load_piece(2 * u + 2, 3)
                            load_vg(1)
                    elif kind == "Z":
                        after((out_done0, out_done1)[i % 2], u * 2 + (i // 2 + 1 + ONE))
                        dst = mixed_dram[i * BT:(i + 1) * BT, bass.ds(u * P, P)]
                        sp.dma_start(dst.rearrange("(c t) n -> t c n", c=CH), vg_blk[i % 2][:, :, P:GC])\
                            .then_inc(out_stored[i % 2], 16)
                        if i < 2:
                            load_vg(i + 2)
                    elif kind == "T":
                        if i in SPLIT_AT["hgrn"]:
                            load_piece(2 * u + 3, SPLIT_AT["hgrn"].index(i))
                        phase1_store(u + 1, i)

            after(out_stored[0], HG_UNITS * 32 + ONE)
            after(out_stored[1], HG_UNITS * 32 + ONE)
            sp.dma_start(rope_sb, rope).then_inc(tab_landed, 16)
            sp.dma_start(near_m, near_mask).then_inc(tab_landed, 16)
            sp.dma_start(far_m, far_mask).then_inc(tab_landed, 16)

            def load_mixed(t):
                sp.dma_start(mx[t % MX_SLOTS], mixed_dram[t * P:(t + 1) * P, :]).then_inc(mx_landed[t % MX_SLOTS], 16)

            def load_residual(t):
                sp.dma_start(xr[t % MX_SLOTS], x[t * P:(t + 1) * P, :]).then_inc(xr_landed[t % MX_SLOTS], 16)

            def attention(v, with_next):
                U = v + HG_UNITS
                T0 = v * TILES

                def load_near(g):
                    if g >= 2:
                        after(pv_mm, T0 + (4 * (g - 1) + 1 + ONE))
                    src = vg_dram[bass.ds(U, 1), g * BT:(g + 1) * BT, 0:P]
                    sp.dma_start(near_v[:, (4 * g) % 8:(4 * g) % 8 + 4, :],
                                 src.rearrange("a (c t) n -> (a t) c n", c=CH)).then_inc(nv_landed[g % 2], 16)

                def load_gate(g):
                    after(comb_stored, v * 64 + (16 * g + ONE))
                    src = vg_dram[bass.ds(U, 1), g * BT:(g + 1) * BT, P:GC]
                    sp.dma_start(gate, src.rearrange("a (c t) n -> (a t) c n", c=CH)).then_inc(gate_landed, 16)

                after(vg_stored[0], U * 128 + 128)
                after(vg_stored[1], U * 128 + 128)
                after(pv_mm, T0 + ONE)
                load_near(0)
                for g in range(BLOCKS):
                    src = vg_dram[bass.ds(U, 1), g * BT:(g + 1) * BT, 0:P]
                    sp.dma_start(far_v[:, 4 * g:4 * g + 4, :],
                                 src.rearrange("a (i q) n -> (a i) q n", q=4)).then_inc(fv_landed, 16)
                load_near(1)
                load_gate(0)
                for kind, i, part in attention_steps(with_next):
                    if kind == "R":
                        if i in (0, 3, 6, 9):
                            load_piece(2 * U + 2, i // 3)
                        if i % 4 == 2 and 4 <= i < 12:
                            load_near(i // 4 + 1)
                        if i % 4 == 3:
                            g = i // 4
                            after(e_done, T0 * 4 + 16 * (g + 1))
                            sd = stat_dram[bass.ds(v, 1), g, :]
                            sp.dma_start(sd.rearrange("a (i w) -> (a i) w", i=P),
                                         st_far[g % 2].rearrange("p a b -> p (a b)")).then_inc(stat_stored, 16)
                            after(stat_stored, v * 64 + 16 * (g + 1) + ONE)
                            sp.dma_start(st_farn[g % 2], sd.rearrange("a (c t w) -> (a t) c w", c=CH, w=4))\
                                .then_inc(stat_landed[g % 2], 16)
                    elif kind == "C":
                        after(comb_done, v * 4 + (i + 1 + ONE))
                        dst = mixed_dram[i * BT:(i + 1) * BT, bass.ds(U * P, P)]
                        sp.dma_start(dst.rearrange("(c t) n -> t c n", c=CH), gate).then_inc(comb_stored, 16)
                        if i + 1 < BLOCKS:
                            load_gate(i + 1)
                        elif not with_next:
                            after(comb_stored, T0 * 4 + 64 + ONE)
                            sp.dma_start(fw, final_w).then_inc(tab_landed, 16)
                    elif kind == "W" and not with_next:
                        for n, q in out_pieces(i, with_next):
                            load_piece(n, q)
                        if i == TILES - 1:
                            after(roped_done, T0 + TILES)
                            after(s_ready, T0 * 4 + 64 + ONE)
                            after(comb_stored, v * 64 + 16 + ONE)
                            for t in range(MX_SLOTS):
                                load_mixed(t)
                            after(pv_mm, T0 + TILES + ONE)
                            for t in range(MX_SLOTS):
                                load_residual(t)
                    elif kind == "T" and part == PARTS - 1:
                        if i in (1, 4, 7, 10):
                            load_piece(2 * U + 3, (i - 1) // 3)
                        phase1_store(U + 1, i)

            with sp.Fori(0, AT_UNITS - 1) as v:
                attention(v, True)
            attention(AT_UNITS - 1, False)

            for t in range(MX_SLOTS, TILES):
                if t % CH == 0:
                    after(comb_stored, (AT_UNITS - 1) * 64 + 16 * (t // CH + 1) + ONE)
                after(mT_mm, t + 1 - MX_SLOTS)
                after(hsum_done, t + 1 - MX_SLOTS)
                load_mixed(t)
                load_residual(t)
                if t >= MX_SLOTS:
                    z = t - MX_SLOTS
                    after(fin_done, z + 1)
                    sp.dma_start(out[z * P:(z + 1) * P, :], hh[z % 2]).then_inc(fin_stored[z % 2], 16)
            for t in range(TILES - MX_SLOTS, TILES):
                after(fin_done, t + 1)
                sp.dma_start(out[t * P:(t + 1) * P, :], hh[t % 2]).then_inc(fin_stored[t % 2], 16)
            after(fin_stored[0], TILES // 2 * 16)
            after(fin_stored[1], TILES // 2 * 16)

        @block.tensor
        def _(pe):
            def split_matmuls(dst, lhs_hi, lhs_lo, rhs_hi, rhs_lo, tiles=range(KT_N)):
                for k in tiles:
                    nc.tensor.matmul(dst, lhs_hi(k), rhs_hi(k), start=(k == 0), stop=False)
                    nc.tensor.matmul(dst, lhs_hi(k), rhs_lo(k), start=False, stop=False)
                    last = nc.tensor.matmul(dst, lhs_lo(k), rhs_hi(k), start=False, stop=(k == KT_N - 1))
                return last

            part_tiles = [range(0, 3), range(3, 6), range(6, KT_N)]

            def phase1_part(U, t, part):
                if part == 0:
                    if t == 0:
                        pe.wait_ge(lo_done, U * 8 + 4)
                        pe.wait_ge(roped_done, U * 16 - 16 * HG_UNITS)
                    elif t < INTER:
                        pe.wait_ge(sig_done, U * 16 + t)
                    elif t == INTER:
                        pe.wait_ge(s_taken, U * 64 - (64 * HG_UNITS - 4))
                    else:
                        pe.wait_ge(sig_done, U * 16 + (t - 1))
                sl = slice(t * P, (t + 1) * P)
                last = split_matmuls(vz_bank(t, "attention")[:, 0:GC],
                                     lambda k: u_hi[:, k, sl], lambda k: u_lo[:, k, sl],
                                     lambda k: w_hi[0][:, k, :], lambda k: w_lo[0][:, k, :], part_tiles[part])
                if part == PARTS - 1:
                    last.then_inc(vz_ready, 1)

            def phase1_tile(U, t, beside):
                if t == 0:
                    pe.wait_ge(lo_done, U * 8 + 4)
                if t >= 2:
                    pe.wait_ge(sig_done, U * 16 + (t - 1))
                if beside == "hgrn" and t % 2:
                    pe.wait_ge(kt_read, U * 4 + (blocks_before("M", t) - BLOCKS + ONE))
                sl = slice(t * P, (t + 1) * P)
                last = split_matmuls(vz_bank(t, beside)[:, 0:GC],
                                     lambda k: u_hi[:, k, sl], lambda k: u_lo[:, k, sl],
                                     lambda k: w_hi[0][:, k, :], lambda k: w_lo[0][:, k, :])
                last.then_inc(vz_ready, 1)

            pe.wait_ge(const_ready, 16 + 1)
            pe.sem_inc(lev_mm, LEVELS)

            def x_transposes(t):
                pe.wait_ge(xn_done, t + 1)
                if t >= 2:
                    pe.wait_ge(un_done, t - 1)
                for k in range(KT_N):
                    last = nc.tensor.transpose(bank[1 + 2 * (t % 2) + k // 4][:, (k % 4) * P:(k % 4 + 1) * P],
                                               xn[t % 2][:, k * P:(k + 1) * P], ident[:, :])
                last.then_inc(xT_done, 1)

            x_transposes(0)
            x_transposes(1)
            for t in range(TILES):
                if t + 2 < TILES:
                    x_transposes(t + 2)
                pe.wait_ge(ulo_done, t + 1)
                phase1_tile(0, t, "prologue")

            level_ops = [(base_k, base_q), (lev8, lev8), (lev16, lev16), (lev32, lev32), (lev64, lev64)]
            with pe.Fori(0, HG_UNITS) as u:
                for kind, b in HG_STEPS:
                    if kind == "P":
                        if b == 0:
                            pe.wait_ge(lo_done, u * 8 + 8)
                            pe.wait_ge(sig_done, u * 16 + 16)
                        sl = slice(b * BT, (b + 1) * BT)
                        pe.wait_ge(q_read, u * 4 + (b + ONE))
                        split_matmuls(bank[0][:, :], lambda k: w_hi[1][:, k, 0:P], lambda k: w_lo[1][:, k, 0:P],
                                      lambda k: u_hi[:, k, sl], lambda k: u_lo[:, k, sl]).then_inc(q_ready, 1)
                        pe.wait_ge(f_read, u * 4 + (b + ONE))
                        last = split_matmuls(bank[1][:, :], lambda k: w_hi[1][:, k, P:GC], lambda k: w_lo[1][:, k, P:GC],
                                             lambda k: u_hi[:, k, sl], lambda k: u_lo[:, k, sl])
                        last.then_inc(f_ready, 1)
                    elif kind == "M":
                        pe.wait_ge(lev_ready, u * 4 + (b + 1 + ONE))
                        pe.wait_ge(kt_read, u * 4 + (b + ONE))
                        pe.wait_ge(sig_done, u * 16 + (16 + tiles_before("M", b)))
                        for c in range(CH):
                            last = nc.tensor.transpose(bank[4][:, c * P:(c + 1) * P], kb[:, c * P:(c + 1) * P], ident[:, :])
                        last.then_inc(kt_mm, 1)
                        for l, (ka, qa) in enumerate(level_ops):
                            pe.wait_ge(lev_read, u * (4 * LEVELS) + (b * LEVELS + l + 1))
                            for c in range(CH):
                                if l < LEVELS - 1:
                                    last = nc.tensor.matmul(bank[2 + l % 2][:, c * P:(c + 1) * P], ka[:, c * P:(c + 1) * P],
                                                            qa[:, c * P:(c + 1) * P], start=True, stop=True)
                                else:
                                    last = nc.tensor.matmul(bank[2 + l % 2][0:64, c * P + 64:(c + 1) * P],
                                                            ka[:, c * P:c * P + 64], qa[:, c * P + 64:(c + 1) * P],
                                                            start=True, stop=True)
                            last.then_inc(lev_mm, 1)
                        pe.wait_ge(kt_read, u * 4 + (b + 1 + ONE))
                        pe.wait_ge(vg_loaded[b % 2], u * 32 + 16 * (b // 2 + 1))
                        pe.wait_ge(st_ready, u * 4 + (b + ONE))
                        for c in range(CH):
                            last = nc.tensor.matmul(bank[5][:, c * P:(c + 1) * P], k_tok[:, c, :], vg_blk[b % 2][:, c, 0:P],
                                                    start=True, stop=True)
                        last.then_inc(u_mm, 1)
                    elif kind == "O":
                        pe.wait_ge(st_ready, u * 4 + (b + 1 + ONE))
                        pe.wait_ge(out_done0, u * 2 + (b + 1) // 2 + ONE)
                        pe.wait_ge(out_done1, u * 2 + (b // 2 + ONE))
                        for c in range(CH):
                            nc.tensor.matmul(bank[6][:, c * P:(c + 1) * P], st[:, c, :], vg_blk[b % 2][:, c, 0:P],
                                             start=True, stop=False)
                            last = nc.tensor.matmul(bank[6][:, c * P:(c + 1) * P], q_in[:, c * P:(c + 1) * P],
                                                    states[b % 2][:, c, :], start=False, stop=True)
                        last.then_inc(o_mm, 1)
                    elif kind == "T":
                        phase1_tile(u + 1, b, "hgrn")

            def attention(v, with_next):
                U = v + HG_UNITS
                T0 = v * TILES
                for kind, i, part in attention_steps(with_next):
                    g, j = i // CH, i % CH
                    if kind == "X":
                        if i == 0 and part == 0:
                            pe.wait_ge(lo_done, U * 8 + 8)
                            pe.wait_ge(sig_done, U * 16 + 16)
                        elif part == 0:
                            pe.wait_ge(roped_done, T0 + i)
                        sl = slice(i * P, (i + 1) * P)
                        last = split_matmuls(bank[0][:, 0:GC], lambda k: u_hi[:, k, sl], lambda k: u_lo[:, k, sl],
                                             lambda k: w_hi[1][:, k, :], lambda k: w_lo[1][:, k, :], part_tiles[part])
                        if part == PARTS - 1:
                            last.then_inc(qk_ready, 1)
                    elif kind == "Y":
                        pe.wait_ge(roped_done, T0 + (i + 1))
                        if i >= 1:
                            pe.wait_ge(yT_read, T0 + i)
                        if i >= 4:
                            pe.wait_ge(s_taken, T0 * 4 + (4 * (i - 4) + 6))
                        for h in range(2):
                            last = nc.tensor.transpose(bank[1][:, h * P:(h + 1) * P],
                                                       roped[i % 2][:, 2 * h:2 * h + 2, :].rearrange("p a b -> p (a b)"),
                                                       ident[:, :])
                        last.then_inc(yT_mm, 1)
                    elif kind == "G":
                        pe.wait_ge(yT_read, T0 + min(max(4 * g + 4, i + 4), TILES))
                        q = qT[g % 2]
                        lo = P if i == 0 else 0
                        for h in range(2):
                            hs = slice(HD * h, HD * h + HD)
                            pe.wait_ge(s_taken, T0 * 4 + (4 * i + 1 + h))
                            last = nc.tensor.matmul(bank[2 - h][:, lo:2 * P], q[hs, j * P:(j + 1) * P],
                                                    kT[hs, (i - 1) * P + lo:(i + 1) * P], start=True, stop=True)
                            last.then_inc(s_ready, 1)
                        for h in range(2):
                            hs = slice(HD * h, HD * h + HD)
                            pe.wait_ge(s_taken, T0 * 4 + (4 * i + 3 + h))
                            last = nc.tensor.matmul(bank[3 + h][:, 0:P * (g + 1)], q[hs, j::4], kT[hs, j:BT * (g + 1):4],
                                                    start=True, stop=True)
                            last.then_inc(s_ready, 1)
                    elif kind in ("F", "H"):
                        fill = v * (FILLS * 4) + (FILLS * g + 3 * j)
                        fb_ = FILLS * g + 3 * j
                        lo = 1 if i == 0 else 0
                        for f in ((0, 1) if kind == "F" else (2,)):
                            pe.wait_ge(e_done, T0 * 4 + (4 * i + (2, 3, 4)[f]))
                            pe.wait_ge(pt_read, fill + (f + 1))
                            bk = bank[5 + (fb_ + f) % 2]
                            if f == 0:
                                src = [(2 * h + kk, p_near[:, h, kk * P:(kk + 1) * P]) for h in range(2) for kk in range(lo, 2)]
                            else:
                                src = [(kk, p_far[:, f - 1, kk * P:(kk + 1) * P]) for kk in range(g + 1)]
                            for slot, ap in src:
                                last = nc.tensor.transpose(bk[:, slot * P:(slot + 1) * P], ap, ident[:, :])
                            last.then_inc(pt_mm, 1)
                    elif kind == "W":
                        fill = v * (FILLS * 4) + (FILLS * g + 3 * j)
                        lo = 1 if i == 0 else 0
                        if i >= 1:
                            pe.wait_ge(oT_read, T0 + i)
                        if j == 0:
                            pe.wait_ge(nv_landed[g % 2], v * 32 + 16 * (g // 2 + 1))
                            pe.wait_ge(fv_landed, v * 64 + 64)
                        pe.wait_ge(pt_read, fill + (1 + 2))
                        for h in range(2):
                            hs = slice(HD * h, HD * h + HD)
                            for kk in range(lo, 2):
                                nc.tensor.matmul(bank[7][hs, 0:P], near_v[:, (i - 1 + kk) % 8, hs], pT[0][:, 2 * h + kk, :],
                                                 start=(kk == lo), stop=(kk == 1))
                        for h in range(2):
                            hs = slice(HD * h, HD * h + HD)
                            pe.wait_ge(pt_read, fill + (2 + h + 2))
                            for kk in range(g + 1):
                                last = nc.tensor.matmul(bank[7][hs, P:2 * P], far_v[:, 4 * kk + j, hs], pT[1 + h][:, kk, :],
                                                        start=(kk == 0), stop=(kk == g))
                        last.then_inc(pv_mm, 1)
                    elif kind == "C":
                        g = i
                        pe.wait_ge(oT_read, T0 + 4 * (g + 1))
                        for f, src in enumerate((oT_near, oT_far)):
                            fill = v * (FILLS * 4) + (FILLS * g + 12 + f)
                            pe.wait_ge(pt_read, fill + 1)
                            for c in range(CH):
                                last = nc.tensor.transpose(bank[5 + f][:, c * P:(c + 1) * P], src[:, c * P:(c + 1) * P], ident[:, :])
                            last.then_inc(pt_mm, 1)
                    elif kind == "T":
                        phase1_part(U + 1, i, part)

            with pe.Fori(0, AT_UNITS - 1) as v:
                attention(v, True)
            attention(AT_UNITS - 1, False)

            pe.wait_ge(pt_read, FILLS * 4 * AT_UNITS + 2)
            pe.wait_ge(lo_done, 4 * (2 * UNITS + OUT_GROUPS))

            def mixed_transposes(t):
                pe.wait_ge(mx_landed[t % MX_SLOTS], 16 * (t // MX_SLOTS + 1))
                if t >= 2:
                    pe.wait_ge(mlo_done, t - 1)
                for k in range(KT_N):
                    last = nc.tensor.transpose(bank[1 + 2 * (t % 2) + k // 4][:, (k % 4) * P:(k % 4 + 1) * P],
                                               mx[t % MX_SLOTS][:, k * P:(k + 1) * P], ident[:, :])
                last.then_inc(mT_mm, 1)

            mixed_transposes(0)
            for t in range(TILES):
                if t + 1 < TILES:
                    mixed_transposes(t + 1)
                pe.wait_ge(mlo_done, t + 1)
                if t >= 2:
                    pe.wait_ge(hsum_done, t - 1)
                for n in range(OUT_GROUPS):
                    yb = (bank[5 + n // 2], (bank[7], bank[0])[n // 2])[t % 2]
                    last = split_matmuls(yb[:, (n % 2) * GC:(n % 2 + 1) * GC],
                                         lambda k: mT_hi[t % 2][:, k, :], lambda k: mT_lo[t % 2][:, k, :],
                                         lambda k: wo_hi[n][:, k, :], lambda k: wo_lo[n][:, k, :])
                last.then_inc(y_ready, 1)

        @block.scalar
        def _(act):
            def split_hi(n, i, slot):
                act.wait_ge(w_landed[i % 2], n * 32 + 16 * (i // 2 + 1))
                nc.scalar.copy(dst_of(slot, 0)[:, 2 * i:2 * i + 2, :], stage[i % 2][:, :, :]).then_inc(hi_done, 1)

            def phase1_tile(U, t, beside):
                vz = vz_bank(t, beside)
                act.wait_ge(vz_ready, U * 16 + (t + 1))
                if not (isinstance(U, int) and U == 0 and t < 2):
                    act.wait_ge(vg_stored[t % 2], U * 128 + 16 * (t // 2))
                nc.scalar.copy(vg_tile[t % 2][:, :], vz[:, 0:GC])
                nc.scalar.activation(sg_tile[t % 2][:, :], vz[:, P:GC], ACT.Sigmoid).then_inc(sig_done, 1)
                if t in SPLIT_AT[beside]:
                    if beside == "attention":
                        act.wait_ge(qk_ready, U * 16 - 16 * HG_UNITS)
                    elif beside == "hgrn":
                        act.wait_ge(f_ready, U * 4)
                    split_hi(2 * U + 1, SPLIT_AT[beside].index(t), 1)

            act.wait_ge(lb_landed, 16)
            act.wait_ge(lb_step, 2)
            nc.scalar.activation(lb_in, lb_in, ACT.Exp).then_inc(lb_step, 1)
            for t in range(TILES):
                act.wait_ge(x_landed[t % 2], 16 * (t // 2 + 1))
                if t >= 1:
                    act.wait_ge(xsq_done, t)
                nc.scalar.activation(xsq, xt[t % 2], ACT.Square, accum_out=ss[:, t:t + 1]).then_inc(xsq_done, 1)
                if t >= 1:
                    act.wait_ge(un_done, t)
                    nc.scalar.copy(u_hi[:, :, (t - 1) * P:t * P], un[(t - 1) % 2]).then_inc(uhi_done, 1)
                if t < 4:
                    split_hi(0, t, 0)
                if t >= 3:
                    phase1_tile(0, t - 3, "prologue")
            act.wait_ge(un_done, TILES)
            nc.scalar.copy(u_hi[:, :, (TILES - 1) * P:], un[(TILES - 1) % 2]).then_inc(uhi_done, 1)
            for t in range(TILES - 3, TILES):
                phase1_tile(0, t, "prologue")

            with act.Fori(0, HG_UNITS) as u:
                for kind, b in HG_STEPS:
                    if kind == "P":
                        if b == 0:
                            act.wait_ge(vz_ready, u * 16 + 16)
                            for i in (0, 1):
                                split_hi(2 * u + 2, i, 0)
                        act.wait_ge(q_ready, u * 4 + (b + 1))
                        act.wait_ge(q_read, u * 4 + (b + ONE))
                        nc.scalar.activation(sgq, bank[0][:, :], ACT.Sigmoid).then_inc(sq_done, 1)
                        if b == 0:
                            for i in (2, 3):
                                split_hi(2 * u + 2, i, 0)
                    elif kind == "K":
                        act.wait_ge(f_ready, u * 4 + (b + 1))
                        act.wait_ge(lev_ready, u * 4 + (b + ONE))
                        act.wait_ge(kt_mm, u * 4 + (b + ONE))
                        nc.scalar.activation(fb, bank[1][:, :], ACT.Sigmoid)
                        nc.scalar.activation(kb, bank[1][:, :], ACT.Sigmoid, scale=-1.0).then_inc(f_read, 1)
                    elif kind == "M":
                        act.wait_ge(kt_mm, u * 4 + (b + 1 + ONE))
                        act.wait_ge(u_mm, u * 4 + (b + ONE))
                        nc.scalar.copy(k_tok.rearrange("p c k -> p (c k)"), bank[4][:, :]).then_inc(kt_read, 1)
                    elif kind == "O":
                        act.wait_ge(o_mm, u * 4 + (b + 1 + ONE))
                        act.wait_ge(osq_done, u * 4 + (b + ONE))
                        act.wait_ge(rs_done, u * 4 + (b + ONE))
                        for c in range(CH):
                            last = nc.scalar.activation(osq[:, c * P:(c + 1) * P], bank[6][:, c * P:(c + 1) * P],
                                                        ACT.Square, accum_out=ms_o[:, c:c + 1])
                        last.then_inc(osq_done, 1)
                    elif kind == "T":
                        phase1_tile(u + 1, b, "hgrn")

            def attention(v, with_next):
                U = v + HG_UNITS
                T0 = v * TILES
                for kind, i, part in attention_steps(with_next):
                    g, j = i // CH, i % CH
                    if kind == "Y":
                        act.wait_ge(yT_mm, T0 + (i + 1 + ONE))
                        if i == 0:
                            act.wait_ge(s_ready, T0 * 4 + ONE)
                        elif j == 0 and g >= 2:
                            act.wait_ge(s_ready, T0 * 4 + (16 * (g - 1) + ONE))
                        nc.scalar.activation(qT[g % 2][:, j * P:(j + 1) * P], bank[1][:, 0:P], ACT.Copy, scale=-(HD ** -0.5))
                        nc.scalar.copy(kT[:, i * P:(i + 1) * P], bank[1][:, P:2 * P]).then_inc(yT_read, 1)
                    elif kind in ("N", "R"):
                        lo = P if i == 0 else 0
                        for n in ((0, 1) if kind == "N" else (2, 3)):
                            h = n % 2
                            act.wait_ge(s_taken, T0 * 4 + (4 * i + n + 1 + 4))
                            buf = p_near[:, h, lo:] if n < 2 else p_far[:, h, 0:P * (g + 1)]
                            stt = (st_near if n < 2 else st_far)[g % 2]
                            nc.scalar.activation(buf, buf, ACT.Exp, scale=-1.0, bias=stt[:, j, h:h + 1],
                                                 accum_out=stt[:, j, 2 + h:3 + h]).then_inc(e_done, 1)
                        if kind == "R" and i in (0, 3, 6, 9):
                            act.wait_ge(vz_ready, U * 16 + 16)
                            split_hi(2 * U + 2, i // 3, 0)
                    elif kind in ("F", "H"):
                        fill = v * (FILLS * 4) + (FILLS * g + 3 * j)
                        for f in ((0,) if kind == "F" else (2,)):
                            act.wait_ge(pt_mm, fill + (f + 1 + ONE))
                            if f == 0:
                                act.wait_ge(pv_mm, T0 + i + ONE)
                            act.wait_ge(pt_read, fill + (f + 2))
                            fb_ = FILLS * g + 3 * j + f
                            if f == 0 and i == 0:
                                nc.scalar.copy(pT[0][:, 1, :], bank[5 + fb_ % 2][:, P:2 * P])
                                nc.scalar.copy(pT[0][:, 3, :], bank[5 + fb_ % 2][:, 3 * P:4 * P]).then_inc(pt_read, 1)
                            else:
                                n = 4 if f == 0 else g + 1
                                nc.scalar.copy(pT[f][:, 0:n, :].rearrange("p a b -> p (a b)"),
                                               bank[5 + fb_ % 2][:, 0:n * P]).then_inc(pt_read, 1)
                    elif kind == "W":
                        act.wait_ge(pv_mm, T0 + (i + 1 + ONE))
                        if j == 0:
                            act.wait_ge(pt_mm, v * (FILLS * 4) + FILLS * g + ONE)
                        nc.scalar.copy(oT_near[:, j * P:(j + 1) * P], bank[7][:, 0:P])
                        nc.scalar.copy(oT_far[:, j::4], bank[7][:, P:2 * P]).then_inc(oT_read, 1)
                        for n, q in out_pieces(i, with_next):
                            act.wait_ge(qk_ready, T0 + TILES)
                            split_hi(n, q, n - 2 * UNITS)
                    elif kind == "D":
                        g = i
                        act.wait_ge(dve_comb, v * 4 + (g + 1))
                        nc.scalar.activation(ea, ea, ACT.Exp)
                        nc.scalar.activation(eb, eb, ACT.Exp).then_inc(exp_comb, 1)
                    elif kind == "T" and part == PARTS - 1:
                        phase1_tile(U + 1, i, "attention")

            with act.Fori(0, AT_UNITS - 1) as v:
                attention(v, True)
            attention(AT_UNITS - 1, False)

            for t in range(TILES + 2):
                if t < TILES:
                    act.wait_ge(mT_mm, t + 1)
                    if t >= 2:
                        act.wait_ge(y_ready, t - 1)
                    for q in range(2):
                        last = nc.scalar.copy(mT_hi[t % 2][:, 4 * q:4 * q + 4, :].rearrange("p a b -> p (a b)"),
                                              bank[1 + 2 * (t % 2) + q][:, :])
                    last.then_inc(mhi_done, 1)
                if t >= 2:
                    act.wait_ge(hsum_done, t - 1)
                    if t >= 3:
                        act.wait_ge(hsq_done, t - 2)
                    nc.scalar.activation(hsq, hh[t % 2], ACT.Square, accum_out=ms_f[:, t - 2:t - 1]).then_inc(hsq_done, 1)

        @block.gpsimd
        def _(pool):
            def split_lo(n, i, slot):
                pool.wait_ge(hi_done, n * 4 + (i + 1))
                nc.gpsimd.tensor_tensor(dst_of(slot, 1)[:, 2 * i:2 * i + 2, :], stage[i % 2][:, :, :],
                                        dst_of(slot, 0)[:, 2 * i:2 * i + 2, :].bitcast(F32), ALU.subtract)\
                    .then_inc(lo_done, 1)

            def phase1_tile(U, t, beside):
                pool.wait_ge(sig_done, U * 16 + (t + 1))
                z = vg_tile[t % 2][:, P:GC]
                if beside == "attention":
                    nc.gpsimd.tensor_tensor(z, z, sg_tile[t % 2][:, :], ALU.mult).then_inc(gated, 1)
                else:
                    nc.gpsimd.tensor_tensor(z, z, sg_tile[t % 2][:, :], ALU.mult).then_inc(gate_done, 1)
                    pool.wait_ge(gate_done, U * 16 + (t + 1))
                    nc.gpsimd.tensor_tensor(z, z, g_cur, ALU.mult).then_inc(gated, 1)
                if t in SPLIT_AT[beside]:
                    split_lo(2 * U + 1, SPLIT_AT[beside].index(t), 1)

            nc.gpsimd.memset(ident[:, :], 0.0).then_inc(pool_step, 1)
            nc.gpsimd.memset(half_neg, -0.5).then_inc(pool_step, 1)
            pool.wait_ge(pool_step, 2)
            nc.gpsimd.affine_select(out=ident[:, :], in_=ident[:, :], compare_op=ALU.not_equal, fill=1.0,
                                    base=0, pattern=[[-1, P]], channel_multiplier=1).then_inc(const_ready, 1)
            step = 2
            for t in range(TILES):
                pool.wait_ge(xsq_done, t + 1)
                nc.gpsimd.tensor_scalar(ss[:, t:t + 1], ss[:, t:t + 1], 1.0 / D, EPS, ALU.mult, ALU.add).then_inc(pool_step, 1)
                step += 1
                pool.wait_ge(pool_step, step)
                nc.gpsimd.tensor_tensor(rstd[:, t:t + 1], ss[:, t:t + 1], half_neg[:, 0:1], ALU.pow).then_inc(rstd_done, 1)
                if t >= 1:
                    pool.wait_ge(uhi_done, t)
                    nc.gpsimd.tensor_tensor(u_lo[:, :, (t - 1) * P:t * P], un[(t - 1) % 2],
                                            u_hi[:, :, (t - 1) * P:t * P].bitcast(F32), ALU.subtract).then_inc(ulo_done, 1)
                if t == 0:
                    pool.wait_ge(g_landed, 16)
                    nc.gpsimd.tensor_copy(g_cur, g_all[:, 0, :]).then_inc(pool_step, 1)
                    step += 1
                if t < 4:
                    split_lo(0, t, 0)
                if t >= 5:
                    if t == 5:
                        pool.wait_ge(pool_step, step)
                    phase1_tile(0, t - 5, "prologue")
            pool.wait_ge(uhi_done, TILES)
            nc.gpsimd.tensor_tensor(u_lo[:, :, (TILES - 1) * P:], un[(TILES - 1) % 2],
                                    u_hi[:, :, (TILES - 1) * P:].bitcast(F32), ALU.subtract).then_inc(ulo_done, 1)
            for t in range(TILES - 5, TILES):
                phase1_tile(0, t, "prologue")

            pool.wait_ge(lb_ready, 1)
            with pool.Fori(0, HG_UNITS) as u:
                for kind, b in HG_STEPS:
                    if kind == "P":
                        if b == 0:
                            pool.wait_ge(fk_ready, u * 4 + ONE)
                            pool.wait_ge(gated, u * 16 + 16)
                            nc.gpsimd.tensor_copy(lb, lb_all[:, bass.ds(u, 1)])
                            nc.gpsimd.tensor_copy(omlb, omlb_all[:, bass.ds(u, 1)])
                            nc.gpsimd.tensor_copy(g_cur, g_all[:, bass.ds(u + 1, 1), :].rearrange("p a b -> p (a b)"))\
                                .then_inc(cur_ready, 1)
                            pool.wait_ge(cur_ready, u + 1)
                            for i in range(PIECES):
                                split_lo(2 * u + 2, i, 0)
                    elif kind == "K":
                        pool.wait_ge(f_read, u * 4 + (b + 1 + ONE))
                        pool.sem_inc(passed_pool, 1)
                        nc.gpsimd.tensor_scalar(fb, fb, omlb[:, 0:1], lb[:, 0:1], ALU.mult, ALU.add)
                        nc.gpsimd.tensor_scalar(kb, kb, omlb[:, 0:1], None, ALU.mult).then_inc(fk_ready, 1)
                    elif kind == "O":
                        pool.wait_ge(osq_done, u * 4 + (b + 1 + ONE))
                        if b % 2 == 0:
                            pool.wait_ge(out_done1, u * 2 + (b // 2 + ONE))
                        else:
                            pool.wait_ge(out_done0, u * 2 + (b + 1) // 2 + ONE)
                        pool.sem_inc(passed_pool, 1)
                        nc.gpsimd.tensor_scalar(rs_o, ms_o, 1.0 / P, EPS, ALU.mult, ALU.add).then_inc(rs_half, 1)
                        pool.wait_ge(rs_half, u * 4 + (b + 1))
                        nc.gpsimd.tensor_tensor(rs_o, rs_o, half_neg[:, 0:CH], ALU.pow).then_inc(rs_done, 1)
                    elif kind == "T":
                        phase1_tile(u + 1, b, "hgrn")

            def attention(v, with_next):
                U = v + HG_UNITS
                for kind, i, part in attention_steps(with_next):
                    if kind == "R" and i in (0, 3, 6, 9):
                        split_lo(2 * U + 2, i // 3, 0)
                    elif kind == "W":
                        for n, q in out_pieces(i, with_next):
                            split_lo(n, q, n - 2 * UNITS)
                    elif kind == "T" and part == PARTS - 1:
                        phase1_tile(U + 1, i, "attention")

            with pool.Fori(0, AT_UNITS - 1) as v:
                attention(v, True)
            attention(AT_UNITS - 1, False)

            pool.wait_ge(comb_stored, AT_UNITS * 64 + ONE)
            nc.gpsimd.memset(o_half, -0.5).then_inc(pool_step, 1)
            step += 1
            for t in range(TILES):
                pool.wait_ge(hsq_done, t + 1)
                nc.gpsimd.tensor_scalar(ms_f[:, t:t + 1], ms_f[:, t:t + 1], 1.0 / D, EPS, ALU.mult, ALU.add).then_inc(pool_step, 1)
                step += 1
                pool.wait_ge(pool_step, step)
                nc.gpsimd.tensor_tensor(rs_f[:, t:t + 1], ms_f[:, t:t + 1], o_half, ALU.pow).then_inc(frs_done, 1)

        @block.vector
        def _(dve):
            count = [0]

            def tick(ins):
                count[0] += 1
                ins.then_inc(dve_step, 1)
                return ins

            def settle():
                dve.wait_ge(dve_step, count[0])

            def restart():
                settle()
                dve.sem_clear(dve_step)
                count[0] = 0

            def tt(dst, a_, b_, op=ALU.mult):
                return nc.vector.tensor_tensor(dst, a_, b_, op)

            dve.wait_ge(lb_landed, 16)
            nc.vector.tensor_tensor(lb_tmp, lb_in[:, 0, :], lb_in[:, 1, :], ALU.max).then_inc(lb_step, 1)
            dve.wait_ge(lb_step, 1)
            nc.vector.tensor_tensor(lb_in, lb_in, lb_tmp[:, None, :].to_broadcast([P, 2, HG_UNITS]),
                                    ALU.subtract).then_inc(lb_step, 1)
            dve.wait_ge(lb_step, 3)
            tick(tt(lb_tmp, lb_in[:, 0, :], lb_in[:, 1, :], ALU.add))
            settle()
            tick(nc.vector.reciprocal(lb_tmp, lb_tmp))
            settle()
            tick(tt(lb_all, lb_in[:, 0, :], lb_tmp))
            settle()
            tick(nc.vector.tensor_scalar(lb_all, lb_all, 1e-6, 1.0 - 1e-6, ALU.max, ALU.min))
            settle()
            nc.vector.tensor_scalar(omlb_all, lb_all, -1.0, 1.0, ALU.mult, ALU.add).then_inc(lb_ready, 1)
            dve.wait_ge(const_ready, 17)
            for t in range(TILES + 1):
                if t < TILES:
                    dve.wait_ge(rstd_done, t + 1)
                    if t >= 2:
                        dve.wait_ge(xT_done, t - 1)
                    nc.vector.tensor_scalar(xn[t % 2], xt[t % 2], rstd[:, t:t + 1], None, ALU.mult).then_inc(xn_done, 1)
                if t >= 1:
                    dve.wait_ge(xT_done, t)
                    if t >= 3:
                        dve.wait_ge(ulo_done, t - 2)
                    for q in range(2):
                        last = tt(un[(t - 1) % 2][:, 4 * q:4 * q + 4, :],
                                  bank[1 + 2 * ((t - 1) % 2) + q][:, :].rearrange("p (k t) -> p k t", k=4),
                                  nw[:, 4 * q:4 * q + 4, None].to_broadcast([P, 4, P]))
                    last.then_inc(un_done, 1)
            dve.wait_ge(ulo_done, TILES)
            tick(nc.vector.memset(st, 0.0))
            tick(nc.vector.memset(Rb, 1.0))
            dve.wait_ge(tri_landed, 16)
            dve.sem_inc(lev_read, 2)

            def halves(ap, h):
                v_ = ap.rearrange("p (n s h) -> p n s h", s=2, h=h)
                return v_[:, :, 0, :], v_[:, :, 1, :]

            def bc(t_ap, side, h):
                v_ = t_ap.rearrange("p (n s) -> p n s", s=2)[:, :, side]
                return v_[:, :, None].to_broadcast([P, v_.shape[1], h])

            restart()
            with dve.Fori(0, HG_UNITS) as u:
                for kind, b in HG_STEPS:
                    if kind == "P":
                        dve.wait_ge(sq_done, u * 4 + (b + 1))
                        settle()
                        tt(qb, bank[0][:, :], sgq).then_inc(q_read, 1)
                    elif kind == "L":
                        dve.wait_ge(fk_ready, u * 4 + (b + 1 + ONE))
                        dve.wait_ge(q_read, u * 4 + (b + 1 + ONE))
                        dve.wait_ge(lev_mm, u * 20 + (5 * b + 1))
                        settle()
                        f4 = fb.rearrange("p (n j) -> p n j", j=4)
                        A4 = Ab.rearrange("p (n j) -> p n j", j=4)
                        R4 = Rb.rearrange("p (n j) -> p n j", j=4)
                        A2, f2 = (z.rearrange("p (n j) -> p n j", j=2) for z in (Ab, fb))
                        tick(tt(A2[:, :, 1], f2[:, :, 0], f2[:, :, 1]))
                        tick(nc.vector.tensor_copy(A2[:, :, 0], f2[:, :, 0]))
                        tick(nc.vector.tensor_copy(R4[:, :, 2], f4[:, :, 3]))
                        settle()
                        tick(tt(R4[:, :, 0], A4[:, :, 3], f4[:, :, 1]))
                        tick(nc.vector.tensor_copy(R4[:, :, 1], A4[:, :, 3]))
                        settle()
                        tick(tt(A4[:, :, 2:4], A4[:, :, 2:4], A4[:, :, 1:2].to_broadcast([P, BT // 4, 2])))
                        A0, A1 = halves(Ab, 4)
                        R0, R1 = halves(Rb, 4)
                        V0, V1 = halves(Vb, 4)
                        q0, q1 = halves(qb, 4)
                        k0, k1 = halves(kb, 4)
                        Q0, Q1 = halves(base_q, 4)
                        K0, K1 = halves(base_k, 4)
                        tick(nc.vector.reciprocal(V0, R0))
                        settle()
                        tick(nc.vector.reciprocal(V1, A1))
                        tick(tt(K0, k0, R0))
                        tick(tt(Q1, q1, A1))
                        tick(tt(Q0, q0, V0))
                        settle()
                        tick(tt(K1, k1, V1))
                        T4 = A4[:, :, 3]
                        T4s = T4.rearrange("p (n s) -> p n s", s=2)
                        t4 = [T4s[:, :, z:z + 1].to_broadcast([P, BT // 8, 4]) for z in range(2)]
                        tick(tt(q0, q0, A0))
                        tick(tt(q1, Q1, t4[0]))
                        tick(tt(k0, K0, t4[1]))
                        tick(tt(tot[8], T4s[:, :, 0], T4s[:, :, 1]))
                        settle()
                        tick(tt(k1, k1, R1))
                        for l, (h, lev) in enumerate(((8, lev8), (16, lev16), (32, lev32), (64, lev64))):
                            dve.wait_ge(lev_mm, u * 20 + (5 * b + l + 2))
                            settle()
                            l0, l1 = halves(lev, h)
                            q0, q1 = halves(qb, h)
                            k0, k1 = halves(kb, h)
                            tick(nc.vector.tensor_copy(l0, k0))
                            tick(nc.vector.tensor_copy(l1, q1))
                            pair = tot[h].rearrange("p (n s) -> p n s", s=2)
                            tick(tt(tot[2 * h], pair[:, :, 0], pair[:, :, 1]))
                            settle()
                            tick(tt(k0, k0, bc(tot[h], 1, h)))
                            if h < 64:
                                tick(tt(q1, q1, bc(tot[h], 0, h)))
                            else:
                                dve.wait_ge(o_mm, u * 4 + (b + ONE))
                                i0, i1 = halves(q_in, h)
                                tick(tt(i1, q1, bc(tot[h], 0, h)))
                                tick(nc.vector.tensor_copy(i0, q0))
                        settle()
                        dve.sem_inc(lev_ready, 1)
                    elif kind == "M":
                        dve.wait_ge(o_mm, u * 4 + (b + ONE))
                        if b == 0:
                            tick(nc.vector.memset(states[0][:, 0, :], 0.0))
                        for l in range(LEVELS):
                            dve.wait_ge(lev_mm, u * 20 + (5 * b + l + 1 + LEVELS))
                            dve.wait_ge(lev_read, u * 20 + (5 * b + l + 2))
                            dve.sem_inc(passed_dve, 1)
                            settle()
                            src = bank[2 + l % 2][:, :].rearrange("p (c t) -> p c t", c=CH)
                            if l < 3:
                                last = nc.vector.copy_predicated(st, tri[:, l:l + 1, :].to_broadcast([P, CH, P]), src)
                            elif l == 3:
                                tick(nc.vector.tensor_copy(st[0:32, :, 32:64], src[0:32, :, 32:64]))
                                last = nc.vector.tensor_copy(st[64:96, :, 96:128], src[64:96, :, 96:128])
                            else:
                                last = nc.vector.tensor_copy(st[0:64, :, 64:128], src[0:64, :, 64:128])
                            last.then_inc(lev_read, 1)
                        dve.wait_ge(u_mm, u * 4 + (b + 1 + ONE))
                        for c in range(CH):
                            if b == BLOCKS - 1 and c == CH - 1:
                                continue
                            settle()
                            nxt = states[b % 2][:, c + 1, :] if c < CH - 1 else states[(b + 1) % 2][:, 0, :]
                            tick(nc.vector.scalar_tensor_tensor(out=nxt, in0=states[b % 2][:, c, :],
                                                                scalar=tot[128][:, c:c + 1],
                                                                in1=bank[5][:, c * P:(c + 1) * P],
                                                                op0=ALU.mult, op1=ALU.add))
                        dve.wait_ge(lev_read, u * 20 + (5 * b + LEVELS + 2))
                        settle()
                        dve.sem_inc(st_ready, 1)
                    elif kind == "Z":
                        dve.wait_ge(rs_done, u * 4 + (b + 1 + ONE))
                        for c in range(CH):
                            last = (nc.vector.scalar_tensor_tensor(
                                out=vg_blk[b % 2][:, c, P:GC], in0=bank[6][:, c * P:(c + 1) * P],
                                scalar=rs_o[:, c:c + 1], in1=vg_blk[b % 2][:, c, P:GC], op0=ALU.mult, op1=ALU.mult))
                        last.then_inc((out_done0, out_done1)[b % 2], 1)
                restart()

            dve.sem_inc(s_taken, 4)
            dve.sem_inc(pt_read, 2)
            dve.wait_ge(tab_landed, 48)

            def attention(v, with_next):
                U = v + HG_UNITS
                T0 = v * TILES
                for kind, i, part in attention_steps(with_next):
                    g, j = i // CH, i % CH
                    if kind == "X" and part == PARTS - 1:
                        dve.wait_ge(qk_ready, T0 + (i + 1))
                        if i >= 2:
                            dve.wait_ge(yT_mm, T0 + (i - 1 + ONE))
                        else:
                            dve.wait_ge(yT_mm, T0 + ONE)
                        x4 = bank[0][:, 0:GC].rearrange("p (n h c) -> p n h c", n=4, h=2)
                        r4 = roped[i % 2].rearrange("p n (h c) -> p n h c", h=2)
                        m4 = rtmp.rearrange("p n (h c) -> p n h c", h=2)
                        cos = rope_sb[:, i, 0:1, :].to_broadcast([P, 4, 32])
                        sin = rope_sb[:, i, 1:2, :].to_broadcast([P, 4, 32])
                        settle()
                        for h in range(2):
                            tick(tt(r4[:, :, h, :], x4[:, :, h, :], cos))
                            last = tick(tt(m4[:, :, h, :], x4[:, :, 1 - h, :], sin))
                        settle()
                        tick(tt(r4[:, :, 0, :], r4[:, :, 0, :], m4[:, :, 0, :], ALU.subtract))
                        tick(tt(r4[:, :, 1, :], r4[:, :, 1, :], m4[:, :, 1, :], ALU.add))
                        settle()
                        dve.sem_inc(roped_done, 1)
                    elif kind in ("N", "R"):
                        lo = P if i == 0 else 0
                        for n in ((0, 1) if kind == "N" else (2, 3)):
                            h = n % 2
                            dve.wait_ge(s_ready, T0 * 4 + (4 * i + n + 1 + ONE))
                            if n != 1:
                                before = FILLS * ((i - 1) // 4) + 3 * ((i - 1) % 4) + max(n, 1) if i else 0
                                dve.wait_ge(pt_mm, v * (FILLS * 4) + (before + ONE))
                            if n == 0 and j == 0 and g < 2:
                                dve.wait_ge(stat_stored, v * 64 + ONE)
                            if n == 0 and j == 0 and g >= 2:
                                dve.wait_ge(stat_stored, v * 64 + (16 * (g - 1) + ONE))
                            if n < 2:
                                src, msk, dst = bank[2 - h][:, lo:2 * P], near_m[:, lo:], p_near[:, h, lo:]
                            else:
                                src, msk, dst = bank[3 + h][:, 0:P * (g + 1)], far_m[:, BT - P * (g + 1):], p_far[:, h, 0:P * (g + 1)]
                            stt = (st_near if n < 2 else st_far)[g % 2]
                            dve.sem_inc(passed_dve, 1)
                            settle()
                            nc.vector.tensor_tensor_reduce(out=dst, in0=src, in1=msk, scale=1.0, scalar=3e38,
                                                           op0=ALU.add, op1=ALU.min, accum_out=stt[:, j, h:h + 1])\
                                .then_inc(s_taken, 1)
                    elif kind == "B":
                        fill = v * (FILLS * 4) + (FILLS * g + 3 * j)
                        fb_ = FILLS * g + 3 * j + 1
                        dve.wait_ge(pt_mm, fill + 2 + ONE)
                        dve.wait_ge(pv_mm, T0 + i + ONE)
                        dve.wait_ge(pt_read, fill + 3)
                        nc.vector.tensor_copy(pT[1][:, 0:g + 1, :].rearrange("p a b -> p (a b)"),
                                              bank[5 + fb_ % 2][:, 0:P * (g + 1)]).then_inc(pt_read, 1)
                    elif kind == "D":
                        g = i
                        near, far = st_near[g % 2], st_farn[g % 2]
                        dve.wait_ge(stat_landed[g % 2], v * 32 + 16 * (g // 2 + 1))
                        settle()
                        tick(tt(top, near[:, :, 0:2], far[:, :, 0:2], ALU.min))
                        settle()
                        tick(tt(ea, top, near[:, :, 0:2], ALU.subtract))
                        tick(tt(eb, top, far[:, :, 0:2], ALU.subtract))
                        settle()
                        dve.sem_inc(dve_comb, 1)
                    elif kind == "E":
                        g = i
                        near, far = st_near[g % 2], st_farn[g % 2]
                        dve.wait_ge(exp_comb, v * 4 + (g + 1))
                        tick(tt(den, ea, near[:, :, 2:4]))
                        tick(tt(tsum, eb, far[:, :, 2:4]))
                        settle()
                        tick(tt(den, den, tsum, ALU.add))
                        settle()
                        tick(nc.vector.reciprocal(rden, den))
                        settle()
                        tick(tt(wa, ea, rden))
                        tick(tt(wb, eb, rden))
                    elif kind == "C":
                        g = i
                        fill = v * (FILLS * 4) + (FILLS * g + 12)
                        settle()
                        dve.wait_ge(pt_mm, fill + 1 + ONE)
                        dve.wait_ge(pt_read, fill + 2)
                        c4 = comb.rearrange("p c (h d) -> p (c h) d", h=2)

                        def v8(ap):
                            return ap.rearrange("p (n d) -> p n d", d=HD)

                        def w8(ap):
                            return ap.rearrange("p c h -> p (c h)")[:, :, None].to_broadcast([P, 2 * CH, HD])
                        dve.wait_ge(comb_done, v * 4 + (g + ONE))
                        tt(c4, v8(bank[5][:, :]), w8(wa)).then_inc(pt_read, 1)
                        dve.wait_ge(pt_mm, fill + 2 + ONE)
                        tick(tt(v8(bank[6][:, :]), v8(bank[6][:, :]), w8(wb)))
                        settle()
                        dve.wait_ge(pt_read, fill + 3)
                        tt(c4, v8(bank[6][:, :]), c4, ALU.add).then_inc(pt_read, 1)
                        dve.wait_ge(gate_landed, v * 64 + 16 * (g + 1))
                        dve.wait_ge(pt_read, fill + 4)
                        tt(gate, gate, comb).then_inc(comb_done, 1)
                restart()

            with dve.Fori(0, AT_UNITS - 1) as v:
                attention(v, True)
            attention(AT_UNITS - 1, False)

            dve.wait_ge(tab_landed, 64)
            for t in range(TILES + 2):
                if t < TILES:
                    dve.wait_ge(mhi_done, t + 1)
                    for q in range(2):
                        last = tt(mT_lo[t % 2][:, 4 * q:4 * q + 4, :].rearrange("p a b -> p (a b)"),
                                  bank[1 + 2 * (t % 2) + q][:, :],
                                  mT_hi[t % 2][:, 4 * q:4 * q + 4, :].rearrange("p a b -> p (a b)").bitcast(F32), ALU.subtract)
                    last.then_inc(mlo_done, 1)
                if t >= 1 and t - 1 < TILES:
                    z = t - 1
                    dve.wait_ge(y_ready, z + 1)
                    dve.wait_ge(xr_landed[z % MX_SLOTS], 16 * (z // MX_SLOTS + 1))
                    if z >= 2:
                        dve.wait_ge(fin_stored[z % 2], 16 * (z // 2))
                    for q in range(2):
                        yb = (bank[5 + q], (bank[7], bank[0])[q])[z % 2]
                        last = tt(hh[z % 2][:, 512 * q:512 * q + 512], yb[:, :], xr[z % MX_SLOTS][:, 512 * q:512 * q + 512], ALU.add)
                    last.then_inc(hsum_done, 1)
                if t >= 2:
                    z = t - 2
                    dve.wait_ge(frs_done, z + 1)
                    nc.vector.scalar_tensor_tensor(out=hh[z % 2], in0=hh[z % 2], scalar=rs_f[:, z:z + 1], in1=fw,
                                                   op0=ALU.mult, op1=ALU.mult).then_inc(fin_done, 1)


def constants():
    half = HD // 2
    inv = (np.float32(1.0) / np.power(np.float32(10000.0), np.arange(half, dtype=np.float32) / np.float32(half))).astype(np.float32)
    ang = (np.arange(SEQ, dtype=np.float32)[:, None] * inv[None, :]).astype(np.float32)
    rope = np.stack([np.cos(ang), np.sin(ang)], 1).astype(np.float32).reshape(TILES, P, 2, half)
    rope = np.ascontiguousarray(rope.transpose(1, 0, 2, 3))
    qi = np.arange(P)[:, None]
    dist = qi + P - np.arange(2 * P)[None, :]
    near = np.where((dist >= 0) & (dist <= 128), 0.0, -MASKED).astype(np.float32)
    step = qi + (CH - 1) * P - np.arange(BT)[None, :]
    times = ((step >= 0) & (step <= 128)).astype(np.int64) + ((step >= 0) & (step % 4 == 0))
    far = np.where(times > 0, -np.log(np.maximum(times, 1)), -MASKED).astype(np.float32)
    si, ti = np.arange(P)[:, None], np.arange(P)[None, :]
    tri = [(si // 8 == ti // 8) & (si <= ti)]
    for h in (8, 16):
        tri.append((si // (2 * h) == ti // (2 * h)) & (si // h < ti // h))
    return rope, near, far, np.ascontiguousarray(np.stack(tri, 1).astype(np.int32))


def kernel(x, norm_w, w_in, hgrn_lb_logits, hg_norm_w, w_out, final_norm_w):
    import concourse.bacc as bacc
    from concourse.bass_utils import run_bass_kernel_spmd

    def tiles_of(w):
        return w.reshape(KT_N, P, GC).transpose(1, 0, 2)

    w = np.asarray(w_in)[0].reshape(D, 8, 4, P)
    groups = []
    for U in range(UNITS):
        f0 = 0 if U < HG_UNITS else 4
        for pair in ((f0 + 2, f0 + 3), (f0, f0 + 1)):
            groups.append(tiles_of(np.concatenate([w[:, c, U % 4, :] for c in pair], 1)))
    wo = np.asarray(w_out)[0]
    for n in range(OUT_GROUPS):
        groups.append(tiles_of(wo[:, n * GC:(n + 1) * GC]))
    g = np.asarray(hg_norm_w)[0].reshape(HG_UNITS, P)
    g = np.concatenate([g, np.ones((1, P), np.float32)], 0)
    rope, near, far, tri = constants()
    arrays = {
        "x": np.asarray(x)[0],
        "w_groups": np.stack(groups),
        "norm_w": np.asarray(norm_w)[0].reshape(KT_N, P).T,
        "gate_g": np.broadcast_to(g[None], (P, HG_UNITS + 1, P)),
        "lb_logits": np.asarray(hgrn_lb_logits).reshape(2, HG_UNITS, P).transpose(2, 0, 1),
        "final_w": np.broadcast_to(np.asarray(final_norm_w)[None], (P, D)),
        "rope": rope, "near_mask": near, "far_mask": far, "tri_masks": tri,
    }
    arrays = {f"in_{k}": np.ascontiguousarray(a) for k, a in arrays.items()}
    nc = bacc.Bacc("TRN2", target_bir_lowering=False, num_devices=1, dynamic_dma_scratch_size=1024)
    args = [nc.dram_tensor(k, a.shape, mybir.dt.from_np(a.dtype), kind="ExternalInput").ap() for k, a in arrays.items()]
    out = nc.dram_tensor("out_0", (SEQ, D), F32, kind="ExternalOutput").ap()
    build(nc, *args, out)
    r = run_bass_kernel_spmd(nc, [arrays], core_ids=[0])
    return r.results[0]["out_0"].reshape(1, SEQ, D)
```

```python
from contextlib import ExitStack

import numpy as np

import concourse.bass as bass
from concourse import mybir

F32 = mybir.dt.float32
F32R = mybir.dt.float32r
I32 = mybir.dt.int32
ALU = mybir.AluOpType
ACT = mybir.ActivationFunctionType

P = 128
SEQ, D = 2048, 1024
KT_N = D // P
TILES = SEQ // P
HG_UNITS, AT_UNITS = 4, 4
UNITS = HG_UNITS + AT_UNITS
GC = 256
PIECES = 4
OUT_GROUPS = D // GC
X_SLOTS = 4
MX_SLOTS = 4
BLOCKS = 4
BT = SEQ // BLOCKS
CH = BT // P
HD = 64
EPS = 1e-6
PARTS = 3
LEVELS = 5
FILLS = 14
MASKED = -1e30
ONE = 1

HG_STEPS = ([("P", 0), ("K", 0), ("L", 0), ("P", 1)] + [("T", t) for t in range(5)]
            + [("M", 0), ("K", 1), ("L", 1), ("P", 2), ("O", 0), ("T", 5), ("T", 6)]
            + [("M", 1), ("Z", 0), ("K", 2), ("L", 2), ("P", 3), ("O", 1), ("T", 7), ("T", 8)]
            + [("M", 2), ("Z", 1), ("K", 3), ("L", 3), ("T", 9), ("O", 2)] + [("T", t) for t in range(10, 15)]
            + [("M", 3), ("Z", 2), ("T", 15), ("O", 3), ("Z", 3)])
SPLIT_AT = {"prologue": (1, 4, 7, 10), "hgrn": (8, 10, 11, 13), "attention": (1, 4, 7, 10)}
"""Phase-1 tiles beside which the pieces of the unit's other weight group are split."""


def tiles_before(kind, b):
    return sum(k == "T" for k, _ in HG_STEPS[:HG_STEPS.index((kind, b))])


def odd_before(kind, b):
    return tiles_before(kind, b) // 2 * 2


def blocks_before(kind, tile):
    return sum(k == kind for k, _ in HG_STEPS[:HG_STEPS.index(("T", tile))])


def attention_steps(with_next):
    steps = [("X", 0, 0), ("X", 1, 0), ("Y", 0, 0), ("X", 2, 0), ("Y", 1, 0), ("X", 3, 0), ("Y", 2, 0), ("X", 4, 0),
             ("Y", 3, 0)]
    steps = [(k, i, part) for k, i, _ in steps for part in (range(PARTS) if k == "X" else (0,))]
    nxt = 0
    for i in range(TILES + 2):
        if i + 5 < TILES:
            filler = [("X", i + 5, part) for part in range(PARTS)]
        elif with_next:
            filler = [("T", nxt, part) for part in range(PARTS)]
            nxt += 1
        else:
            filler = []
        if i < TILES:
            steps.append(("G", i, 0))
        steps += filler[0:1]
        closes = i >= 2 and (i - 2) % CH == CH - 1
        if closes:
            steps.append(("E", (i - 2) // CH, 0))
            steps.append(("C", (i - 2) // CH, 0))
            steps += filler[1:2]
        if 1 <= i <= TILES:
            steps.append(("F", i - 1, 0))
        if i < TILES:
            steps.append(("N", i, 0))
        if 1 <= i <= TILES:
            steps.append(("B", i - 1, 0))
        if not closes:
            steps += filler[1:2]
        if i + 4 < TILES:
            steps.append(("Y", i + 4, 0))
        if 1 <= i <= TILES:
            steps.append(("H", i - 1, 0))
        if i < TILES:
            steps.append(("R", i, 0))
        steps += filler[2:3]
        if 1 <= i <= TILES:
            steps.append(("W", i - 1, 0))
            if (i - 1) % CH == CH - 1:
                steps.append(("D", (i - 1) // CH, 0))
    if with_next:
        steps += [("T", t, part) for t in range(nxt, TILES) for part in range(PARTS)]
    return steps


def build(nc, x, w_groups, norm_w, gate_g, lb_logits, final_w, rope, near_mask, far_mask, tri_masks, out):
    vg_dram = nc.dram_tensor("values_gates", (UNITS, SEQ, GC), F32, kind="Internal").ap()
    mixed_dram = nc.dram_tensor("mixed", (SEQ, D), F32, kind="Internal").ap()
    stat_dram = nc.dram_tensor("far_stats", (AT_UNITS, BLOCKS, BT * 4), F32, kind="Internal").ap()

    with ExitStack() as ctx:
        def sb(name, shape, dt=F32):
            return ctx.enter_context(nc.sbuf_tensor(name, shape, dt))

        def sem(name):
            return ctx.enter_context(nc.semaphore(name))

        bank = [ctx.enter_context(nc.psum_tensor(f"bank{i}", [P, 512], F32)) for i in range(8)]

        u_hi = sb("u_hi", [P, KT_N, SEQ], F32R)
        u_lo = sb("u_lo", [P, KT_N, SEQ], F32R)
        w_hi = [sb(f"w_hi{s}", [P, KT_N, GC], F32R) for s in range(2)]
        w_lo = [sb(f"w_lo{s}", [P, KT_N, GC], F32R) for s in range(2)]
        stage = [sb(f"stage{s}", [P, 2, GC]) for s in range(2)]
        ident = sb("ident", [P, P])
        vg_tile = [sb(f"vg_tile{s}", [P, GC]) for s in range(2)]
        sg_tile = [sb(f"sg_tile{s}", [P, P]) for s in range(2)]
        nw = sb("nw", [P, KT_N])

        ROOM = 14160
        room = sb("room", [P, ROOM])

        class Room:
            def __init__(self):
                self.at = 0

            def take(self, *shape):
                n = int(np.prod(shape))
                a = room[:, self.at:self.at + n]
                self.at += n
                assert self.at <= ROOM, self.at
                if len(shape) == 2:
                    a = a.rearrange("p (a b) -> p a b", a=shape[0])
                elif len(shape) == 3:
                    a = a.rearrange("p (a b c) -> p a b c", a=shape[0], b=shape[1])
                return a

        r = Room()
        tri = r.take(3 * P).bitcast(I32).rearrange("p (m t) -> p m t", m=3)
        lb_all, omlb_all = r.take(HG_UNITS), r.take(HG_UNITS)
        lb, omlb = r.take(1), r.take(1)
        lb_in, lb_tmp = r.take(2, HG_UNITS), r.take(HG_UNITS)
        half_neg = r.take(16)
        g_all = r.take(HG_UNITS + 1, P)
        g_cur = r.take(P)
        qb, kb, fb, Ab, Rb, Vb = (r.take(BT) for _ in range(6))
        sgq, osq = r.take(BT), r.take(BT)
        base_k, base_q, lev8, lev16, lev32, lev64 = (r.take(BT) for _ in range(6))
        q_in = r.take(BT)
        st = r.take(CH, P)
        k_tok = r.take(CH, P)
        states = [r.take(CH, P) for _ in range(2)]
        tot = {h: r.take(BT // h) for h in (8, 16, 32, 64, 128)}
        vg_blk = [r.take(CH, GC) for _ in range(2)]
        ms_o, rs_o = r.take(CH), r.take(CH)
        p = Room()
        p.at = r.at - 2 * CH * GC - 2 * CH
        xt = [p.take(D) for _ in range(2)]
        p2 = Room()
        p2.at = (3 * P + 2 * HG_UNITS + 2 + 3 * HG_UNITS + 16 + (HG_UNITS + 1) * P + P)
        xn = [p2.take(D) for _ in range(2)]
        xsq = p2.take(D)
        un = [p2.take(KT_N, P) for _ in range(2)]
        xt += [p2.take(D) for _ in range(2)]
        ss, rstd = p2.take(TILES), p2.take(TILES)
        assert p2.at <= r.at - 2 * CH * GC - 2 * CH

        c = Room()
        c.at = r.at
        rope_at = r.at
        rope_sb = c.take(TILES, 2, HD // 2)

        a = Room()
        roped = [a.take(4, HD) for _ in range(2)]
        rtmp = a.take(4, HD)
        o_at = a.at
        kT, far_v = a.take(SEQ), a.take(TILES, P)
        near_v = a.take(8, P)
        qT = [a.take(BT) for _ in range(2)]
        p_near, p_far = a.take(2, 2 * P), a.take(2, BT)
        pT = [a.take(4, P) for _ in range(3)]
        oT_near, oT_far = a.take(BT), a.take(BT)
        gate, comb = a.take(CH, P), a.take(CH, P)
        near_m, far_m = a.take(2 * P), a.take(BT)
        st_near = [a.take(CH, 4) for _ in range(2)]
        st_far = [a.take(CH, 4) for _ in range(2)]
        st_farn = [a.take(CH, 4) for _ in range(2)]
        top, ea, eb, den, rden, wa, wb, tsum = (a.take(CH, 2) for _ in range(8))
        assert a.at <= rope_at

        o = Room()
        o.at = o_at
        mx1, mx2 = o.take(D), o.take(D)
        xr = [o.take(D) for _ in range(3)]
        mx3 = o.take(D)
        xr.append(o.take(D))
        hh = [o.take(D) for _ in range(2)]
        hsq = o.take(D)
        fw = o.take(D)
        mx = [room[:, rope_at:rope_at + D], mx1, mx2, mx3]
        ms_f, rs_f, o_half = o.take(TILES), o.take(TILES), o.take(1)

        def strip(half, k):
            return [half[:, k, s * D:(s + 1) * D] for s in range(2)]

        mT_hi = [z.rearrange("p (k t) -> p k t", k=KT_N) for z in strip(u_hi, 4)]
        mT_lo = [z.rearrange("p (k t) -> p k t", k=KT_N) for z in strip(u_lo, 4)]
        wo_hi = w_hi + [u_hi[:, g, :].rearrange("p (k c) -> p k c", k=KT_N) for g in range(2)]
        wo_lo = w_lo + [u_lo[:, g, :].rearrange("p (k c) -> p k c", k=KT_N) for g in range(2)]

        const_ready, tri_landed, lb_landed = sem("const_ready"), sem("tri_landed"), sem("lb_landed")
        lb_step, lb_ready, g_landed = sem("lb_step"), sem("lb_ready"), sem("g_landed")
        x_landed0, x_landed1, xsq_done = sem("x_landed0"), sem("x_landed1"), sem("xsq_done")
        rstd_done, xn_done, xT_done = sem("rstd_done"), sem("xn_done"), sem("xT_done")
        un_done, uhi_done, ulo_done = sem("un_done"), sem("uhi_done"), sem("ulo_done")
        w_landed0, w_landed1, hi_done = sem("w_landed0"), sem("w_landed1"), sem("hi_done")
        lo_done, vz_ready, sig_done = sem("lo_done"), sem("vz_ready"), sem("sig_done")
        gate_done, gated, vg_stored0 = sem("gate_done"), sem("gated"), sem("vg_stored0")
        vg_stored1, q_ready, f_ready = sem("vg_stored1"), sem("q_ready"), sem("f_ready")
        sq_done, f_read, q_read = sem("sq_done"), sem("f_read"), sem("q_read")
        fk_ready, lev_ready, lev_mm = sem("fk_ready"), sem("lev_ready"), sem("lev_mm")
        lev_read, kt_mm, kt_read = sem("lev_read"), sem("kt_mm"), sem("kt_read")
        u_mm, st_ready, o_mm = sem("u_mm"), sem("st_ready"), sem("o_mm")
        osq_done, rs_done, out_done0 = sem("osq_done"), sem("rs_done"), sem("out_done0")
        out_done1, vg_loaded0, vg_loaded1 = sem("out_done1"), sem("vg_loaded0"), sem("vg_loaded1")
        out_stored0, out_stored1, cur_ready = sem("out_stored0"), sem("out_stored1"), sem("cur_ready")
        passed_sp, passed_dve, passed_pool = sem("passed_sp"), sem("passed_dve"), sem("passed_pool")
        rs_half, dve_comb, exp_comb = sem("rs_half"), sem("dve_comb"), sem("exp_comb")
        dve_step, pool_step, qk_ready = sem("dve_step"), sem("pool_step"), sem("qk_ready")
        roped_done, yT_mm, yT_read = sem("roped_done"), sem("yT_mm"), sem("yT_read")
        s_ready, s_taken, e_done = sem("s_ready"), sem("s_taken"), sem("e_done")
        pt_mm, pt_read, pv_mm = sem("pt_mm"), sem("pt_read"), sem("pv_mm")
        oT_read, tab_landed, nv_landed0 = sem("oT_read"), sem("tab_landed"), sem("nv_landed0")
        nv_landed1, fv_landed, gate_landed = sem("nv_landed1"), sem("fv_landed"), sem("gate_landed")
        stat_stored, stat_landed0, stat_landed1 = sem("stat_stored"), sem("stat_landed0"), sem("stat_landed1")
        comb_done, comb_stored, mx_landed0 = sem("comb_done"), sem("comb_stored"), sem("mx_landed0")
        mx_landed1, mT_mm, mhi_done = sem("mx_landed1"), sem("mT_mm"), sem("mhi_done")
        mlo_done, y_ready, hsum_done = sem("mlo_done"), sem("y_ready"), sem("hsum_done")
        hsq_done, frs_done, fin_done = sem("hsq_done"), sem("frs_done"), sem("fin_done")
        fin_stored0, fin_stored1 = sem("fin_stored0"), sem("fin_stored1")
        mx_landed2, mx_landed3 = sem("mx_landed2"), sem("mx_landed3")
        rope_landed = sem("rope_landed")
        xr_landed = [sem(f"xr_landed{i}") for i in range(MX_SLOTS)]
        x_landed = [x_landed0, x_landed1, sem("x_landed2"), sem("x_landed3")]
        w_landed = [w_landed0, w_landed1]
        vg_stored = [vg_stored0, vg_stored1]
        vg_loaded = [vg_loaded0, vg_loaded1]
        out_stored = [out_stored0, out_stored1]
        nv_landed = [nv_landed0, nv_landed1]
        stat_landed = [stat_landed0, stat_landed1]
        mx_landed = [mx_landed0, mx_landed1, mx_landed2, mx_landed3]
        fin_stored = [fin_stored0, fin_stored1]

        def dst_of(group_slot, part):
            return (wo_hi if part == 0 else wo_lo)[group_slot]

        def out_pieces(i, with_next):
            if with_next or not TILES - 7 <= i < TILES - 1:
                return []
            return [(2 * UNITS + 1 + z // PIECES, z % PIECES) for z in range(2 * (i - TILES + 7), 2 * (i - TILES + 8))]

        INTER = 8

        def qk_bank(i):
            return bank[7] if i in (1, 3) else bank[0]

        def vz_bank(t, beside):
            return {"prologue": (bank[7], bank[0]), "hgrn": (bank[7], bank[4]),
                    "attention": (bank[0] if t < INTER else bank[1], bank[0])}[beside][t % 2]

        ctx.enter_context(nc.allow_non_contiguous_dma(reason="strips of 512 bytes and more"))
        block = ctx.enter_context(nc.Block())

        @block.sync
        def _(sp):
            def after(semaphore, value):
                sp.wait_ge(semaphore, value)
                if not isinstance(value, int):
                    sp.sem_inc(passed_sp, 1)

            def load_piece(n, i):
                if not (isinstance(n, int) and 4 * n + i < 2):
                    after(lo_done, n * 4 + (i - 1))
                sp.dma_start(stage[i % 2][:, :, :],
                             w_groups[bass.ds(n, 1), :, 2 * i:2 * i + 2, :].rearrange("a p k c -> (a p) k c"))\
                    .then_inc(w_landed[i % 2], 16)

            def phase1_store(U, t):
                after(gated, U * 16 + (t + 1))
                sp.dma_start(vg_dram[bass.ds(U, 1), t * P:(t + 1) * P, :].rearrange("a t c -> (a t) c"),
                             vg_tile[t % 2][:, :]).then_inc(vg_stored[t % 2], 16)

            for counted in (q_read, f_read, kt_read, st_ready, out_done0, out_done1, lev_ready, kt_mm,
                            u_mm, osq_done, rs_done, fk_ready, o_mm, out_stored0, out_stored1, s_ready,
                            pv_mm, pt_mm, yT_mm, stat_stored, comb_done, comb_stored):
                sp.sem_inc(counted, ONE)

            sp.dma_start(nw[:, :], norm_w).then_inc(const_ready, 16)
            def load_x(t):
                sp.dma_start(xt[t % X_SLOTS], x[t * P:(t + 1) * P, :]).then_inc(x_landed[t % X_SLOTS], 16)

            load_x(0)
            load_piece(0, 0)
            load_x(1)
            load_piece(0, 1)
            sp.dma_start(lb_in, lb_logits).then_inc(lb_landed, 16)
            sp.dma_start(g_all, gate_g).then_inc(g_landed, 16)
            load_x(2)
            load_piece(0, 2)
            load_x(3)
            load_piece(0, 3)
            sp.dma_start(tri, tri_masks).then_inc(tri_landed, 16)
            sp.dma_start(rope_sb, rope).then_inc(rope_landed, 16)
            for step in range(TILES + 5):
                if step >= 5:
                    phase1_store(0, step - 5)
                if step - 3 in SPLIT_AT["prologue"]:
                    load_piece(1, SPLIT_AT["prologue"].index(step - 3))
                if step + X_SLOTS < TILES:
                    after(xn_done, step + 1)
                    load_x(step + X_SLOTS)

            with sp.Fori(0, HG_UNITS) as u:
                def load_vg(b):
                    if b == 0:
                        after(vg_stored[0], u * 128 + 128)
                        after(vg_stored[1], u * 128 + 128)
                    after(out_stored[b % 2], u * 32 + (16 * (b // 2) + ONE))
                    src = vg_dram[bass.ds(u, 1), b * BT:(b + 1) * BT, :]
                    sp.dma_start(vg_blk[b % 2], src.rearrange("a (c t) n -> (a t) c n", c=CH))\
                        .then_inc(vg_loaded[b % 2], 16)

                for kind, i in HG_STEPS:
                    if kind == "P":
                        if i == 0:
                            load_piece(2 * u + 2, 0)
                            load_piece(2 * u + 2, 1)
                            load_vg(0)
                            load_piece(2 * u + 2, 2)
                            load_piece(2 * u + 2, 3)
                            load_vg(1)
                    elif kind == "Z":
                        after((out_done0, out_done1)[i % 2], u * 2 + (i // 2 + 1 + ONE))
                        dst = mixed_dram[i * BT:(i + 1) * BT, bass.ds(u * P, P)]
                        sp.dma_start(dst.rearrange("(c t) n -> t c n", c=CH), vg_blk[i % 2][:, :, P:GC])\
                            .then_inc(out_stored[i % 2], 16)
                        if i < 2:
                            load_vg(i + 2)
                    elif kind == "T":
                        if i in SPLIT_AT["hgrn"]:
                            load_piece(2 * u + 3, SPLIT_AT["hgrn"].index(i))
                        phase1_store(u + 1, i)

            after(out_stored[0], HG_UNITS * 32 + ONE)
            after(out_stored[1], HG_UNITS * 32 + ONE)
            sp.dma_start(near_m, near_mask).then_inc(tab_landed, 16)
            sp.dma_start(far_m, far_mask).then_inc(tab_landed, 16)

            def load_mixed(t):
                sp.dma_start(mx[t % MX_SLOTS], mixed_dram[t * P:(t + 1) * P, :]).then_inc(mx_landed[t % MX_SLOTS], 16)

            def load_residual(t):
                sp.dma_start(xr[t % MX_SLOTS], x[t * P:(t + 1) * P, :]).then_inc(xr_landed[t % MX_SLOTS], 16)

            def attention(v, with_next):
                U = v + HG_UNITS
                T0 = v * TILES

                def load_near(g):
                    if g >= 2:
                        after(pv_mm, T0 + (4 * (g - 1) + 1 + ONE))
                    src = vg_dram[bass.ds(U, 1), g * BT:(g + 1) * BT, 0:P]
                    sp.dma_start(near_v[:, (4 * g) % 8:(4 * g) % 8 + 4, :],
                                 src.rearrange("a (c t) n -> (a t) c n", c=CH)).then_inc(nv_landed[g % 2], 16)

                def load_gate(g):
                    after(comb_stored, v * 64 + (16 * g + ONE))
                    src = vg_dram[bass.ds(U, 1), g * BT:(g + 1) * BT, P:GC]
                    sp.dma_start(gate, src.rearrange("a (c t) n -> (a t) c n", c=CH)).then_inc(gate_landed, 16)

                after(vg_stored[0], U * 128 + 128)
                after(vg_stored[1], U * 128 + 128)
                after(pv_mm, T0 + ONE)
                load_near(0)
                for g in range(BLOCKS):
                    src = vg_dram[bass.ds(U, 1), g * BT:(g + 1) * BT, 0:P]
                    sp.dma_start(far_v[:, 4 * g:4 * g + 4, :],
                                 src.rearrange("a (i q) n -> (a i) q n", q=4)).then_inc(fv_landed, 16)
                load_near(1)
                load_gate(0)
                for kind, i, part in attention_steps(with_next):
                    if kind == "R":
                        if i in (0, 3, 6, 9):
                            load_piece(2 * U + 2, i // 3)
                        if i % 4 == 2 and 4 <= i < 12:
                            load_near(i // 4 + 1)
                        if i == TILES - 1 and not with_next:
                            after(roped_done, T0 + TILES)
                            after(s_ready, T0 * 4 + 64 + ONE)
                            after(comb_stored, v * 64 + 16 + ONE)
                            load_mixed(0)
                        if i % 4 == 3:
                            g = i // 4
                            after(e_done, T0 * 4 + 16 * (g + 1))
                            sd = stat_dram[bass.ds(v, 1), g, :]
                            sp.dma_start(sd.rearrange("a (i w) -> (a i) w", i=P),
                                         st_far[g % 2].rearrange("p a b -> p (a b)")).then_inc(stat_stored, 16)
                            after(stat_stored, v * 64 + 16 * (g + 1) + ONE)
                            sp.dma_start(st_farn[g % 2], sd.rearrange("a (c t w) -> (a t) c w", c=CH, w=4))\
                                .then_inc(stat_landed[g % 2], 16)
                        if i == TILES - 1 and not with_next:
                            for t in range(1, MX_SLOTS):
                                load_mixed(t)
                    elif kind == "C":
                        after(comb_done, v * 4 + (i + 1 + ONE))
                        dst = mixed_dram[i * BT:(i + 1) * BT, bass.ds(U * P, P)]
                        sp.dma_start(dst.rearrange("(c t) n -> t c n", c=CH), gate).then_inc(comb_stored, 16)
                        if i + 1 < BLOCKS:
                            load_gate(i + 1)
                        elif not with_next:
                            for t in range(MX_SLOTS):
                                load_residual(t)
                            after(comb_stored, T0 * 4 + 64 + ONE)
                            sp.dma_start(fw, final_w).then_inc(tab_landed, 16)
                    elif kind == "F":
                        for n, q in out_pieces(i, with_next):
                            load_piece(n, q)
                    elif kind == "T" and part == PARTS - 1:
                        if i in (1, 4, 7, 10):
                            load_piece(2 * U + 3, (i - 1) // 3)
                        phase1_store(U + 1, i)

            with sp.Fori(0, AT_UNITS - 1) as v:
                attention(v, True)
            attention(AT_UNITS - 1, False)

            for t in range(MX_SLOTS, TILES):
                if t % CH == 0:
                    after(comb_stored, (AT_UNITS - 1) * 64 + 16 * (t // CH + 1) + ONE)
                after(mT_mm, t + 1 - MX_SLOTS)
                after(hsum_done, t + 1 - MX_SLOTS)
                load_mixed(t)
                load_residual(t)
                if t >= MX_SLOTS:
                    z = t - MX_SLOTS
                    after(fin_done, z + 1)
                    sp.dma_start(out[z * P:(z + 1) * P, :], hh[z % 2]).then_inc(fin_stored[z % 2], 16)
            for t in range(TILES - MX_SLOTS, TILES):
                after(fin_done, t + 1)
                sp.dma_start(out[t * P:(t + 1) * P, :], hh[t % 2]).then_inc(fin_stored[t % 2], 16)
            after(fin_stored[0], TILES // 2 * 16)
            after(fin_stored[1], TILES // 2 * 16)

        @block.tensor
        def _(pe):
            def split_matmuls(dst, lhs_hi, lhs_lo, rhs_hi, rhs_lo, tiles=range(KT_N)):
                for k in tiles:
                    nc.tensor.matmul(dst, lhs_hi(k), rhs_hi(k), start=(k == 0), stop=False)
                    nc.tensor.matmul(dst, lhs_hi(k), rhs_lo(k), start=False, stop=False)
                    last = nc.tensor.matmul(dst, lhs_lo(k), rhs_hi(k), start=False, stop=(k == KT_N - 1))
                return last

            part_tiles = [range(0, 3), range(3, 6), range(6, KT_N)]

            def phase1_part(U, t, part):
                if part == 0:
                    if t == 0:
                        pe.wait_ge(lo_done, U * 8 + 4)
                        pe.wait_ge(roped_done, U * 16 - 16 * HG_UNITS)
                    elif t < INTER:
                        pe.wait_ge(sig_done, U * 16 + t)
                    elif t == INTER:
                        pe.wait_ge(s_taken, U * 64 - (64 * HG_UNITS - 4))
                    else:
                        pe.wait_ge(sig_done, U * 16 + (t - 1))
                sl = slice(t * P, (t + 1) * P)
                last = split_matmuls(vz_bank(t, "attention")[:, 0:GC],
                                     lambda k: u_hi[:, k, sl], lambda k: u_lo[:, k, sl],
                                     lambda k: w_hi[0][:, k, :], lambda k: w_lo[0][:, k, :], part_tiles[part])
                if part == PARTS - 1:
                    last.then_inc(vz_ready, 1)

            def phase1_tile(U, t, beside):
                if t == 0:
                    pe.wait_ge(lo_done, U * 8 + 4)
                if t >= 2:
                    pe.wait_ge(sig_done, U * 16 + (t - 1))
                if beside == "hgrn" and t % 2:
                    pe.wait_ge(kt_read, U * 4 + (blocks_before("M", t) - BLOCKS + ONE))
                sl = slice(t * P, (t + 1) * P)
                last = split_matmuls(vz_bank(t, beside)[:, 0:GC],
                                     lambda k: u_hi[:, k, sl], lambda k: u_lo[:, k, sl],
                                     lambda k: w_hi[0][:, k, :], lambda k: w_lo[0][:, k, :])
                last.then_inc(vz_ready, 1)

            pe.wait_ge(const_ready, 16 + 1)
            pe.sem_inc(lev_mm, LEVELS)

            def x_transposes(t):
                pe.wait_ge(xn_done, t + 1)
                if t >= 2:
                    pe.wait_ge(un_done, t - 1)
                for k in range(KT_N):
                    last = nc.tensor.transpose(bank[1 + 2 * (t % 2) + k // 4][:, (k % 4) * P:(k % 4 + 1) * P],
                                               xn[t % 2][:, k * P:(k + 1) * P], ident[:, :])
                last.then_inc(xT_done, 1)

            x_transposes(0)
            x_transposes(1)
            for t in range(TILES):
                if t + 2 < TILES:
                    x_transposes(t + 2)
                pe.wait_ge(ulo_done, t + 1)
                phase1_tile(0, t, "prologue")

            level_ops = [(base_k, base_q), (lev8, lev8), (lev16, lev16), (lev32, lev32), (lev64, lev64)]
            with pe.Fori(0, HG_UNITS) as u:
                for kind, b in HG_STEPS:
                    if kind == "P":
                        if b == 0:
                            pe.wait_ge(lo_done, u * 8 + 8)
                            pe.wait_ge(sig_done, u * 16 + 16)
                        sl = slice(b * BT, (b + 1) * BT)
                        pe.wait_ge(q_read, u * 4 + (b + ONE))
                        split_matmuls(bank[0][:, :], lambda k: w_hi[1][:, k, 0:P], lambda k: w_lo[1][:, k, 0:P],
                                      lambda k: u_hi[:, k, sl], lambda k: u_lo[:, k, sl]).then_inc(q_ready, 1)
                        pe.wait_ge(f_read, u * 4 + (b + ONE))
                        last = split_matmuls(bank[1][:, :], lambda k: w_hi[1][:, k, P:GC], lambda k: w_lo[1][:, k, P:GC],
                                             lambda k: u_hi[:, k, sl], lambda k: u_lo[:, k, sl])
                        last.then_inc(f_ready, 1)
                    elif kind == "M":
                        pe.wait_ge(lev_ready, u * 4 + (b + 1 + ONE))
                        pe.wait_ge(kt_read, u * 4 + (b + ONE))
                        pe.wait_ge(sig_done, u * 16 + (16 + odd_before("M", b)))
                        for c in range(CH):
                            last = nc.tensor.transpose(bank[4][:, c * P:(c + 1) * P], kb[:, c * P:(c + 1) * P], ident[:, :])
                        last.then_inc(kt_mm, 1)
                        for l, (ka, qa) in enumerate(level_ops):
                            pe.wait_ge(lev_read, u * (4 * LEVELS) + (b * LEVELS + l + 1))
                            for c in range(CH):
                                if 0 < l < LEVELS - 1:
                                    later = qa[:, c * P:(c + 1) * P].rearrange("p (n s h) -> p n s h", s=2, h=4 << l)[:, :, 1, :]
                                    last = nc.tensor.matmul(bank[2 + l % 2][:, c * P // 2:(c + 1) * P // 2],
                                                            ka[:, c * P:(c + 1) * P], later, start=True, stop=True)
                                elif l == 0:
                                    last = nc.tensor.matmul(bank[2 + l % 2][:, c * P:(c + 1) * P], ka[:, c * P:(c + 1) * P],
                                                            qa[:, c * P:(c + 1) * P], start=True, stop=True)
                                else:
                                    last = nc.tensor.matmul(bank[2 + l % 2][0:64, c * P + 64:(c + 1) * P],
                                                            ka[:, c * P:c * P + 64], qa[:, c * P + 64:(c + 1) * P],
                                                            start=True, stop=True)
                            last.then_inc(lev_mm, 1)
                        pe.wait_ge(kt_read, u * 4 + (b + 1 + ONE))
                        pe.wait_ge(vg_loaded[b % 2], u * 32 + 16 * (b // 2 + 1))
                        pe.wait_ge(st_ready, u * 4 + (b + ONE))
                        for c in range(CH):
                            last = nc.tensor.matmul(bank[5][:, c * P:(c + 1) * P], k_tok[:, c, :], vg_blk[b % 2][:, c, 0:P],
                                                    start=True, stop=True)
                        last.then_inc(u_mm, 1)
                    elif kind == "O":
                        pe.wait_ge(st_ready, u * 4 + (b + 1 + ONE))
                        pe.wait_ge(out_done0, u * 2 + (b + 1) // 2 + ONE)
                        pe.wait_ge(out_done1, u * 2 + (b // 2 + ONE))
                        for c in range(CH):
                            nc.tensor.matmul(bank[6][:, c * P:(c + 1) * P], st[:, c, :], vg_blk[b % 2][:, c, 0:P],
                                             start=True, stop=False)
                            last = nc.tensor.matmul(bank[6][:, c * P:(c + 1) * P], q_in[:, c * P:(c + 1) * P],
                                                    states[b % 2][:, c, :], start=False, stop=True)
                        last.then_inc(o_mm, 1)
                    elif kind == "T":
                        phase1_tile(u + 1, b, "hgrn")

            def attention(v, with_next):
                U = v + HG_UNITS
                T0 = v * TILES
                for kind, i, part in attention_steps(with_next):
                    g, j = i // CH, i % CH
                    if kind == "X":
                        if i == 0 and part == 0:
                            pe.wait_ge(lo_done, U * 8 + 8)
                            pe.wait_ge(sig_done, U * 16 + 16)
                        elif part == 0 and i != 1:
                            pe.wait_ge(roped_done, T0 + (i if i >= 5 else i - 1))
                        sl = slice(i * P, (i + 1) * P)
                        last = split_matmuls(qk_bank(i)[:, 0:GC], lambda k: u_hi[:, k, sl], lambda k: u_lo[:, k, sl],
                                             lambda k: w_hi[1][:, k, :], lambda k: w_lo[1][:, k, :], part_tiles[part])
                        if part == PARTS - 1:
                            last.then_inc(qk_ready, 1)
                    elif kind == "Y":
                        pe.wait_ge(roped_done, T0 + (i + 1))
                        if i >= 1:
                            pe.wait_ge(yT_read, T0 + i)
                        if i >= 4:
                            pe.wait_ge(s_taken, T0 * 4 + (4 * (i - 4) + 6))
                        for h in range(2):
                            last = nc.tensor.transpose(bank[1][:, h * P:(h + 1) * P],
                                                       roped[i % 2][:, 2 * h:2 * h + 2, :].rearrange("p a b -> p (a b)"),
                                                       ident[:, :])
                        last.then_inc(yT_mm, 1)
                    elif kind == "G":
                        pe.wait_ge(yT_read, T0 + min(max(4 * g + 4, i + 4), TILES))
                        q = qT[g % 2]
                        lo = P if i == 0 else 0
                        for h in range(2):
                            hs = slice(HD * h, HD * h + HD)
                            pe.wait_ge(s_taken, T0 * 4 + (4 * i + 1 + h))
                            last = nc.tensor.matmul(bank[2 - h][:, lo:2 * P], q[hs, j * P:(j + 1) * P],
                                                    kT[hs, (i - 1) * P + lo:(i + 1) * P], start=True, stop=True)
                            last.then_inc(s_ready, 1)
                        for h in range(2):
                            hs = slice(HD * h, HD * h + HD)
                            pe.wait_ge(s_taken, T0 * 4 + (4 * i + 3 + h))
                            last = nc.tensor.matmul(bank[3 + h][:, 0:P * (g + 1)], q[hs, j::4], kT[hs, j:BT * (g + 1):4],
                                                    start=True, stop=True)
                            last.then_inc(s_ready, 1)
                    elif kind in ("F", "H"):
                        fill = v * (FILLS * 4) + (FILLS * g + 3 * j)
                        fb_ = FILLS * g + 3 * j
                        lo = 1 if i == 0 else 0
                        for f in ((0, 1) if kind == "F" else (2,)):
                            pe.wait_ge(e_done, T0 * 4 + (4 * i + (2, 3, 4)[f]))
                            pe.wait_ge(pt_read, fill + (f + 1))
                            bk = bank[5 + (fb_ + f) % 2]
                            if f == 0:
                                src = [(2 * h + kk, p_near[:, h, kk * P:(kk + 1) * P]) for h in range(2) for kk in range(lo, 2)]
                            else:
                                src = [(kk, p_far[:, f - 1, kk * P:(kk + 1) * P]) for kk in range(g + 1)]
                            for slot, ap in src:
                                last = nc.tensor.transpose(bk[:, slot * P:(slot + 1) * P], ap, ident[:, :])
                            last.then_inc(pt_mm, 1)
                    elif kind == "W":
                        fill = v * (FILLS * 4) + (FILLS * g + 3 * j)
                        lo = 1 if i == 0 else 0
                        if i >= 1:
                            pe.wait_ge(oT_read, T0 + i)
                        if j == 0:
                            pe.wait_ge(nv_landed[g % 2], v * 32 + 16 * (g // 2 + 1))
                            pe.wait_ge(fv_landed, v * 64 + 64)
                        pe.wait_ge(pt_read, fill + (1 + 2))
                        for h in range(2):
                            hs = slice(HD * h, HD * h + HD)
                            for kk in range(lo, 2):
                                nc.tensor.matmul(bank[7][hs, 0:P], near_v[:, (i - 1 + kk) % 8, hs], pT[0][:, 2 * h + kk, :],
                                                 start=(kk == lo), stop=(kk == 1))
                        for h in range(2):
                            hs = slice(HD * h, HD * h + HD)
                            pe.wait_ge(pt_read, fill + (2 + h + 2))
                            for kk in range(g + 1):
                                last = nc.tensor.matmul(bank[7][hs, P:2 * P], far_v[:, 4 * kk + j, hs], pT[1 + h][:, kk, :],
                                                        start=(kk == 0), stop=(kk == g))
                        last.then_inc(pv_mm, 1)
                    elif kind == "C":
                        g = i
                        pe.wait_ge(oT_read, T0 + 4 * (g + 1))
                        for f, src in enumerate((oT_near, oT_far)):
                            fill = v * (FILLS * 4) + (FILLS * g + 12 + f)
                            pe.wait_ge(pt_read, fill + 1)
                            for c in range(CH):
                                last = nc.tensor.transpose(bank[5 + f][:, c * P:(c + 1) * P], src[:, c * P:(c + 1) * P], ident[:, :])
                            last.then_inc(pt_mm, 1)
                    elif kind == "T":
                        phase1_part(U + 1, i, part)

            with pe.Fori(0, AT_UNITS - 1) as v:
                attention(v, True)
            attention(AT_UNITS - 1, False)

            pe.wait_ge(pt_read, FILLS * 4 * AT_UNITS + 2)
            pe.wait_ge(lo_done, 4 * (2 * UNITS + OUT_GROUPS))

            def mixed_transposes(t):
                pe.wait_ge(mx_landed[t % MX_SLOTS], 16 * (t // MX_SLOTS + 1))
                if t >= 2:
                    pe.wait_ge(mlo_done, t - 1)
                for k in range(KT_N):
                    last = nc.tensor.transpose(bank[1 + 2 * (t % 2) + k // 4][:, (k % 4) * P:(k % 4 + 1) * P],
                                               mx[t % MX_SLOTS][:, k * P:(k + 1) * P], ident[:, :])
                last.then_inc(mT_mm, 1)

            mixed_transposes(0)
            for t in range(TILES):
                if t + 1 < TILES:
                    mixed_transposes(t + 1)
                pe.wait_ge(mlo_done, t + 1)
                if t >= 2:
                    pe.wait_ge(hsum_done, t - 1)
                for n in range(OUT_GROUPS):
                    yb = (bank[5 + n // 2], (bank[7], bank[0])[n // 2])[t % 2]
                    last = split_matmuls(yb[:, (n % 2) * GC:(n % 2 + 1) * GC],
                                         lambda k: mT_hi[t % 2][:, k, :], lambda k: mT_lo[t % 2][:, k, :],
                                         lambda k: wo_hi[n][:, k, :], lambda k: wo_lo[n][:, k, :])
                last.then_inc(y_ready, 1)

        @block.scalar
        def _(act):
            def split_hi(n, i, slot):
                act.wait_ge(w_landed[i % 2], n * 32 + 16 * (i // 2 + 1))
                nc.scalar.copy(dst_of(slot, 0)[:, 2 * i:2 * i + 2, :], stage[i % 2][:, :, :]).then_inc(hi_done, 1)

            def phase1_tile(U, t, beside):
                vz = vz_bank(t, beside)
                act.wait_ge(vz_ready, U * 16 + (t + 1))
                if not (isinstance(U, int) and U == 0 and t < 2):
                    act.wait_ge(vg_stored[t % 2], U * 128 + 16 * (t // 2))
                nc.scalar.copy(vg_tile[t % 2][:, :], vz[:, 0:GC])
                if beside == "attention":
                    nc.scalar.activation(sg_tile[t % 2][:, :], vz[:, P:GC], ACT.Exp, scale=-1.0).then_inc(sig_done, 1)
                else:
                    nc.scalar.activation(sg_tile[t % 2][:, :], vz[:, P:GC], ACT.Sigmoid).then_inc(sig_done, 1)
                if t in SPLIT_AT[beside]:
                    if beside == "attention":
                        act.wait_ge(qk_ready, U * 16 - 16 * HG_UNITS)
                    elif beside == "hgrn":
                        act.wait_ge(f_ready, U * 4)
                    split_hi(2 * U + 1, SPLIT_AT[beside].index(t), 1)

            for step in range(TILES + 4):
                if step < TILES:
                    act.wait_ge(x_landed[step % X_SLOTS], 16 * (step // X_SLOTS + 1))
                    if step >= 1:
                        act.wait_ge(xsq_done, step)
                    nc.scalar.activation(xsq, xt[step % X_SLOTS], ACT.Square,
                                         accum_out=ss[:, step:step + 1]).then_inc(xsq_done, 1)
                t = step - 2
                if 0 <= t < TILES:
                    act.wait_ge(un_done, t + 1)
                    nc.scalar.copy(u_hi[:, :, t * P:(t + 1) * P], un[t % 2]).then_inc(uhi_done, 1)
                if step < 3:
                    for i in ((0,), (1, 2), (3,))[step]:
                        split_hi(0, i, 0)
                if step == 3:
                    act.wait_ge(lb_step, 2)
                    nc.scalar.activation(lb_in, lb_in, ACT.Exp).then_inc(lb_step, 1)
                if step >= 4:
                    phase1_tile(0, step - 4, "prologue")

            with act.Fori(0, HG_UNITS) as u:
                for kind, b in HG_STEPS:
                    if kind == "P":
                        if b == 0:
                            act.wait_ge(vz_ready, u * 16 + 16)
                            for i in (0, 1):
                                split_hi(2 * u + 2, i, 0)
                        act.wait_ge(q_ready, u * 4 + (b + 1))
                        act.wait_ge(q_read, u * 4 + (b + ONE))
                        nc.scalar.activation(sgq, bank[0][:, :], ACT.Sigmoid).then_inc(sq_done, 1)
                        if b == 0:
                            for i in (2, 3):
                                split_hi(2 * u + 2, i, 0)
                    elif kind == "K":
                        act.wait_ge(f_ready, u * 4 + (b + 1))
                        act.wait_ge(lev_ready, u * 4 + (b + ONE))
                        act.wait_ge(kt_mm, u * 4 + (b + ONE))
                        nc.scalar.activation(fb, bank[1][:, :], ACT.Sigmoid)
                        nc.scalar.activation(kb, bank[1][:, :], ACT.Sigmoid, scale=-1.0).then_inc(f_read, 1)
                    elif kind == "M":
                        act.wait_ge(kt_mm, u * 4 + (b + 1 + ONE))
                        act.wait_ge(u_mm, u * 4 + (b + ONE))
                        nc.scalar.copy(k_tok.rearrange("p c k -> p (c k)"), bank[4][:, :]).then_inc(kt_read, 1)
                    elif kind == "O":
                        act.wait_ge(o_mm, u * 4 + (b + 1 + ONE))
                        act.wait_ge(osq_done, u * 4 + (b + ONE))
                        act.wait_ge(rs_done, u * 4 + (b + ONE))
                        for c in range(CH):
                            last = nc.scalar.activation(osq[:, c * P:(c + 1) * P], bank[6][:, c * P:(c + 1) * P],
                                                        ACT.Square, accum_out=ms_o[:, c:c + 1])
                        last.then_inc(osq_done, 1)
                    elif kind == "T":
                        phase1_tile(u + 1, b, "hgrn")

            def attention(v, with_next):
                U = v + HG_UNITS
                T0 = v * TILES
                for kind, i, part in attention_steps(with_next):
                    g, j = i // CH, i % CH
                    if kind == "Y":
                        act.wait_ge(yT_mm, T0 + (i + 1 + ONE))
                        if i == 0:
                            act.wait_ge(s_ready, T0 * 4 + ONE)
                        elif j == 0 and g >= 2:
                            act.wait_ge(s_ready, T0 * 4 + (16 * (g - 1) + ONE))
                        nc.scalar.activation(qT[g % 2][:, j * P:(j + 1) * P], bank[1][:, 0:P], ACT.Copy, scale=-(HD ** -0.5))
                        nc.scalar.copy(kT[:, i * P:(i + 1) * P], bank[1][:, P:2 * P]).then_inc(yT_read, 1)
                    elif kind in ("N", "R"):
                        lo = P if i == 0 else 0
                        for n in ((0, 1) if kind == "N" else (2, 3)):
                            h = n % 2
                            act.wait_ge(s_taken, T0 * 4 + (4 * i + n + 1 + 4))
                            buf = p_near[:, h, lo:] if n < 2 else p_far[:, h, 0:P * (g + 1)]
                            stt = (st_near if n < 2 else st_far)[g % 2]
                            nc.scalar.activation(buf, buf, ACT.Exp, scale=-1.0, bias=stt[:, j, h:h + 1],
                                                 accum_out=stt[:, j, 2 + h:3 + h]).then_inc(e_done, 1)
                        if kind == "R" and i in (0, 3, 6, 9):
                            act.wait_ge(vz_ready, U * 16 + 16)
                            split_hi(2 * U + 2, i // 3, 0)
                    elif kind in ("F", "H"):
                        fill = v * (FILLS * 4) + (FILLS * g + 3 * j)
                        for f in ((0,) if kind == "F" else (2,)):
                            act.wait_ge(pt_mm, fill + (f + 1 + ONE))
                            if f == 0:
                                act.wait_ge(pv_mm, T0 + i + ONE)
                            act.wait_ge(pt_read, fill + (f + 2))
                            fb_ = FILLS * g + 3 * j + f
                            if f == 0 and i == 0:
                                nc.scalar.copy(pT[0][:, 1, :], bank[5 + fb_ % 2][:, P:2 * P])
                                nc.scalar.copy(pT[0][:, 3, :], bank[5 + fb_ % 2][:, 3 * P:4 * P]).then_inc(pt_read, 1)
                            else:
                                n = 4 if f == 0 else g + 1
                                nc.scalar.copy(pT[f][:, 0:n, :].rearrange("p a b -> p (a b)"),
                                               bank[5 + fb_ % 2][:, 0:n * P]).then_inc(pt_read, 1)
                    elif kind == "W":
                        act.wait_ge(pv_mm, T0 + (i + 1 + ONE))
                        if j == 0:
                            act.wait_ge(pt_mm, v * (FILLS * 4) + FILLS * g + ONE)
                        nc.scalar.copy(oT_near[:, j * P:(j + 1) * P], bank[7][:, 0:P])
                        nc.scalar.copy(oT_far[:, j::4], bank[7][:, P:2 * P]).then_inc(oT_read, 1)
                        for n, q in out_pieces(i, with_next):
                            act.wait_ge(qk_ready, T0 + TILES)
                            split_hi(n, q, n - 2 * UNITS)
                    elif kind == "D":
                        g = i
                        act.wait_ge(dve_comb, v * 4 + (g + 1))
                        nc.scalar.activation(ea, ea, ACT.Exp)
                        nc.scalar.activation(eb, eb, ACT.Exp).then_inc(exp_comb, 1)
                    elif kind == "T" and part == PARTS - 1:
                        phase1_tile(U + 1, i, "attention")

            with act.Fori(0, AT_UNITS - 1) as v:
                attention(v, True)
            attention(AT_UNITS - 1, False)

            for t in range(TILES + 2):
                if t < TILES:
                    act.wait_ge(mT_mm, t + 1)
                    if t >= 2:
                        act.wait_ge(y_ready, t - 1)
                    for q in range(2):
                        last = nc.scalar.copy(mT_hi[t % 2][:, 4 * q:4 * q + 4, :].rearrange("p a b -> p (a b)"),
                                              bank[1 + 2 * (t % 2) + q][:, :])
                    last.then_inc(mhi_done, 1)
                if t >= 2:
                    act.wait_ge(hsum_done, t - 1)
                    if t >= 3:
                        act.wait_ge(hsq_done, t - 2)
                    nc.scalar.activation(hsq, hh[t % 2], ACT.Square, accum_out=ms_f[:, t - 2:t - 1]).then_inc(hsq_done, 1)

        @block.gpsimd
        def _(pool):
            def split_lo(n, i, slot):
                pool.wait_ge(hi_done, n * 4 + (i + 1))
                nc.gpsimd.tensor_tensor(dst_of(slot, 1)[:, 2 * i:2 * i + 2, :], stage[i % 2][:, :, :],
                                        dst_of(slot, 0)[:, 2 * i:2 * i + 2, :].bitcast(F32), ALU.subtract)\
                    .then_inc(lo_done, 1)

            def phase1_tile(U, t, beside):
                z = vg_tile[t % 2][:, P:GC]
                if beside == "attention":
                    pool.wait_ge(gate_done, U * 16 + (t + 1))
                    nc.gpsimd.tensor_tensor(z, z, sg_tile[t % 2][:, :], ALU.mult).then_inc(gated, 1)
                else:
                    pool.wait_ge(sig_done, U * 16 + (t + 1))
                    nc.gpsimd.tensor_tensor(z, z, sg_tile[t % 2][:, :], ALU.mult).then_inc(gate_done, 1)
                    pool.wait_ge(gate_done, U * 16 + (t + 1))
                    nc.gpsimd.tensor_tensor(z, z, g_cur, ALU.mult).then_inc(gated, 1)
                if t in SPLIT_AT[beside]:
                    split_lo(2 * U + 1, SPLIT_AT[beside].index(t), 1)

            nc.gpsimd.memset(ident[:, :], 0.0).then_inc(pool_step, 1)
            nc.gpsimd.memset(half_neg, -0.5).then_inc(pool_step, 1)
            pool.wait_ge(pool_step, 2)
            nc.gpsimd.affine_select(out=ident[:, :], in_=ident[:, :], compare_op=ALU.not_equal, fill=1.0,
                                    base=0, pattern=[[-1, P]], channel_multiplier=1).then_inc(const_ready, 1)
            own = 2
            for step in range(TILES + 4):
                if step < TILES:
                    pool.wait_ge(xsq_done, step + 1)
                    nc.gpsimd.tensor_scalar(ss[:, step:step + 1], ss[:, step:step + 1], 1.0 / D, EPS,
                                            ALU.mult, ALU.add).then_inc(pool_step, 1)
                    own += 1
                    pool.wait_ge(pool_step, own)
                    nc.gpsimd.tensor_tensor(rstd[:, step:step + 1], ss[:, step:step + 1], half_neg[:, 0:1],
                                            ALU.pow).then_inc(rstd_done, 1)
                if step < 3:
                    for i in ((0,), (1, 2), (3,))[step]:
                        split_lo(0, i, 0)
                if step == 3:
                    pool.wait_ge(g_landed, 16)
                    nc.gpsimd.tensor_copy(g_cur, g_all[:, 0, :]).then_inc(pool_step, 1)
                    own += 1
                if step >= 4:
                    phase1_tile(0, step - 4, "prologue")

            pool.wait_ge(lb_ready, 1)
            with pool.Fori(0, HG_UNITS) as u:
                for kind, b in HG_STEPS:
                    if kind == "P":
                        if b == 0:
                            pool.wait_ge(fk_ready, u * 4 + ONE)
                            pool.wait_ge(gated, u * 16 + 16)
                            nc.gpsimd.tensor_copy(lb, lb_all[:, bass.ds(u, 1)])
                            nc.gpsimd.tensor_copy(omlb, omlb_all[:, bass.ds(u, 1)])
                            nc.gpsimd.tensor_copy(g_cur, g_all[:, bass.ds(u + 1, 1), :].rearrange("p a b -> p (a b)"))\
                                .then_inc(cur_ready, 1)
                            pool.wait_ge(cur_ready, u + 1)
                            for i in range(PIECES):
                                split_lo(2 * u + 2, i, 0)
                    elif kind == "K":
                        pool.wait_ge(f_read, u * 4 + (b + 1 + ONE))
                        pool.sem_inc(passed_pool, 1)
                        nc.gpsimd.tensor_scalar(fb, fb, omlb[:, 0:1], lb[:, 0:1], ALU.mult, ALU.add)
                        nc.gpsimd.tensor_scalar(kb, kb, omlb[:, 0:1], None, ALU.mult).then_inc(fk_ready, 1)
                    elif kind == "O":
                        pool.wait_ge(osq_done, u * 4 + (b + 1 + ONE))
                        if b % 2 == 0:
                            pool.wait_ge(out_done1, u * 2 + (b // 2 + ONE))
                        else:
                            pool.wait_ge(out_done0, u * 2 + (b + 1) // 2 + ONE)
                        pool.sem_inc(passed_pool, 1)
                        nc.gpsimd.tensor_scalar(rs_o, ms_o, 1.0 / P, EPS, ALU.mult, ALU.add).then_inc(rs_half, 1)
                        pool.wait_ge(rs_half, u * 4 + (b + 1))
                        nc.gpsimd.tensor_tensor(rs_o, rs_o, half_neg[:, 0:CH], ALU.pow).then_inc(rs_done, 1)
                    elif kind == "T":
                        phase1_tile(u + 1, b, "hgrn")

            def attention(v, with_next):
                U = v + HG_UNITS
                for kind, i, part in attention_steps(with_next):
                    if kind == "R" and i in (0, 3, 6, 9):
                        split_lo(2 * U + 2, i // 3, 0)
                    elif kind == "W":
                        for n, q in out_pieces(i, with_next):
                            split_lo(n, q, n - 2 * UNITS)
                    elif kind == "T" and part == PARTS - 1:
                        phase1_tile(U + 1, i, "attention")

            with pool.Fori(0, AT_UNITS - 1) as v:
                attention(v, True)
            attention(AT_UNITS - 1, False)

            pool.wait_ge(comb_stored, AT_UNITS * 64 + ONE)
            nc.gpsimd.memset(o_half, -0.5).then_inc(pool_step, 1)
            own += 1
            for t in range(TILES):
                pool.wait_ge(hsq_done, t + 1)
                nc.gpsimd.tensor_scalar(ms_f[:, t:t + 1], ms_f[:, t:t + 1], 1.0 / D, EPS, ALU.mult, ALU.add).then_inc(pool_step, 1)
                own += 1
                pool.wait_ge(pool_step, own)
                nc.gpsimd.tensor_tensor(rs_f[:, t:t + 1], ms_f[:, t:t + 1], o_half, ALU.pow).then_inc(frs_done, 1)

        @block.vector
        def _(dve):
            count = [0]

            def tick(ins):
                count[0] += 1
                ins.then_inc(dve_step, 1)
                return count[0]

            def settle(upto=None):
                dve.wait_ge(dve_step, upto or count[0])

            def restart():
                settle()
                dve.sem_clear(dve_step)
                count[0] = 0

            def tt(dst, a_, b_, op=ALU.mult):
                return nc.vector.tensor_tensor(dst, a_, b_, op)

            dve.wait_ge(const_ready, 17)
            for step in range(TILES + 2):
                t = step - 1
                if 0 <= t < TILES:
                    dve.wait_ge(xT_done, t + 1)
                    if t >= 2:
                        dve.wait_ge(ulo_done, t - 1)
                    for q in range(2):
                        last = tt(un[t % 2][:, 4 * q:4 * q + 4, :],
                                  bank[1 + 2 * (t % 2) + q][:, :].rearrange("p (k t) -> p k t", k=4),
                                  nw[:, 4 * q:4 * q + 4, None].to_broadcast([P, 4, P]))
                    last.then_inc(un_done, 1)
                if step < TILES:
                    dve.wait_ge(rstd_done, step + 1)
                    if step >= 2:
                        dve.wait_ge(xT_done, step - 1)
                    nc.vector.tensor_scalar(xn[step % 2], xt[step % X_SLOTS], rstd[:, step:step + 1], None,
                                            ALU.mult).then_inc(xn_done, 1)
                t = step - 2
                if t >= 0:
                    dve.wait_ge(uhi_done, t + 1)
                    tt(u_lo[:, :, t * P:(t + 1) * P], un[t % 2], u_hi[:, :, t * P:(t + 1) * P].bitcast(F32),
                       ALU.subtract).then_inc(ulo_done, 1)
                if step == 2:
                    dve.wait_ge(lb_landed, 16)
                    nc.vector.tensor_tensor(lb_tmp, lb_in[:, 0, :], lb_in[:, 1, :], ALU.max).then_inc(lb_step, 1)
                    dve.wait_ge(lb_step, 1)
                    nc.vector.tensor_tensor(lb_in, lb_in, lb_tmp[:, None, :].to_broadcast([P, 2, HG_UNITS]),
                                            ALU.subtract).then_inc(lb_step, 1)
                if step == 5:
                    dve.wait_ge(lb_step, 3)
                    tick(tt(lb_tmp, lb_in[:, 0, :], lb_in[:, 1, :], ALU.add))
                    settle()
                    tick(nc.vector.reciprocal(lb_tmp, lb_tmp))
                    settle()
                    tick(tt(lb_all, lb_in[:, 0, :], lb_tmp))
                    settle()
                    tick(nc.vector.tensor_scalar(lb_all, lb_all, 1e-6, 1.0 - 1e-6, ALU.max, ALU.min))
                    settle()
                    nc.vector.tensor_scalar(omlb_all, lb_all, -1.0, 1.0, ALU.mult, ALU.add).then_inc(lb_ready, 1)
            dve.wait_ge(ulo_done, TILES)
            tick(nc.vector.memset(st, 0.0))
            tick(nc.vector.memset(Rb, 1.0))
            dve.wait_ge(tri_landed, 16)
            dve.sem_inc(lev_read, 2)

            def halves(ap, h):
                v_ = ap.rearrange("p (n s h) -> p n s h", s=2, h=h)
                return v_[:, :, 0, :], v_[:, :, 1, :]

            def bc(t_ap, side, h):
                v_ = t_ap.rearrange("p (n s) -> p n s", s=2)[:, :, side]
                return v_[:, :, None].to_broadcast([P, v_.shape[1], h])

            restart()
            with dve.Fori(0, HG_UNITS) as u:
                for kind, b in HG_STEPS:
                    if kind == "P":
                        dve.wait_ge(sq_done, u * 4 + (b + 1))
                        settle()
                        tt(qb, bank[0][:, :], sgq).then_inc(q_read, 1)
                    elif kind == "L":
                        dve.wait_ge(fk_ready, u * 4 + (b + 1 + ONE))
                        dve.wait_ge(q_read, u * 4 + (b + 1 + ONE))
                        dve.wait_ge(lev_mm, u * 20 + (5 * b + 1))
                        settle()
                        f4 = fb.rearrange("p (n j) -> p n j", j=4)
                        A4 = Ab.rearrange("p (n j) -> p n j", j=4)
                        R4 = Rb.rearrange("p (n j) -> p n j", j=4)
                        A2, f2 = (z.rearrange("p (n j) -> p n j", j=2) for z in (Ab, fb))
                        tick(tt(A2[:, :, 1], f2[:, :, 0], f2[:, :, 1]))
                        tick(nc.vector.tensor_copy(A2[:, :, 0], f2[:, :, 0]))
                        tick(nc.vector.tensor_copy(R4[:, :, 2], f4[:, :, 3]))
                        settle()
                        tick(tt(R4[:, :, 0], A4[:, :, 3], f4[:, :, 1]))
                        tick(nc.vector.tensor_copy(R4[:, :, 1], A4[:, :, 3]))
                        settle()
                        tick(tt(A4[:, :, 2:4], A4[:, :, 2:4], A4[:, :, 1:2].to_broadcast([P, BT // 4, 2])))
                        A0, A1 = halves(Ab, 4)
                        R0, R1 = halves(Rb, 4)
                        V0, V1 = halves(Vb, 4)
                        q0, q1 = halves(qb, 4)
                        k0, k1 = halves(kb, 4)
                        Q0, Q1 = halves(base_q, 4)
                        K0, K1 = halves(base_k, 4)
                        tick(nc.vector.reciprocal(V0, R0))
                        settle()
                        tick(nc.vector.reciprocal(V1, A1))
                        tick(tt(K0, k0, R0))
                        tick(tt(Q1, q1, A1))
                        tick(tt(Q0, q0, V0))
                        settle()
                        tick(tt(K1, k1, V1))
                        T4 = A4[:, :, 3]
                        T4s = T4.rearrange("p (n s) -> p n s", s=2)
                        t4 = [T4s[:, :, z:z + 1].to_broadcast([P, BT // 8, 4]) for z in range(2)]
                        tick(tt(q0, q0, A0))
                        tick(tt(q1, Q1, t4[0]))
                        tick(tt(k0, K0, t4[1]))
                        tick(tt(tot[8], T4s[:, :, 0], T4s[:, :, 1]))
                        settle()
                        tick(tt(k1, k1, R1))
                        for l, (h, lev) in enumerate(((8, lev8), (16, lev16), (32, lev32), (64, lev64))):
                            dve.wait_ge(lev_mm, u * 20 + (5 * b + l + 2))
                            if l == 0:
                                settle()
                                k_scaled = q_scaled = count[0]
                            l0, l1 = halves(lev, h)
                            q0, q1 = halves(qb, h)
                            k0, k1 = halves(kb, h)
                            settle(k_scaled)
                            k_copied = tick(nc.vector.tensor_copy(l0, k0))
                            settle(q_scaled)
                            q_copied = tick(nc.vector.tensor_copy(l1, q1))
                            pair = tot[h].rearrange("p (n s) -> p n s", s=2)
                            tick(tt(tot[2 * h], pair[:, :, 0], pair[:, :, 1]))
                            settle(k_copied)
                            k_scaled = tick(tt(k0, k0, bc(tot[h], 1, h)))
                            settle(q_copied)
                            if h < 64:
                                q_scaled = tick(tt(q1, q1, bc(tot[h], 0, h)))
                            else:
                                dve.wait_ge(o_mm, u * 4 + (b + ONE))
                                i0, i1 = halves(q_in, h)
                                tick(tt(i1, q1, bc(tot[h], 0, h)))
                                tick(nc.vector.tensor_copy(i0, q0))
                        settle()
                        dve.sem_inc(lev_ready, 1)
                    elif kind == "M":
                        dve.wait_ge(o_mm, u * 4 + (b + ONE))
                        if b == 0:
                            tick(nc.vector.memset(states[0][:, 0, :], 0.0))
                        for l in range(LEVELS):
                            dve.wait_ge(lev_mm, u * 20 + (5 * b + l + 1 + LEVELS))
                            dve.wait_ge(lev_read, u * 20 + (5 * b + l + 2))
                            dve.sem_inc(passed_dve, 1)
                            settle()
                            src = bank[2 + l % 2][:, :].rearrange("p (c t) -> p c t", c=CH)
                            half = bank[2 + l % 2][:, 0:BT // 2].rearrange("p (c t) -> p c t", c=CH)
                            if l == 0:
                                last = nc.vector.copy_predicated(st, tri[:, l:l + 1, :].to_broadcast([P, CH, P]), src)
                            elif l < 3:
                                h = 4 << l
                                sel = tri[:, l:l + 1, 0:P // 2].to_broadcast([P, CH, P // 2])
                                into = st.rearrange("p c (n s h) -> p c n s h", s=2, h=h)[:, :, :, 1, :]
                                last = nc.vector.copy_predicated(into, sel.rearrange("p c (n h) -> p c n h", h=h),
                                                                 half.rearrange("p c (n h) -> p c n h", h=h))
                            elif l == 3:
                                tick(nc.vector.tensor_copy(st[0:32, :, 32:64], half[0:32, :, 0:32]))
                                last = nc.vector.tensor_copy(st[64:96, :, 96:128], half[64:96, :, 32:64])
                            else:
                                last = nc.vector.tensor_copy(st[0:64, :, 64:128], src[0:64, :, 64:128])
                            last.then_inc(lev_read, 1)
                        dve.wait_ge(u_mm, u * 4 + (b + 1 + ONE))
                        for c in range(CH):
                            if b == BLOCKS - 1 and c == CH - 1:
                                continue
                            settle()
                            nxt = states[b % 2][:, c + 1, :] if c < CH - 1 else states[(b + 1) % 2][:, 0, :]
                            tick(nc.vector.scalar_tensor_tensor(out=nxt, in0=states[b % 2][:, c, :],
                                                                scalar=tot[128][:, c:c + 1],
                                                                in1=bank[5][:, c * P:(c + 1) * P],
                                                                op0=ALU.mult, op1=ALU.add))
                        dve.wait_ge(lev_read, u * 20 + (5 * b + LEVELS + 2))
                        settle()
                        dve.sem_inc(st_ready, 1)
                    elif kind == "Z":
                        dve.wait_ge(rs_done, u * 4 + (b + 1 + ONE))
                        for c in range(CH):
                            last = (nc.vector.scalar_tensor_tensor(
                                out=vg_blk[b % 2][:, c, P:GC], in0=bank[6][:, c * P:(c + 1) * P],
                                scalar=rs_o[:, c:c + 1], in1=vg_blk[b % 2][:, c, P:GC], op0=ALU.mult, op1=ALU.mult))
                        last.then_inc((out_done0, out_done1)[b % 2], 1)
                restart()

            dve.sem_inc(s_taken, 4)
            dve.sem_inc(pt_read, 2)
            dve.wait_ge(rope_landed, 16)

            def attention(v, with_next):
                U = v + HG_UNITS
                T0 = v * TILES
                for kind, i, part in attention_steps(with_next):
                    g, j = i // CH, i % CH
                    if kind == "X" and part == PARTS - 1:
                        dve.wait_ge(qk_ready, T0 + (i + 1))
                        if i >= 2:
                            dve.wait_ge(yT_mm, T0 + (i - 1 + ONE))
                        else:
                            dve.wait_ge(yT_mm, T0 + ONE)
                        x4 = qk_bank(i)[:, 0:GC].rearrange("p (n h c) -> p n h c", n=4, h=2)
                        r4 = roped[i % 2].rearrange("p n (h c) -> p n h c", h=2)
                        m4 = rtmp.rearrange("p n (h c) -> p n h c", h=2)
                        cos = rope_sb[:, i, 0:1, :].to_broadcast([P, 4, 32])
                        sin = rope_sb[:, i, 1:2, :].to_broadcast([P, 4, 32])
                        settle()
                        for h in range(2):
                            tick(tt(r4[:, :, h, :], x4[:, :, h, :], cos))
                            last = tick(tt(m4[:, :, h, :], x4[:, :, 1 - h, :], sin))
                        settle()
                        tick(tt(r4[:, :, 0, :], r4[:, :, 0, :], m4[:, :, 0, :], ALU.subtract))
                        tick(tt(r4[:, :, 1, :], r4[:, :, 1, :], m4[:, :, 1, :], ALU.add))
                        settle()
                        dve.sem_inc(roped_done, 1)
                    elif kind in ("N", "R"):
                        lo = P if i == 0 else 0
                        for n in ((0, 1) if kind == "N" else (2, 3)):
                            h = n % 2
                            dve.wait_ge(s_ready, T0 * 4 + (4 * i + n + 1 + ONE))
                            if n != 1:
                                before = FILLS * ((i - 1) // 4) + 3 * ((i - 1) % 4) + max(n, 1) if i else 0
                                dve.wait_ge(pt_mm, v * (FILLS * 4) + (before + ONE))
                            if n == 0 and j == 0 and g < 2:
                                dve.wait_ge(stat_stored, v * 64 + ONE)
                            if n == 0 and j == 0 and g >= 2:
                                dve.wait_ge(stat_stored, v * 64 + (16 * (g - 1) + ONE))
                            if n < 2:
                                src, msk, dst = bank[2 - h][:, lo:2 * P], near_m[:, lo:], p_near[:, h, lo:]
                            else:
                                src, msk, dst = bank[3 + h][:, 0:P * (g + 1)], far_m[:, BT - P * (g + 1):], p_far[:, h, 0:P * (g + 1)]
                            stt = (st_near if n < 2 else st_far)[g % 2]
                            if i == 0:
                                dve.wait_ge(tab_landed, 32)
                            dve.sem_inc(passed_dve, 1)
                            settle()
                            nc.vector.tensor_tensor_reduce(out=dst, in0=src, in1=msk, scale=1.0, scalar=3e38,
                                                           op0=ALU.add, op1=ALU.min, accum_out=stt[:, j, h:h + 1])\
                                .then_inc(s_taken, 1)
                    elif kind == "B":
                        fill = v * (FILLS * 4) + (FILLS * g + 3 * j)
                        fb_ = FILLS * g + 3 * j + 1
                        dve.wait_ge(pt_mm, fill + 2 + ONE)
                        dve.wait_ge(pv_mm, T0 + i + ONE)
                        dve.wait_ge(pt_read, fill + 3)
                        nc.vector.tensor_copy(pT[1][:, 0:g + 1, :].rearrange("p a b -> p (a b)"),
                                              bank[5 + fb_ % 2][:, 0:P * (g + 1)]).then_inc(pt_read, 1)
                    elif kind == "D":
                        g = i
                        near, far = st_near[g % 2], st_farn[g % 2]
                        dve.wait_ge(stat_landed[g % 2], v * 32 + 16 * (g // 2 + 1))
                        settle()
                        tick(tt(top, near[:, :, 0:2], far[:, :, 0:2], ALU.min))
                        settle()
                        tick(tt(ea, top, near[:, :, 0:2], ALU.subtract))
                        tick(tt(eb, top, far[:, :, 0:2], ALU.subtract))
                        settle()
                        dve.sem_inc(dve_comb, 1)
                    elif kind == "E":
                        g = i
                        near, far = st_near[g % 2], st_farn[g % 2]
                        dve.wait_ge(exp_comb, v * 4 + (g + 1))
                        tick(tt(den, ea, near[:, :, 2:4]))
                        tick(tt(tsum, eb, far[:, :, 2:4]))
                        settle()
                        tick(tt(den, den, tsum, ALU.add))
                        settle()
                        tick(nc.vector.reciprocal(rden, den))
                        settle()
                        tick(tt(wa, ea, rden))
                        tick(tt(wb, eb, rden))
                    elif kind == "C":
                        g = i
                        fill = v * (FILLS * 4) + (FILLS * g + 12)
                        settle()
                        dve.wait_ge(pt_mm, fill + 1 + ONE)
                        dve.wait_ge(pt_read, fill + 2)
                        c4 = comb.rearrange("p c (h d) -> p (c h) d", h=2)

                        def v8(ap):
                            return ap.rearrange("p (n d) -> p n d", d=HD)

                        def w8(ap):
                            return ap.rearrange("p c h -> p (c h)")[:, :, None].to_broadcast([P, 2 * CH, HD])
                        dve.wait_ge(comb_done, v * 4 + (g + ONE))
                        tt(c4, v8(bank[5][:, :]), w8(wa)).then_inc(pt_read, 1)
                        dve.wait_ge(pt_mm, fill + 2 + ONE)
                        tick(tt(v8(bank[6][:, :]), v8(bank[6][:, :]), w8(wb)))
                        settle()
                        dve.wait_ge(pt_read, fill + 3)
                        tt(c4, v8(bank[6][:, :]), c4, ALU.add).then_inc(pt_read, 1)
                        dve.wait_ge(gate_landed, v * 64 + 16 * (g + 1))
                        dve.wait_ge(pt_read, fill + 4)
                        tt(gate, gate, comb).then_inc(comb_done, 1)
                    elif kind == "T" and part == PARTS - 1:
                        dve.wait_ge(sig_done, (U + 1) * 16 + (i + 1))
                        dve.sem_inc(passed_dve, 1)
                        settle()
                        sg = sg_tile[i % 2][:, :]
                        tick(nc.vector.tensor_scalar(sg, sg, 1.0, None, ALU.add))
                        settle()
                        nc.vector.reciprocal(sg, sg).then_inc(gate_done, 1)
                restart()

            with dve.Fori(0, AT_UNITS - 1) as v:
                attention(v, True)
            attention(AT_UNITS - 1, False)

            for t in range(TILES + 2):
                if t < TILES:
                    dve.wait_ge(mhi_done, t + 1)
                    for q in range(2):
                        last = tt(mT_lo[t % 2][:, 4 * q:4 * q + 4, :].rearrange("p a b -> p (a b)"),
                                  bank[1 + 2 * (t % 2) + q][:, :],
                                  mT_hi[t % 2][:, 4 * q:4 * q + 4, :].rearrange("p a b -> p (a b)").bitcast(F32), ALU.subtract)
                    last.then_inc(mlo_done, 1)
                if t >= 1 and t - 1 < TILES:
                    z = t - 1
                    dve.wait_ge(y_ready, z + 1)
                    dve.wait_ge(xr_landed[z % MX_SLOTS], 16 * (z // MX_SLOTS + 1))
                    if z >= 2:
                        dve.wait_ge(fin_stored[z % 2], 16 * (z // 2))
                    for q in range(2):
                        yb = (bank[5 + q], (bank[7], bank[0])[q])[z % 2]
                        last = tt(hh[z % 2][:, 512 * q:512 * q + 512], yb[:, :], xr[z % MX_SLOTS][:, 512 * q:512 * q + 512], ALU.add)
                    last.then_inc(hsum_done, 1)
                if t >= 2:
                    z = t - 2
                    dve.wait_ge(frs_done, z + 1)
                    if z == 0:
                        dve.wait_ge(tab_landed, 48)
                    nc.vector.scalar_tensor_tensor(out=hh[z % 2], in0=hh[z % 2], scalar=rs_f[:, z:z + 1], in1=fw,
                                                   op0=ALU.mult, op1=ALU.mult).then_inc(fin_done, 1)


def constants():
    half = HD // 2
    inv = (np.float32(1.0) / np.power(np.float32(10000.0), np.arange(half, dtype=np.float32) / np.float32(half))).astype(np.float32)
    ang = (np.arange(SEQ, dtype=np.float32)[:, None] * inv[None, :]).astype(np.float32)
    rope = np.stack([np.cos(ang), np.sin(ang)], 1).astype(np.float32).reshape(TILES, P, 2, half)
    rope = np.ascontiguousarray(rope.transpose(1, 0, 2, 3))
    qi = np.arange(P)[:, None]
    dist = qi + P - np.arange(2 * P)[None, :]
    near = np.where((dist >= 0) & (dist <= 128), 0.0, -MASKED).astype(np.float32)
    step = qi + (CH - 1) * P - np.arange(BT)[None, :]
    times = ((step >= 0) & (step <= 128)).astype(np.int64) + ((step >= 0) & (step % 4 == 0))
    far = np.where(times > 0, -np.log(np.maximum(times, 1)), -MASKED).astype(np.float32)
    si, ti = np.arange(P)[:, None], np.arange(P)[None, :]
    tri = [(si // 8 == ti // 8) & (si <= ti)]
    for h in (8, 16):
        pairs = (si // (2 * h) == ti // (2 * h)) & (si // h < ti // h)
        later = pairs.reshape(P, P // (2 * h), 2, h)[:, :, 1, :].reshape(P, P // 2)
        tri.append(np.concatenate([later, np.zeros_like(later)], 1))
    return rope, near, far, np.ascontiguousarray(np.stack(tri, 1).astype(np.int32))


def kernel(x, norm_w, w_in, hgrn_lb_logits, hg_norm_w, w_out, final_norm_w):
    import concourse.bacc as bacc
    from concourse.bass_utils import run_bass_kernel_spmd

    def tiles_of(w):
        return w.reshape(KT_N, P, GC).transpose(1, 0, 2)

    w = np.asarray(w_in)[0].reshape(D, 8, 4, P)
    groups = []
    for U in range(UNITS):
        f0 = 0 if U < HG_UNITS else 4
        for pair in ((f0 + 2, f0 + 3), (f0, f0 + 1)):
            groups.append(tiles_of(np.concatenate([w[:, c, U % 4, :] for c in pair], 1)))
    wo = np.asarray(w_out)[0]
    for n in range(OUT_GROUPS):
        groups.append(tiles_of(wo[:, n * GC:(n + 1) * GC]))
    g = np.asarray(hg_norm_w)[0].reshape(HG_UNITS, P)
    g = np.concatenate([g, np.ones((1, P), np.float32)], 0)
    rope, near, far, tri = constants()
    arrays = {
        "x": np.asarray(x)[0],
        "w_groups": np.stack(groups),
        "norm_w": np.asarray(norm_w)[0].reshape(KT_N, P).T,
        "gate_g": np.broadcast_to(g[None], (P, HG_UNITS + 1, P)),
        "lb_logits": np.asarray(hgrn_lb_logits).reshape(2, HG_UNITS, P).transpose(2, 0, 1),
        "final_w": np.broadcast_to(np.asarray(final_norm_w)[None], (P, D)),
        "rope": rope, "near_mask": near, "far_mask": far, "tri_masks": tri,
    }
    arrays = {f"in_{k}": np.ascontiguousarray(a) for k, a in arrays.items()}
    nc = bacc.Bacc("TRN2", target_bir_lowering=False, num_devices=1, dynamic_dma_scratch_size=1024)
    args = [nc.dram_tensor(k, a.shape, mybir.dt.from_np(a.dtype), kind="ExternalInput").ap() for k, a in arrays.items()]
    out = nc.dram_tensor("out_0", (SEQ, D), F32, kind="ExternalOutput").ap()
    build(nc, *args, out)
    r = run_bass_kernel_spmd(nc, [arrays], core_ids=[0])
    return r.results[0]["out_0"].reshape(1, SEQ, D)
```
